# Optimizing a Trainium2 kernel written in Bass

```python
import jax, jax.numpy as jnp
from jax import lax
import numpy as np

D_MODEL = 1024
BATCH = 1
SEQ = 1024
DEPTH = 1

PLE_DIM = 256
EPS = 1e-6
HG_HEADS = 4
HG_DK = 128
HG_DV = 128
HG_WIDTH = HG_HEADS * HG_DK
HG_CHUNK = 64
RET_HEADS = 4
RET_DK = 128
RET_DV = 256
RET_QK_WIDTH = RET_HEADS * RET_DK
RET_V_WIDTH = RET_HEADS * RET_DV
RET_CHUNK = 128
ROPE_BASE = 10000.0
IN_SPLITS = [HG_WIDTH, HG_WIDTH, HG_WIDTH, HG_WIDTH,
             RET_QK_WIDTH, RET_QK_WIDTH, RET_V_WIDTH, RET_V_WIDTH,
             D_MODEL, D_MODEL]
IN_TOTAL = sum(IN_SPLITS)
N_GROUPS = 4
EXPERTS_PER_GROUP = 8
N_EXPERTS = N_GROUPS * EXPERTS_PER_GROUP
TOP_K_IN_GROUP = 2
D_EXPERT = 256

kernel_name = 'hybrid_hgrn2_retention_hmoe_block'

def rmsnorm(x, g):
    xf = x.astype(jnp.float32)
    y = xf * lax.rsqrt(jnp.mean(xf * xf, axis=-1, keepdims=True) + EPS)
    return (y * g.astype(jnp.float32)).astype(x.dtype)

def _chunks(t, n_heads, chunk):
    b, s, w = t.shape
    return t.reshape(b, s // chunk, chunk, n_heads, w // n_heads).transpose(1, 0, 3, 2, 4)

def _unchunks(t):
    nc, b, h, c, d = t.shape
    return t.transpose(1, 0, 3, 2, 4).reshape(b, nc * c, h, d)

def hgrn2_lower_bound(lb_logits, layer):
    sm = jax.nn.softmax(lb_logits.astype(jnp.float32), axis=0)
    return jnp.cumsum(sm, axis=0)[layer]

def hgrn2_mix(q, f_logit, i, g, lb, norm_g):
    B, S, _ = q.shape
    C = HG_CHUNK
    qf = jax.nn.silu(q.astype(jnp.float32))
    z = f_logit.astype(jnp.float32)
    log_f = jnp.logaddexp(jnp.log(lb), jnp.log1p(-lb) + jax.nn.log_sigmoid(z))
    k = -jnp.expm1(log_f)
    qc = _chunks(qf, HG_HEADS, C)
    kc = _chunks(k, HG_HEADS, C)
    lc = _chunks(log_f, HG_HEADS, C)
    vc = _chunks(i.astype(jnp.float32), HG_HEADS, C)
    causal = jnp.tril(jnp.ones((C, C), dtype=bool))[:, :, None]

    def step(state, inp):
        q_, k_, lf, v_ = inp
        b = jnp.cumsum(lf, axis=2)
        diff = b[:, :, :, None, :] - b[:, :, None, :, :]
        decay = jnp.exp(jnp.where(causal, diff, -jnp.inf))
        scores = jnp.einsum('bhtk,bhsk,bhtsk->bhts', q_, k_, decay)
        o = (jnp.einsum('bhts,bhsv->bhtv', scores, v_)
             + jnp.einsum('bhtk,bhkv->bhtv', q_ * jnp.exp(b), state))
        b_last = b[:, :, -1, :]
        new_state = (jnp.exp(b_last)[..., None] * state
                     + jnp.einsum('bhsk,bhsv->bhkv', k_ * jnp.exp(b_last[:, :, None, :] - b), v_))
        return new_state, o

    s0 = jnp.zeros((B, HG_HEADS, HG_DK, HG_DV), jnp.float32)
    _, o = lax.scan(step, s0, (qc, kc, lc, vc))
    o = rmsnorm(_unchunks(o), norm_g).reshape(B, S, HG_HEADS * HG_DV)
    return (o * jax.nn.silu(g.astype(jnp.float32))).astype(q.dtype)

def rotary(t, pos):
    d = t.shape[-1]
    inv = ROPE_BASE ** (-jnp.arange(0, d, 2, dtype=jnp.float32) / d)
    ang = pos[:, None] * inv[None, :]
    cos = jnp.cos(ang)[None, :, None, :]
    sin = jnp.sin(ang)[None, :, None, :]
    t1, t2 = t[..., : d // 2], t[..., d // 2:]
    return jnp.concatenate([t1 * cos - t2 * sin, t1 * sin + t2 * cos], axis=-1)

def retention_mix(q, k, v, g, pos, norm_g):
    B, S, _ = q.shape
    C = RET_CHUNK
    qh = rotary(q.astype(jnp.float32).reshape(B, S, RET_HEADS, RET_DK), pos) * (RET_DK ** -0.5)
    kh = rotary(k.astype(jnp.float32).reshape(B, S, RET_HEADS, RET_DK), pos)
    qc = _chunks(qh.reshape(B, S, RET_QK_WIDTH), RET_HEADS, C)
    kc = _chunks(kh.reshape(B, S, RET_QK_WIDTH), RET_HEADS, C)
    vc = _chunks(v.astype(jnp.float32), RET_HEADS, C)
    lg = jnp.log1p(-jnp.exp2(-5.0 - jnp.arange(RET_HEADS, dtype=jnp.float32)))
    idx = jnp.arange(C, dtype=jnp.float32)
    rel = idx[:, None] - idx[None, :]
    intra = jnp.exp(jnp.where(rel >= 0, rel[None] * lg[:, None, None], -jnp.inf))
    inter = jnp.exp((idx[None, :] + 1.0) * lg[:, None])
    to_state = jnp.exp((C - 1.0 - idx[None, :]) * lg[:, None])
    chunk_decay = jnp.exp(C * lg)

    def step(R, inp):
        q_, k_, v_ = inp
        att = jnp.einsum('bhtk,bhsk->bhts', q_, k_) * intra
        o = (jnp.einsum('bhts,bhsv->bhtv', att, v_)
             + jnp.einsum('bhtk,bhkv->bhtv', q_, R) * inter[:, :, None])
        R = (chunk_decay[:, None, None] * R
             + jnp.einsum('bhsk,bhsv->bhkv', k_ * to_state[:, :, None], v_))
        return R, o

    r0 = jnp.zeros((B, RET_HEADS, RET_DK, RET_DV), jnp.float32)
    _, o = lax.scan(step, r0, (qc, kc, vc))
    o = rmsnorm(_unchunks(o), norm_g).reshape(B, S, RET_V_WIDTH)
    return (o * jax.nn.silu(g.astype(jnp.float32))).astype(q.dtype)

def hier_moe(h, w_rg, b_rg, w_re, b_re, w_gate, w_up, w_down):
    T, D = h.shape
    g_logits = (h @ w_rg).astype(jnp.float32) + b_rg.astype(jnp.float32)
    g_prob = jax.nn.softmax(g_logits, axis=-1)
    g_idx = jnp.argmax(g_logits, axis=-1)
    g_w = jnp.take_along_axis(g_prob, g_idx[:, None], axis=-1)[:, 0]
    e_logits = ((h @ w_re).astype(jnp.float32) + b_re.astype(jnp.float32)).reshape(T, N_GROUPS, EXPERTS_PER_GROUP)
    e_logits = jnp.take_along_axis(e_logits, g_idx[:, None, None], axis=1)[:, 0]
    top_l, top_i = lax.top_k(e_logits, TOP_K_IN_GROUP)
    w = jax.nn.softmax(top_l, axis=-1) * g_w[:, None]
    eid = (g_idx[:, None] * EXPERTS_PER_GROUP + top_i).reshape(-1)
    order = jnp.argsort(eid)
    xs = h[order // TOP_K_IN_GROUP]
    sizes = jnp.bincount(eid, length=N_EXPERTS).astype(jnp.int32)
    a = lax.ragged_dot(xs, w_gate, sizes)
    u = lax.ragged_dot(xs, w_up, sizes)
    ys = lax.ragged_dot(jax.nn.silu(a) * u, w_down, sizes)
    y = jnp.zeros_like(ys).at[order].set(ys).reshape(T, TOP_K_IN_GROUP, D)
    return jnp.einsum('tkd,tk->td', y, w.astype(y.dtype))

def setup_inputs(seed: int = 0) -> dict:
    key = jax.random.key(seed)
    ks = jax.random.split(key, 24)
    f32 = jnp.float32

    def nrm(k, shape, fan):
        return jax.random.normal(k, shape, f32) * (fan ** -0.5)

    def gain(k, shape):
        return 1.0 + 0.02 * jax.random.normal(k, shape, f32)

    return {
        'x': jax.random.normal(ks[0], (BATCH, SEQ, D_MODEL), f32),
        'p': jax.random.normal(ks[1], (DEPTH, BATCH, SEQ, PLE_DIM), f32),
        'mix_norm': gain(ks[2], (DEPTH, D_MODEL)),
        'w_in': nrm(ks[3], (DEPTH, D_MODEL, IN_TOTAL), D_MODEL),
        'hg_lb_logits': 0.5 * jax.random.normal(ks[4], (DEPTH + 1, HG_WIDTH), f32),
        'hg_norm': gain(ks[5], (DEPTH, HG_DV)),
        'ret_norm': gain(ks[6], (DEPTH, RET_DV)),
        'w_branch_a': nrm(ks[7], (DEPTH, HG_WIDTH, D_MODEL), HG_WIDTH),
        'w_branch_b': nrm(ks[8], (DEPTH, RET_V_WIDTH, D_MODEL), RET_V_WIDTH),
        'w_out': nrm(ks[9], (DEPTH, D_MODEL, D_MODEL), D_MODEL),
        'ffn_norm': gain(ks[10], (DEPTH, D_MODEL)),
        'w_router_group': nrm(ks[11], (DEPTH, D_MODEL, N_GROUPS), D_MODEL),
        'b_router_group': 0.01 * jax.random.normal(ks[12], (DEPTH, N_GROUPS), f32),
        'w_router_expert': nrm(ks[13], (DEPTH, D_MODEL, N_EXPERTS), D_MODEL),
        'b_router_expert': 0.01 * jax.random.normal(ks[14], (DEPTH, N_EXPERTS), f32),
        'w_expert_gate': nrm(ks[15], (DEPTH, N_EXPERTS, D_MODEL, D_EXPERT), D_MODEL),
        'w_expert_up': nrm(ks[16], (DEPTH, N_EXPERTS, D_MODEL, D_EXPERT), D_MODEL),
        'w_expert_down': nrm(ks[17], (DEPTH, N_EXPERTS, D_EXPERT, D_MODEL), D_EXPERT),
        'ple_norm': gain(ks[18], (DEPTH, D_MODEL)),
        'w_ple_gate': nrm(ks[19], (DEPTH, D_MODEL, D_MODEL), D_MODEL),
        'w_ple_proj': nrm(ks[20], (DEPTH, PLE_DIM, D_MODEL), PLE_DIM),
        'final_norm': gain(ks[21], (D_MODEL,)),
    }

def reference(x, p, mix_norm, w_in, hg_lb_logits, hg_norm, ret_norm, w_branch_a, w_branch_b, w_out,
              ffn_norm, w_router_group, b_router_group, w_router_expert, b_router_expert,
              w_expert_gate, w_expert_up, w_expert_down, ple_norm, w_ple_gate, w_ple_proj, final_norm):
    B, S, D = x.shape
    pos = jnp.arange(S, dtype=jnp.float32)
    split_at = [int(v) for v in np.cumsum(IN_SPLITS)[:-1]]
    for layer in range(DEPTH):
        h = rmsnorm(x, mix_norm[layer])
        proj = h @ w_in[layer]
        hq, hf, hi, hg, rq, rk, rv, rg, ga, gb = jnp.split(proj, split_at, axis=-1)
        lb = hgrn2_lower_bound(hg_lb_logits, layer)
        ya = hgrn2_mix(hq, hf, hi, hg, lb, hg_norm[layer])
        yb = retention_mix(rq, rk, rv, rg, pos, ret_norm[layer])
        merged = (jax.nn.sigmoid(ga) * (ya @ w_branch_a[layer])
                  + jax.nn.sigmoid(gb) * (yb @ w_branch_b[layer]))
        x = x + merged @ w_out[layer]
        h2 = rmsnorm(x, ffn_norm[layer]).reshape(B * S, D)
        x = x + hier_moe(h2, w_router_group[layer], b_router_group[layer], w_router_expert[layer],
                         b_router_expert[layer], w_expert_gate[layer], w_expert_up[layer],
                         w_expert_down[layer]).reshape(B, S, D)
        hp = rmsnorm(x, ple_norm[layer])
        x = x + jax.nn.sigmoid(hp @ w_ple_gate[layer]) * (p[layer] @ w_ple_proj[layer])
    return rmsnorm(x, final_norm)


_drawn_inputs = setup_inputs


def setup_inputs(seed=0):
    import zlib

    import numpy as np

    out = dict(_drawn_inputs(seed))
    spreads = {}
    factors = {'hg_norm': 10.97,
     'ret_norm': 11.892,
     'b_router_group': 6.343,
     'b_router_expert': 14.468,
     'ple_norm': 64.0,
     'final_norm': 7.563,
     'ffn_norm': 3.167}
    for name, (base, spread) in spreads.items():
        noise = np.random.default_rng([zlib.crc32(name.encode()), seed]).standard_normal(out[name].shape)
        drawn = base * np.exp(spread * noise) if base else spread * noise
        out[name] = __import__('jax').numpy.asarray(drawn.astype(out[name].dtype))
    for name, factor in factors.items():
        out[name] = (out[name] * factor).astype(out[name].dtype)
    return out
```

```python
from contextlib import ExitStack

import numpy as np

import concourse.bass as bass
import concourse.mybir as mybir

F32 = mybir.dt.float32
F32R = mybir.dt.float32r
I32 = mybir.dt.int32
ALU = mybir.AluOpType
ACT = mybir.ActivationFunctionType
AX = mybir.AxisListType

P = 128
S = 1024
D = 1024
KT = D // P
TT = S // P
HALF = 512
EPS = 1e-6

HG_HEADS, HG_DK, HG_DV = 4, 128, 128
HG_CHUNK = 64
HG_NC = S // HG_CHUNK
RET_HEADS, RET_DK, RET_DV = 4, 128, 256
HG_W = HG_HEADS * HG_DV
RET_QK = RET_HEADS * RET_DK
RET_V = RET_HEADS * RET_DV
VW = HG_W + RET_V
HQ, HF, HI, HGATE = 0, HG_W, 2 * HG_W, 3 * HG_W
RQ = 4 * HG_W
RK = RQ + RET_QK
RV = RK + RET_QK
RGATE = RV + RET_V
GA = RGATE + RET_V
GB = GA + D
IN_TOTAL = GB + D
PLE = 256

GROUPS, PER_GROUP = 4, 8
EXPERTS = GROUPS * PER_GROUP
DE = 256
PAIRS = 2 * S
OVER = (PAIRS - 1) // P
COLS = EXPERTS + OVER
LEVELS = [32, 16, 8, 4, 2, 1]
FAR = 1 << 20


class Steps:

    def __init__(self, eng, sem, base=0):
        self.eng, self.sem, self.base, self.n = eng, sem, base, 0

    def add(self, ins):
        ins.then_inc(self.sem, 1)
        self.n += 1
        return self.n

    def wait(self, n=None):
        self.eng.wait_ge(self.sem, self.base + (self.n if n is None else n))

    def link(self, ins):
        self.add(ins)
        self.wait()


def over(eng, n, body):
    body(0)
    if n > 2:
        with eng.Fori(1, n - 1) as i:
            body(i)
    if n > 1:
        body(n - 1)


def at(i, n):
    return isinstance(i, int) and i == n


def first(i):
    return at(i, 0)


def bc(ap, dim, n):
    a = ap.unsqueeze(dim)
    shape = list(a.shape)
    shape[dim] = n
    return a.to_broadcast(shape)


class Memory:

    sems = []

    @classmethod
    def recycle(cls, nc):
        nc.clear_and_free_semaphores(cls.sems)
        nc.all_engine_barrier()
        cls.sems.clear()

    def __init__(self, nc, stage):
        self.nc, self.stage, self.ctx = nc, stage, ExitStack()

    def __enter__(self):
        return self

    def __exit__(self, *a):
        return self.ctx.__exit__(*a)

    def sb(self, name, shape, dt=F32):
        return self.ctx.enter_context(self.nc.sbuf_tensor(f"{self.stage}_{name}", shape, dt))

    def ps(self, name, shape):
        return self.ctx.enter_context(self.nc.psum_tensor(f"{self.stage}_{name}", shape, F32))

    def sem(self, name):
        self.sems.append(self.nc.alloc_semaphore(f"{self.stage}_{name}"))
        return self.sems[-1]

    def block(self):
        return self.ctx.enter_context(self.nc.Block())


def normalise_input(nc, dram, kept):
    with Memory(nc, "norm") as m:
        xt = m.sb("xt", [P, 2, D])
        sq = m.sb("sq", [P, D])
        xn = m.sb("xn", [P, 2, D])
        stat = m.sb("stat", [P, 2, 4])
        gain = m.sb("gain", [P, KT])
        whole = m.sb("whole", [P, 2, KT, P])
        turned = m.ps("turned", [P, 2, KT, P])
        loaded = [m.sem(f"loaded{u}") for u in range(2)]
        consts = m.sem("consts")
        summed, scaled, rooted = m.sem("summed"), m.sem("scaled"), m.sem("rooted")
        mean, rstd = m.sem("mean"), m.sem("rstd")
        turned_ok, gained, hi_ok, lo_ok = m.sem("turned_ok"), m.sem("gained"), m.sem("hi_ok"), m.sem("lo_ok")
        block = m.block()

        @block.sync
        def _(sp):
            sp.dma_start(gain[:], dram["mix_norm"]).then_inc(consts, 16)
            sp.dma_start(kept["ident"][:], dram["ident"]).then_inc(consts, 16)

            def tile(i):
                for u in range(2):
                    if not first(i):
                        sp.wait_ge(scaled, 2 * i - 1 + u)
                    sp.dma_start(xt[:, u, :], dram["x"][bass.ds((2 * i + u) * P, P), :]).then_inc(loaded[u], 16)
            over(sp, TT // 2, tile)

        @block.scalar
        def _(act):
            act.wait_ge(consts, 32)

            def tile(i):
                for u in range(2):
                    t = 2 * i + u
                    act.wait_ge(loaded[u], 16 * i + 16)
                    if not (first(i) and u == 0):
                        act.wait_ge(rooted, t)
                        act.wait_ge(summed, t)
                    nc.scalar.activation(sq[:], xt[:, u, :], ACT.Square,
                                         accum_out=stat[:, u, 0:1]).then_inc(summed, 1)
                    act.wait_ge(mean, t + 1)
                    nc.scalar.activation(stat[:, u, 2:3], stat[:, u, 1:2], ACT.Sqrt).then_inc(rooted, 1)
                    act.wait_ge(rstd, t + 1)
                    if not first(i):
                        act.wait_ge(turned_ok, t - 1)
                    nc.scalar.activation(xn[:, u, :], xt[:, u, :], ACT.Copy,
                                         scale=stat[:, u, 3:4]).then_inc(scaled, 1)
                    act.wait_ge(gained, t + 1)
                    nc.scalar.copy(kept["hT_hi"][:, :, bass.ds(t * P, P)], whole[:, u, :, :]).then_inc(hi_ok, 1)
            over(act, TT // 2, tile)

        @block.tensor
        def _(pe):
            pe.wait_ge(consts, 32)

            def tile(i):
                for u in range(2):
                    t = 2 * i + u
                    pe.wait_ge(scaled, t + 1)
                    if not first(i):
                        pe.wait_ge(gained, t - 1)
                    for k in range(KT):
                        mm = nc.tensor.transpose(turned[:, u, k, :], xn[:, u, k * P:(k + 1) * P], kept["ident"][:])
                    mm.then_inc(turned_ok, 1)
            over(pe, TT // 2, tile)

        @block.vector
        def _(dve):
            dve.wait_ge(consts, 32)

            def tile(i):
                for u in range(2):
                    t = 2 * i + u
                    dve.wait_ge(summed, t + 1)
                    nc.vector.tensor_scalar(stat[:, u, 1:2], stat[:, u, 0:1], 1.0 / D, EPS,
                                            ALU.mult, ALU.add).then_inc(mean, 1)
                    dve.wait_ge(rooted, t + 1)
                    nc.vector.reciprocal(stat[:, u, 3:4], stat[:, u, 2:3]).then_inc(rstd, 1)
                    dve.wait_ge(turned_ok, t + 1)
                    if not first(i):
                        dve.wait_ge(lo_ok, t - 1)
                    nc.vector.tensor_tensor(whole[:, u, :, :], turned[:, u, :, :], bc(gain[:], 2, P),
                                            ALU.mult).then_inc(gained, 1)
                    dve.wait_ge(hi_ok, t + 1)
                    nc.vector.tensor_tensor(kept["hT_lo"][:, :, bass.ds(t * P, P)], whole[:, u, :, :],
                                            kept["hT_hi"][:, :, bass.ds(t * P, P)].bitcast(F32),
                                            ALU.subtract).then_inc(lo_ok, 1)
            over(dve, TT // 2, tile)


def three_passes(nc, out, parts):
    n = len(parts)
    for k, (sh, sl, mh, ml) in enumerate(parts):
        nc.tensor.matmul(out, sh, mh, start=(k == 0), stop=False)
        nc.tensor.matmul(out, sh, ml, start=False, stop=False)
        mm = nc.tensor.matmul(out, sl, mh, start=False, stop=(k == n - 1))
    return mm


class Ring:

    def __init__(self, nc, m, kt, w, used, per=1, name="w"):
        self.nc = nc
        self.raw = m.sb(name + "_raw", [P, 2, kt, w])
        self.hi = m.sb(name + "_hi", [P, 2, kt, w], F32R)
        self.lo = m.sb(name + "_lo", [P, 2, kt, w], F32R)
        self.loaded = [m.sem(f"{name}_loaded{u}") for u in range(2)]
        self.hi_ok, self.lo_ok = m.sem(name + "_hi_ok"), m.sem(name + "_lo_ok")
        self.used, self.per = used, per

    def load(self, sp, i, u, src, kt=KT):
        if not first(i):
            sp.wait_ge(self.lo_ok, 2 * i - 1 + u)
        sp.dma_start(self.raw[:, u, 0:kt], src).then_inc(self.loaded[u], 16)

    def split_hi(self, act, i, u, kt=KT):
        act.wait_ge(self.loaded[u], 16 * i + 16)
        if not first(i):
            act.wait_ge(self.used, self.per * (2 * i - 1 + u))
        self.nc.scalar.copy(self.hi[:, u, 0:kt], self.raw[:, u, 0:kt]).then_inc(self.hi_ok, 1)

    def split_lo(self, dve, i, u, kt=KT):
        dve.wait_ge(self.hi_ok, 2 * i + u + 1)
        self.nc.vector.tensor_tensor(self.lo[:, u, 0:kt], self.raw[:, u, 0:kt],
                                     self.hi[:, u, 0:kt].bitcast(F32), ALU.subtract).then_inc(self.lo_ok, 1)


def tokens_out(nc, m, src_hi, src_lo, w_dram, runs, store, act_banks):
    W = 256
    BANKS = TT // 2
    sums = m.ps("sums", [P, 2, BANKS, 2, W])
    full = m.sem("full")
    stored = {True: m.sem("stored_act"), False: m.sem("stored_dve")}
    dve_banks = [b for b in range(BANKS) if b not in act_banks]
    ring = Ring(nc, m, KT, W, full, BANKS)
    pairs = sum(n for n, _ in runs)
    w_dram = w_dram.rearrange("(k p) c -> p k c", p=P)
    block = m.block()

    @block.sync
    def _(sp):
        done = 0
        for n, col in runs:
            if done == 0:
                def pair(i, col=col):
                    for u in range(2):
                        ring.load(sp, i, u, w_dram[:, :, bass.ds(col + (2 * i + u) * W, W)])
                over(sp, n, pair)
            else:
                with sp.Fori(done, done + n) as i:
                    for u in range(2):
                        ring.load(sp, i, u, w_dram[:, :, bass.ds(col + (2 * (i - done) + u) * W, W)])
            done += n

    def drain(eng, i, u, banks, mine):
        for b in banks:
            eng.wait_ge(full, (2 * i + u) * BANKS + b + 1)
            store(eng, b, (2 * i + u) * W, sums[:, u, b]).then_inc(stored[mine], 1)

    @block.scalar
    def _(act):
        ring.split_hi(act, 0, 0)

        def pair(i):
            ring.split_hi(act, i, 1)
            drain(act, i, 0, act_banks, True)
            if not at(i, pairs - 1):
                ring.split_hi(act, i + 1, 0)
            drain(act, i, 1, act_banks, True)
        over(act, pairs, pair)

    @block.vector
    def _(dve):
        ring.split_lo(dve, 0, 0)

        def pair(i):
            ring.split_lo(dve, i, 1)
            drain(dve, i, 0, dve_banks, False)
            if not at(i, pairs - 1):
                ring.split_lo(dve, i + 1, 0)
            drain(dve, i, 1, dve_banks, False)
        over(dve, pairs, pair)

    @block.tensor
    def _(pe):
        def pair(i):
            for u in range(2):
                pe.wait_ge(ring.lo_ok, 2 * i + u + 1)
                for tt in range(TT):
                    b = tt // 2
                    if not first(i) and tt % 2 == 0:
                        mine = b in act_banks
                        banks = act_banks if mine else dve_banks
                        pe.wait_ge(stored[mine], (2 * i - 2 + u) * len(banks) + banks.index(b) + 1)
                    mm = three_passes(nc, sums[:, u, b, tt % 2, :],
                                      [(src_hi[:, k, tt * P:(tt + 1) * P], src_lo[:, k, tt * P:(tt + 1) * P],
                                        ring.hi[:, u, k, :], ring.lo[:, u, k, :]) for k in range(KT)])
                    if tt % 2 == 1:
                        mm.then_inc(full, 1)
        over(pe, pairs, pair)


def project_values(nc, dram, kept):
    with Memory(nc, "vals") as m:
        values = kept["values"]

        def store(eng, b, col, psum):
            dst = values[:, 2 * b:2 * b + 2, bass.ds(col, 256)]
            if eng.engine == nc.scalar.engine:
                return nc.scalar.copy(dst, psum)
            return nc.vector.tensor_copy(dst, psum)

        tokens_out(nc, m, kept["hT_hi"], kept["hT_lo"], dram["w_in"], [(1, HI), (2, RV)], store, [0, 2])


def project_block(nc, pe, ring, kept, i, u, sums, per_done, then=None):
    pe.wait_ge(ring.lo_ok, 2 * i + u + 1)
    for half in range(2):
        cols = slice(half * HALF, (half + 1) * HALF)
        mm = three_passes(nc, sums[:, half, :],
                          [(ring.hi[:, u, k, :], ring.lo[:, u, k, :], kept["hT_hi"][:, k, cols],
                            kept["hT_lo"][:, k, cols]) for k in range(KT)])
    mm.then_inc(per_done, 1)


def hgrn_heads(nc, dram, kept):
    NL = len(LEVELS)
    with Memory(nc, "hgrn") as m:
        ga, gb_, gc = m.sb("sig_z", [P, S]), m.sb("sig_minus_z", [P, S]), m.sb("sig_q", [P, S])
        q, k, b = m.sb("q", [P, S]), m.sb("k", [P, S]), m.sb("b", [P, S])
        X = m.sb("scaled", [P, 3, S])
        q_in, k_out = m.sb("q_in", [P, S]), m.sb("k_out", [P, S])
        k_tok = m.sb("k_tok", [P, TT, P])
        v = m.sb("v", [P, TT, HG_DV])
        scores = m.sb("scores", [P, TT, HG_CHUNK])
        state = m.sb("state", [P, HG_NC, HG_DV])
        masks = m.sb("masks", [P, NL + 1, HG_CHUNK], I32)
        reset = m.sb("reset", [P, S])
        logits = m.sb("logits", [P, 2, HG_HEADS])
        lb = m.sb("lb", [P, 4, HG_HEADS])
        tick = m.sb("tick", [P, NL + 1])
        ticked = m.sem("ticked")
        sums = m.ps("sums", [P, 2, 2, HALF])
        pairs = m.ps("pairs", [P, 2, TT, HG_CHUNK])
        kv = m.ps("kv", [P, 4, P])
        outs = m.ps("outs", [P, 4, HG_DV])
        consts, bound_d, bound, zeroed = m.sem("consts"), m.sem("bound_d"), m.sem("bound"), m.sem("zeroed")
        projected = m.sem("projected")
        sig = m.sem("sig")
        qk = m.sem("qk")
        sub, expd, mul = m.sem("sub"), m.sem("expd"), m.sem("mul")
        paired, masked = m.sem("paired"), m.sem("masked")
        since, tail_sub, tail = m.sem("since"), m.sem("tail_sub"), m.sem("tail")
        q_in_ok, k_out_ok = m.sem("q_in_ok"), m.sem("k_out_ok")
        k_turned, k_tok_ok = m.sem("k_turned"), m.sem("k_tok_ok")
        kv_ok, state_ok = m.sem("kv_ok"), m.sem("state_ok")
        out_ok, out_stored = m.sem("out_ok"), m.sem("out_stored")
        v_ok = m.sem("v_ok")
        ring = Ring(nc, m, KT, P, projected)
        values, ident = kept["values"], kept["ident"]
        w_in = dram["w_in"].rearrange("(k p) c -> p k c", p=P)
        SU = 15
        block = m.block()

        @block.sync
        def _(sp):
            sp.dma_start(masks[:], dram["hg_masks"]).then_inc(consts, 16)
            sp.dma_start(reset[:], dram["hg_reset"]).then_inc(consts, 16)
            sp.dma_start(logits[:], dram["hg_lb_logits"]).then_inc(consts, 16)

            def head(i):
                ring.load(sp, i, 0, w_in[:, :, bass.ds(HQ + i * HG_DK, P)])
                ring.load(sp, i, 1, w_in[:, :, bass.ds(HF + i * HG_DK, P)])
            over(sp, HG_HEADS, head)

        @block.gpsimd
        def _(pool):
            def head(i):
                if not first(i):
                    pool.wait_ge(out_ok, 2 * i)
                nc.gpsimd.tensor_copy(v[:], values[:, :, bass.ds(i * HG_DV, HG_DV)]).then_inc(v_ok, 1)
            over(pool, HG_HEADS, head)

        @block.scalar
        def _(act):
            act.wait_ge(bound_d, 1)
            nc.scalar.activation(lb[:, 1, :], lb[:, 0, :], ACT.Sigmoid).then_inc(bound, 1)
            nc.scalar.activation(lb[:, 2, :], lb[:, 0, :], ACT.Sigmoid, scale=-1.0).then_inc(bound, 1)
            act.wait_ge(bound, 2)
            ring.split_hi(act, 0, 0)
            ring.split_hi(act, 0, 1)

            def head(i):
                act.wait_ge(state_ok, SU * i)
                act.wait_ge(k_out_ok, i)
                act.wait_ge(q_in_ok, i)
                act.wait_ge(qk, 3 * i)
                act.wait_ge(projected, 2 * i + 1)
                nc.scalar.activation(gc[:], sums[:, 0].rearrange("p a b -> p (a b)"), ACT.Sigmoid).then_inc(sig, 1)
                act.wait_ge(projected, 2 * i + 2)
                nc.scalar.activation(ga[:], sums[:, 1].rearrange("p a b -> p (a b)"), ACT.Sigmoid).then_inc(sig, 1)
                nc.scalar.activation(gb_[:], sums[:, 1].rearrange("p a b -> p (a b)"), ACT.Sigmoid,
                                     scale=-1.0).then_inc(sig, 1)
                act.wait_ge(sig, 4 * i + 2)
                nc.scalar.activation(ga[:], ga[:], ACT.Ln, bias=lb[:, 1, bass.ds(i, 1)],
                                     scale=lb[:, 2, bass.ds(i, 1)]).then_inc(sig, 1)
                if not at(i, HG_HEADS - 1):
                    ring.split_hi(act, i + 1, 0)
                    ring.split_hi(act, i + 1, 1)
                act.wait_ge(qk, 3 * i + 3)
                nc.scalar.activation(gb_[:], b[:], ACT.Exp).then_inc(since, 1)

                def level(l):
                    act.wait_ge(sub, 2 * NL * i + 2 * l + 2)
                    nc.scalar.activation(X[:, l % 3, :], X[:, l % 3, :], ACT.Exp).then_inc(expd, 1)

                def keys(half):
                    act.wait_ge(k_turned, 2 * i + half + 1)
                    nc.scalar.copy(k_tok[:, 4 * half:4 * half + 4, :], kv[:]).then_inc(k_tok_ok, 1)

                level(0)
                level(1)
                act.wait_ge(tail_sub, i + 1)
                nc.scalar.activation(ga[:], ga[:], ACT.Exp).then_inc(tail, 1)
                level(2)
                level(3)
                level(4)
                keys(0)
                level(5)
                keys(1)
                for half in range(2):
                    act.wait_ge(out_ok, 2 * i + half + 1)
                    nc.scalar.copy(values[:, 4 * half:4 * half + 4, bass.ds(i * HG_DV, HG_DV)],
                                   outs[:]).then_inc(out_stored, 1)
            over(act, HG_HEADS, head)

        @block.vector
        def _(dve):
            nc.vector.memset(scores[:], 0.0).then_inc(zeroed, 1)
            nc.vector.memset(state[:, 0, :], 0.0).then_inc(zeroed, 1)
            nc.vector.memset(lb[:, 3, :], 0.0).then_inc(zeroed, 1)
            dve.wait_ge(consts, 48)
            nc.vector.tensor_tensor(lb[:, 0, :], logits[:, 0, :], logits[:, 1, :], ALU.subtract).then_inc(bound_d, 1)
            dve.wait_ge(zeroed, 3)
            dve.wait_ge(bound, 2)
            ring.split_lo(dve, 0, 0)
            ring.split_lo(dve, 0, 1)

            def halves(t, h):
                v = t.rearrange("p (n two h) -> p n two h", two=2, h=h)
                return v[:, :, 0, :], v[:, :, 1, :]

            def head(i):
                if not first(i):
                    dve.wait_ge(paired, (NL + 1) * i)
                    dve.wait_ge(since, i)
                dve.wait_ge(sig, 4 * i + 1)
                nc.vector.tensor_tensor(q[:], sums[:, 0].rearrange("p a b -> p (a b)"), gc[:], ALU.mult).then_inc(qk, 1)
                dve.wait_ge(sig, 4 * i + 3)
                nc.vector.tensor_scalar(k[:], gb_[:], lb[:, 2, bass.ds(i, 1)], None, ALU.mult).then_inc(qk, 1)
                dve.wait_ge(sig, 4 * i + 4)
                nc.vector.tensor_tensor_scan(b[:], reset[:], ga[:], 0.0, ALU.mult, ALU.add).then_inc(qk, 1)
                dve.wait_ge(qk, 3 * i + 3)

                def exponents(l):
                    h = LEVELS[l]
                    lower, upper = halves(b[:], h)
                    x_lower, x_upper = halves(X[:, l % 3, :], h)
                    ref = lower[:, :, h - 1:h].to_broadcast([P, S // (2 * h), h])
                    nc.vector.tensor_tensor(x_upper, upper, ref, ALU.subtract).then_inc(sub, 1)
                    nc.vector.tensor_tensor(x_lower, ref, lower, ALU.subtract).then_inc(sub, 1)

                def products(l):
                    h = LEVELS[l]
                    x_lower, x_upper = halves(X[:, l % 3, :], h)
                    dve.wait_ge(expd, NL * i + l + 1)
                    nc.vector.tensor_tensor(x_upper, x_upper, halves(q[:], h)[1], ALU.mult).then_inc(mul, 1)
                    nc.vector.tensor_tensor(x_lower, x_lower, halves(k[:], h)[0], ALU.mult).then_inc(mul, 1)

                def mask(l):
                    dve.wait_ge(paired, (NL + 1) * i + l + 1)
                    if not (first(i) and l == 0):
                        dve.wait_ge(masked, (NL + 1) * i + l)
                    nc.vector.tensor_copy(tick[:, l:l + 1], lb[:, 3, 0:1]).then_inc(ticked, 1)
                    nc.vector.copy_predicated(scores[:], bc(masks[:, l, :], 1, TT), pairs[:, l % 2]).then_inc(masked, 1)

                def states(g):
                    dve.wait_ge(kv_ok, 2 * i + g + 1)
                    for c in range(8 * g, min(8 * g + 8, SU)):
                        if c:
                            dve.wait_ge(state_ok, SU * i + c)
                        nc.vector.scalar_tensor_tensor(
                            out=state[:, c + 1, :], in0=state[:, c, :],
                            scalar=gb_[:, c * HG_CHUNK + HG_CHUNK - 1:c * HG_CHUNK + HG_CHUNK],
                            in1=(kv, outs)[c % 2][:, (c // 2) % 4, :], op0=ALU.mult, op1=ALU.add).then_inc(state_ok, 1)

                exponents(0)
                exponents(1)
                bv = b[:].rearrange("p (n c) -> p n c", c=HG_CHUNK)
                nc.vector.tensor_tensor(ga[:].rearrange("p (n c) -> p n c", c=HG_CHUNK),
                                        bv[:, :, HG_CHUNK - 1:HG_CHUNK].to_broadcast([P, HG_NC, HG_CHUNK]), bv,
                                        ALU.subtract).then_inc(tail_sub, 1)
                if not at(i, HG_HEADS - 1):
                    ring.split_lo(dve, i + 1, 0)
                    ring.split_lo(dve, i + 1, 1)
                products(0)
                exponents(2)
                products(1)
                dve.wait_ge(tail, i + 1)
                nc.vector.tensor_tensor(k_out[:], k[:], ga[:], ALU.mult).then_inc(k_out_ok, 1)
                mask(0)
                exponents(3)
                products(2)
                if not first(i):
                    dve.wait_ge(out_ok, 2 * i)
                dve.wait_ge(since, i + 1)
                nc.vector.tensor_tensor(q_in[:], q[:], gb_[:], ALU.mult).then_inc(q_in_ok, 1)
                mask(1)
                exponents(4)
                products(3)
                mask(2)
                exponents(5)
                products(4)
                mask(3)
                products(5)
                mask(4)
                states(0)
                mask(5)
                mask(6)
                states(1)
            over(dve, HG_HEADS, head)

        @block.tensor
        def _(pe):
            def project(i):
                if not first(i):
                    pe.wait_ge(qk, 3 * i - 2)
                project_block(nc, pe, ring, kept, i, 0, sums[:, 0], projected)
                if not first(i):
                    pe.wait_ge(sig, 4 * i - 1)
                project_block(nc, pe, ring, kept, i, 1, sums[:, 1], projected)

            def chunk(t, c):
                return t[:, c * HG_CHUNK:(c + 1) * HG_CHUNK]

            def head(i):
                if not at(i, HG_HEADS - 1):
                    project(i + 1)

                def pair(l):
                    if l < NL:
                        pe.wait_ge(mul, 2 * NL * i + 2 * l + 2)
                    else:
                        pe.wait_ge(qk, 3 * i + 2)
                    if l >= 2:
                        pe.wait_ge(masked, (NL + 1) * i + l - 1)
                    elif not first(i):
                        pe.wait_ge(masked, (NL + 1) * i)
                    for c in range(HG_NC):
                        lhs, rhs = (X[:, l % 3, :], X[:, l % 3, :]) if l < NL else (k[:], q[:])
                        r = HG_CHUNK * (c % 2)
                        mm = nc.tensor.matmul(pairs[r:r + HG_CHUNK, l % 2, c // 2, :], chunk(lhs, c), chunk(rhs, c),
                                              start=True, stop=True)
                    mm.then_inc(paired, 1)

                def keys(half):
                    pe.wait_ge(k_out_ok, i + 1)
                    if half:
                        pe.wait_ge(k_tok_ok, 2 * i + 1)
                    elif not first(i):
                        pe.wait_ge(state_ok, SU * i)
                    for j in range(4):
                        t = 4 * half + j
                        mm = nc.tensor.transpose(kv[:, j, :], k_out[:, t * P:(t + 1) * P], ident[:])
                    mm.then_inc(k_turned, 1)

                def updates(g):
                    if g:
                        pe.wait_ge(state_ok, SU * i + 8)
                    else:
                        pe.wait_ge(k_tok_ok, 2 * i + 2)
                        pe.wait_ge(v_ok, i + 1)
                        if not first(i):
                            pe.wait_ge(out_stored, 2 * i)
                    for c in range(8 * g, min(8 * g + 8, SU)):
                        r = HG_CHUNK * (c % 2)
                        mm = nc.tensor.matmul((kv, outs)[c % 2][:, (c // 2) % 4, :], k_tok[r:r + HG_CHUNK, c // 2, :],
                                              v[r:r + HG_CHUNK, c // 2, :], start=True, stop=True)
                    mm.then_inc(kv_ok, 1)

                def output(half):
                    if half:
                        pe.wait_ge(out_stored, 2 * i + 1)
                    else:
                        pe.wait_ge(masked, (NL + 1) * i + NL + 1)
                        pe.wait_ge(q_in_ok, i + 1)
                        pe.wait_ge(state_ok, SU * i + SU)
                    for c in range(8 * half, 8 * half + 8):
                        r = HG_CHUNK * (c % 2)
                        out = outs[r:r + HG_CHUNK, (c // 2) % 4, :]
                        nc.tensor.matmul(out, chunk(q_in[:], c), state[:, c, :], start=True, stop=False)
                        mm = nc.tensor.matmul(out, scores[r:r + HG_CHUNK, c // 2, :],
                                              v[r:r + HG_CHUNK, c // 2, :], start=False, stop=True)
                    mm.then_inc(out_ok, 1)

                pair(0)
                pair(1)
                pair(2)
                keys(0)
                pair(3)
                keys(1)
                pair(4)
                updates(0)
                pair(5)
                pair(6)
                updates(1)
                output(0)
                output(1)

            pe.wait_ge(consts, 48)
            pe.wait_ge(zeroed, 3)
            project(0)
            over(pe, HG_HEADS, head)


def retention_heads(nc, dram, kept):
    NC = TT
    with Memory(nc, "reten") as m:
        raw = m.sb("raw", [P, 2, S])
        swapped = m.sb("swapped", [P, 2, S])
        rot = m.sb("rot", [P, 2, S])
        q_in = m.sb("q_in", [P, S])
        k_tok = m.sb("k_tok", [P, NC, P])
        scores = m.sb("scores", [P, NC, P])
        v = m.sb("v", [P, NC, RET_DV])
        state = m.sb("state", [P, NC, RET_DV])
        cos, sin = m.sb("cos", [P, S]), m.sb("sin", [P, S])
        intra = m.sb("intra", [P, RET_HEADS, P])
        inter = m.sb("inter", [P, RET_HEADS, P])
        to_state = m.sb("to_state", [P, RET_HEADS])
        decay = m.sb("decay", [P, RET_HEADS])
        sums = m.ps("sums", [P, 2, 2, HALF])
        keys_ps = m.ps("keys", [P, 4, P])
        pairs = m.ps("pairs", [P, 4, P])
        kv = m.ps("kv", [P, 2, RET_DV])
        outs = m.ps("outs", [P, 2, RET_DV])
        consts, zeroed = m.sem("consts"), m.sem("zeroed")
        projected, copied, swap_ok = m.sem("projected"), m.sem("copied"), m.sem("swap_ok")
        parts, rot_ok, q_in_ok = m.sem("parts"), m.sem("rot_ok"), m.sem("q_in_ok")
        k_turned, k_tok_ok = m.sem("k_turned"), m.sem("k_tok_ok")
        paired, scored = m.sem("paired"), m.sem("scored")
        kv_ok, state_ok = m.sem("kv_ok"), m.sem("state_ok")
        out_ok, out_stored, v_ok = m.sem("out_ok"), m.sem("out_stored"), m.sem("v_ok")
        ring = Ring(nc, m, KT, P, projected)
        values, ident = kept["values"], kept["ident"]
        w_in = dram["w_in"].rearrange("(k p) c -> p k c", p=P)
        SU = NC - 1
        H = P // 2
        block = m.block()

        @block.sync
        def _(sp):
            for tile, name in ((cos, "cos"), (sin, "sin"), (intra, "ret_intra"), (inter, "ret_inter"),
                               (to_state, "ret_to_state"), (decay, "ret_decay")):
                sp.dma_start(tile[:], dram[name]).then_inc(consts, 16)
            ring.load(sp, 0, 0, w_in[:, :, RQ:RQ + P])
            ring.load(sp, 0, 1, w_in[:, :, RK:RK + P])

            def head(i):
                if not at(i, RET_HEADS - 1):
                    ring.load(sp, i + 1, 0, w_in[:, :, bass.ds(RQ + P + i * RET_DK, P)])
                    ring.load(sp, i + 1, 1, w_in[:, :, bass.ds(RK + P + i * RET_DK, P)])
                sp.wait_ge(copied, 2 * i + 2)
                if not first(i):
                    sp.wait_ge(rot_ok, 2 * i)
                sp.dma_start(swapped[0:H], raw[H:P]).then_inc(swap_ok, 16)
                sp.dma_start(swapped[H:P], raw[0:H]).then_inc(swap_ok, 16)
            over(sp, RET_HEADS, head)

        @block.gpsimd
        def _(pool):
            def head(i):
                if not first(i):
                    pool.wait_ge(out_ok, 4 * i)
                nc.gpsimd.tensor_copy(v[:], values[:, :, bass.ds(HG_W + i * RET_DV, RET_DV)]).then_inc(v_ok, 1)
            over(pool, RET_HEADS, head)

        @block.scalar
        def _(act):
            act.wait_ge(consts, 16 * 6)
            ring.split_hi(act, 0, 0)
            ring.split_hi(act, 0, 1)

            def head(i):
                if not first(i):
                    act.wait_ge(rot_ok, 2 * i)
                    act.wait_ge(swap_ok, 32 * i)
                for u in range(2):
                    act.wait_ge(projected, 2 * i + u + 1)
                    nc.scalar.copy(raw[:, u, :], sums[:, u].rearrange("p a b -> p (a b)")).then_inc(copied, 1)
                if not at(i, RET_HEADS - 1):
                    ring.split_hi(act, i + 1, 0)
                    ring.split_hi(act, i + 1, 1)

                def keys(half):
                    act.wait_ge(consts, 16 * 6)
                    act.wait_ge(k_turned, 2 * i + half + 1)
                    nc.scalar.activation(k_tok[:, 4 * half:4 * half + 4, :], keys_ps[:], ACT.Copy,
                                         scale=to_state[:, bass.ds(i, 1)]).then_inc(k_tok_ok, 1)

                keys(0)
                keys(1)
                for g in range(4):
                    act.wait_ge(out_ok, 4 * i + g + 1)
                    nc.scalar.copy(values[:, 2 * g:2 * g + 2, bass.ds(HG_W + i * RET_DV, RET_DV)],
                                   outs[:]).then_inc(out_stored, 1)
            over(act, RET_HEADS, head)

        @block.vector
        def _(dve):
            nc.vector.memset(state[:, 0, :], 0.0).then_inc(zeroed, 1)
            dve.wait_ge(consts, 16 * 6)
            dve.wait_ge(zeroed, 1)
            ring.split_lo(dve, 0, 0)
            ring.split_lo(dve, 0, 1)

            def head(i):
                dve.wait_ge(copied, 2 * i + 2)
                dve.wait_ge(swap_ok, 32 * i + 32)
                nc.vector.tensor_tensor(raw[:], raw[:], bc(cos[:], 1, 2), ALU.mult).then_inc(parts, 1)
                nc.vector.tensor_tensor(swapped[:], swapped[:], bc(sin[:], 1, 2), ALU.mult).then_inc(parts, 1)
                dve.wait_ge(parts, 2 * i + 2)
                if not first(i):
                    dve.wait_ge(out_ok, 4 * i)
                for u in range(2):
                    nc.vector.tensor_tensor(rot[:, u, :], raw[:, u, :], swapped[:, u, :], ALU.add).then_inc(rot_ok, 1)
                dve.wait_ge(rot_ok, 2 * i + 1)
                nc.vector.tensor_tensor(q_in[:].rearrange("p (n c) -> p n c", c=P),
                                        rot[:, 0, :].rearrange("p (n c) -> p n c", c=P),
                                        inter[:, bass.ds(i, 1), :].to_broadcast([P, NC, P]),
                                        ALU.mult).then_inc(q_in_ok, 1)
                if not at(i, RET_HEADS - 1):
                    ring.split_lo(dve, i + 1, 0)
                    ring.split_lo(dve, i + 1, 1)

                def score(half):
                    dve.wait_ge(paired, 2 * i + half + 1)
                    nc.vector.tensor_tensor(scores[:, 4 * half:4 * half + 4, :], pairs[:],
                                            intra[:, bass.ds(i, 1), :].to_broadcast([P, 4, P]),
                                            ALU.mult).then_inc(scored, 1)

                def states(g):
                    dve.wait_ge(kv_ok, 4 * i + g + 1)
                    for c in range(2 * g, min(2 * g + 2, SU)):
                        if c:
                            dve.wait_ge(state_ok, SU * i + c)
                        nc.vector.scalar_tensor_tensor(out=state[:, c + 1, :], in0=state[:, c, :],
                                                       scalar=decay[:, bass.ds(i, 1)], in1=kv[:, c % 2, :],
                                                       op0=ALU.mult, op1=ALU.add).then_inc(state_ok, 1)

                score(0)
                score(1)
                for g in range(4):
                    states(g)
            over(dve, RET_HEADS, head)

        @block.tensor
        def _(pe):
            def project(i):
                for u in range(2):
                    if not first(i):
                        pe.wait_ge(copied, 2 * i - 1 + u)
                    project_block(nc, pe, ring, kept, i, u, sums[:, u], projected)

            def chunk(t, c):
                return t[:, c * P:(c + 1) * P]

            def head(i):
                if not at(i, RET_HEADS - 1):
                    project(i + 1)

                def keys(half):
                    pe.wait_ge(rot_ok, 2 * i + 2)
                    if half or not first(i):
                        pe.wait_ge(k_tok_ok, 2 * i + half)
                    for j in range(4):
                        mm = nc.tensor.transpose(keys_ps[:, j, :], chunk(rot[:, 1, :], 4 * half + j), ident[:])
                    mm.then_inc(k_turned, 1)

                def pair(half):
                    if half or not first(i):
                        pe.wait_ge(scored, 2 * i + half)
                    for j in range(4):
                        c = 4 * half + j
                        mm = nc.tensor.matmul(pairs[:, j, :], chunk(rot[:, 1, :], c), chunk(rot[:, 0, :], c),
                                              start=True, stop=True)
                    mm.then_inc(paired, 1)

                def updates(g):
                    if g:
                        pe.wait_ge(state_ok, SU * i + 2 * g)
                    else:
                        pe.wait_ge(k_tok_ok, 2 * i + 2)
                        pe.wait_ge(v_ok, i + 1)
                        if not first(i):
                            pe.wait_ge(state_ok, SU * i)
                    for c in range(2 * g, min(2 * g + 2, SU)):
                        mm = nc.tensor.matmul(kv[:, c % 2, :], k_tok[:, c, :], v[:, c, :], start=True, stop=True)
                    mm.then_inc(kv_ok, 1)

                def output(g):
                    if g or not first(i):
                        pe.wait_ge(out_stored, 4 * i + g)
                    pe.wait_ge(scored, 2 * i + g // 2 + 1)
                    pe.wait_ge(q_in_ok, i + 1)
                    pe.wait_ge(state_ok, SU * i + 2 * g + 1)
                    for c in range(2 * g, 2 * g + 2):
                        nc.tensor.matmul(outs[:, c % 2, :], scores[:, c, :], v[:, c, :], start=True, stop=False)
                        mm = nc.tensor.matmul(outs[:, c % 2, :], chunk(q_in[:], c), state[:, c, :],
                                              start=False, stop=True)
                    mm.then_inc(out_ok, 1)

                keys(0)
                pair(0)
                keys(1)
                pair(1)
                updates(0)
                updates(1)
                output(0)
                updates(2)
                output(1)
                updates(3)
                output(2)
                output(3)

            pe.wait_ge(consts, 16 * 6)
            pe.wait_ge(zeroed, 1)
            project(0)
            over(pe, RET_HEADS, head)


def gate_heads(nc, dram, kept):
    NJ = VW // P
    HG_PAIRS = HG_W // (2 * P)
    HEADS = HG_HEADS + RET_HEADS
    with Memory(nc, "gate") as m:
        values, y_hi, y_lo, ident = kept["values"], kept["y_hi"], kept["y_lo"], kept["ident"]
        sq = m.sb("sq", [P, VW])
        mean, root, rstd = (m.sb(n, [P, TT, HEADS]) for n in ("mean", "root", "rstd"))
        hg_gain, ret_gain = m.sb("hg_gain", [P, 1]), m.sb("ret_gain", [P, 2])
        scaled = m.sb("scaled", [P, TT, P])
        silu = m.sb("silu", [P, S])
        y = m.sb("y", [P, S])
        gates = m.ps("gates", [P, 2, 2, HALF])
        turned = m.ps("turned", [P, 2, TT, P])
        consts = m.sem("consts")
        squared, reduced = m.sem("squared"), m.sem("reduced")
        means, rooted, rstd_ok = m.sem("means"), m.sem("rooted"), m.sem("rstd_ok")
        projected, scaled_ok, turned_ok = m.sem("projected"), m.sem("scaled_ok"), m.sem("turned_ok")
        silu_ok, y_ok, hi_ok, lo_ok = m.sem("silu_ok"), m.sem("y_ok"), m.sem("hi_ok"), m.sem("lo_ok")
        ring = Ring(nc, m, KT, P, projected)
        w_in = dram["w_in"].rearrange("(k p) c -> p k c", p=P)
        block = m.block()

        def is_hg(i):
            return isinstance(i, int) and i < HG_PAIRS

        def over_pairs(eng, body):
            for i in range(HG_PAIRS):
                body(i)
            with eng.Fori(HG_PAIRS, NJ // 2 - 1) as i:
                body(i)
            body(NJ // 2 - 1)

        def is_last(i, u):
            return at(i, NJ // 2 - 1) and u == 1

        @block.sync
        def _(sp):
            sp.dma_start(hg_gain[:], dram["hg_norm"]).then_inc(consts, 16)
            sp.dma_start(ret_gain[:], dram["ret_norm"]).then_inc(consts, 16)

            def pair(i):
                for u in range(2):
                    col = HGATE + (2 * i + u) * P if is_hg(i) else RGATE + (2 * i + u - HG_W // P) * P
                    ring.load(sp, i, u, w_in[:, :, bass.ds(col, P)])
            over_pairs(sp, pair)

        @block.scalar
        def _(act):
            ring.split_hi(act, 0, 0)

            def squares(t):
                for n, (a, b) in enumerate(((0, HG_W), (HG_W, VW))):
                    if not first(t):
                        act.wait_ge(reduced, 2 * t - 1 + n)
                    nc.scalar.activation(sq[:, a:b], values[:, bass.ds(t, 1), a:b].rearrange("p o c -> p (o c)"),
                                         ACT.Square).then_inc(squared, 1)
            over(act, TT, squares)
            act.wait_ge(means, 2)
            nc.scalar.activation(root[:], mean[:], ACT.Sqrt).then_inc(rooted, 1)

            def pair(i):
                for u in range(2):
                    t = 2 * i + u
                    if not is_last(i, u):
                        ring.split_hi(act, i + u, 1 - u)
                    act.wait_ge(projected, t + 1)
                    if not (first(i) and u == 0):
                        act.wait_ge(y_ok, t)
                    nc.scalar.activation(silu[:], gates[:, u].rearrange("p a b -> p (a b)"),
                                         ACT.Silu).then_inc(silu_ok, 1)
                    act.wait_ge(y_ok, t + 1)
                    nc.scalar.copy(y_hi[:, :, bass.ds(t * P, P)],
                                   y[:].rearrange("p (a b) -> p a b", b=P)).then_inc(hi_ok, 1)
            over_pairs(act, pair)

        @block.vector
        def _(dve):
            ring.split_lo(dve, 0, 0)

            def sums(t):
                dve.wait_ge(squared, 2 * t + 1)
                nc.vector.reduce_sum(mean[:, bass.ds(t, 1), 0:HG_HEADS].rearrange("p o h -> p (o h)"),
                                     sq[:, 0:HG_W].rearrange("p (h c) -> p h c", c=HG_DV), AX.X).then_inc(reduced, 1)
                dve.wait_ge(squared, 2 * t + 2)
                nc.vector.reduce_sum(mean[:, bass.ds(t, 1), HG_HEADS:HEADS].rearrange("p o h -> p (o h)"),
                                     sq[:, HG_W:VW].rearrange("p (h c) -> p h c", c=RET_DV), AX.X).then_inc(reduced, 1)
            over(dve, TT, sums)
            dve.wait_ge(reduced, 2 * TT)
            nc.vector.tensor_scalar(mean[:, :, 0:HG_HEADS], mean[:, :, 0:HG_HEADS], 1.0 / HG_DV, EPS,
                                    ALU.mult, ALU.add).then_inc(means, 1)
            nc.vector.tensor_scalar(mean[:, :, HG_HEADS:HEADS], mean[:, :, HG_HEADS:HEADS], 1.0 / RET_DV, EPS,
                                    ALU.mult, ALU.add).then_inc(means, 1)
            dve.wait_ge(rooted, 1)
            nc.vector.reciprocal(rstd[:], root[:]).then_inc(rstd_ok, 1)
            dve.wait_ge(rstd_ok, 1)
            dve.wait_ge(consts, 32)

            def scale(i, u):
                t = 2 * i + u
                if not (first(i) and u == 0):
                    dve.wait_ge(turned_ok, t)
                head = bass.ds(t, 1) if is_hg(i) else bass.ds(i - HG_PAIRS + HG_HEADS, 1)
                nc.vector.tensor_tensor(scaled[:], values[:, :, bass.ds(t * P, P)],
                                        rstd[:, :, head].to_broadcast([P, TT, P]), ALU.mult).then_inc(scaled_ok, 1)

            scale(0, 0)

            def pair(i):
                for u in range(2):
                    t = 2 * i + u
                    if not is_last(i, u):
                        ring.split_lo(dve, i + u, 1 - u)
                        scale(i + u, 1 - u)
                    dve.wait_ge(silu_ok, t + 1)
                    dve.wait_ge(turned_ok, t + 1)
                    if not (first(i) and u == 0):
                        dve.wait_ge(lo_ok, t)
                        dve.wait_ge(hi_ok, t)
                    nc.vector.scalar_tensor_tensor(
                        out=y[:], in0=turned[:, u].rearrange("p a b -> p (a b)"),
                        scalar=hg_gain[:, 0:1] if is_hg(i) else ret_gain[:, u:u + 1],
                        in1=silu[:], op0=ALU.mult, op1=ALU.mult).then_inc(y_ok, 1)
                    dve.wait_ge(hi_ok, t + 1)
                    nc.vector.tensor_tensor(y_lo[:, bass.ds(t, 1), :].rearrange("p o (a b) -> p (o a) b", b=P),
                                            y[:].rearrange("p (a b) -> p a b", b=P),
                                            y_hi[:, :, bass.ds(t * P, P)].bitcast(F32), ALU.subtract).then_inc(lo_ok, 1)
            over_pairs(dve, pair)

        @block.tensor
        def _(pe):
            def pair(i):
                for u in range(2):
                    t = 2 * i + u
                    if not first(i):
                        pe.wait_ge(y_ok, t - 1)
                    project_block(nc, pe, ring, kept, i, u, gates[:, u], projected)
                    pe.wait_ge(scaled_ok, t + 1)
                    for j in range(TT):
                        mm = nc.tensor.transpose(turned[:, u, j, :], scaled[:, j, :], ident[:])
                    mm.then_inc(turned_ok, 1)
            over_pairs(pe, pair)


def merge_branches(nc, dram, kept):
    KA, KB = HG_W // P, RET_V // P
    with Memory(nc, "merge") as m:
        y_hi, y_lo = kept["y_hi"], kept["y_lo"]
        sig = m.sb("sig", [P, 2, S])
        merged = m.sb("merged", [P, S])
        sums = [m.ps(n, [P, 2, HALF]) for n in ("ga", "gb", "a", "b")]
        multiplied = m.sem("multiplied")
        sig_ok, gated, merged_ok, stored = m.sem("sig_ok"), m.sem("gated"), m.sem("merged_ok"), m.sem("stored")
        ring = Ring(nc, m, KT, P, multiplied)
        w_in = dram["w_in"].rearrange("(k p) c -> p k c", p=P)
        w_a = dram["w_a"].rearrange("(k p) c -> p k c", p=P)
        w_b = dram["w_b"].rearrange("(k p) c -> p k c", p=P)
        kts = [KT, KT, KA, KB]
        block = m.block()

        def slot(c, n):
            return 2 * c + n // 2, n % 2

        @block.sync
        def _(sp):
            def load(c, n):
                i, u = slot(c, n)
                src = [w_in[:, :, bass.ds(GA + c * P, P)], w_in[:, :, bass.ds(GB + c * P, P)],
                       w_a[:, :, bass.ds(c * P, P)], w_b[:, :, bass.ds(c * P, P)]][n]
                ring.load(sp, i, u, src, kts[n])

            load(0, 0)
            load(0, 1)

            def tile(c):
                load(c, 2)
                load(c, 3)
                if not at(c, KT - 1):
                    load(c + 1, 0)
                    load(c + 1, 1)
                sp.wait_ge(merged_ok, c + 1)
                sp.dma_start(dram["merged"][bass.ds(c * P, P), :], merged[:]).then_inc(stored, 16)
            over(sp, KT, tile)
            sp.wait_ge(stored, 16 * KT)

        @block.scalar
        def _(act):
            ring.split_hi(act, 0, 0)

            def tile(c):
                ring.split_hi(act, *slot(c, 1))
                for n in range(2):
                    act.wait_ge(multiplied, 4 * c + n + 1)
                    if not first(c):
                        act.wait_ge(merged_ok, c)
                    nc.scalar.activation(sig[:, n], sums[n][:].rearrange("p a b -> p (a b)"),
                                         ACT.Sigmoid).then_inc(sig_ok, 1)
                    ring.split_hi(act, *slot(c, 2 + n), kt=kts[2 + n])
                if not at(c, KT - 1):
                    ring.split_hi(act, *slot(c + 1, 0))
            over(act, KT, tile)

        @block.vector
        def _(dve):
            ring.split_lo(dve, 0, 0)

            def tile(c):
                for n in range(1, 4):
                    ring.split_lo(dve, *slot(c, n), kt=kts[n])
                for n in range(2):
                    dve.wait_ge(multiplied, 4 * c + 3 + n)
                    dve.wait_ge(sig_ok, 2 * c + n + 1)
                    nc.vector.tensor_tensor(sig[:, n], sums[2 + n][:].rearrange("p a b -> p (a b)"), sig[:, n],
                                            ALU.mult).then_inc(gated, 1)
                    if n == 0 and not at(c, KT - 1):
                        ring.split_lo(dve, *slot(c + 1, 0))
                dve.wait_ge(gated, 2 * c + 2)
                if not first(c):
                    dve.wait_ge(stored, 16 * c)
                nc.vector.tensor_tensor(merged[:], sig[:, 0], sig[:, 1], ALU.add).then_inc(merged_ok, 1)
            over(dve, KT, tile)

        @block.tensor
        def _(pe):
            def tile(c):
                for n in range(2):
                    i, u = slot(c, n)
                    if not first(c):
                        pe.wait_ge(sig_ok, 2 * c - 1 + n)
                    project_block(nc, pe, ring, kept, i, u, sums[n], multiplied)
                for n, (j0, kt) in enumerate(((0, KA), (KA, KB))):
                    i, u = slot(c, 2 + n)
                    if not first(c):
                        pe.wait_ge(gated, 2 * c - 1 + n)
                    pe.wait_ge(ring.lo_ok, 2 * i + u + 1)
                    for half in range(2):
                        out = sums[2 + n][:, half, :].rearrange("p (a b) -> p a b", b=P)
                        mm = three_passes(nc, out, [
                            (ring.hi[:, u, k, :], ring.lo[:, u, k, :],
                             y_hi[:, 4 * half:4 * half + 4, (j0 + k) * P:(j0 + k + 1) * P],
                             y_lo[:, j0 + k, half * HALF:(half + 1) * HALF].rearrange("p (a b) -> p a b", b=P))
                            for k in range(kt)])
                    mm.then_inc(multiplied, 1)
            over(pe, KT, tile)


def project_out(nc, dram, kept):
    with Memory(nc, "out") as m:
        x2 = kept["x2"]
        m_hi, m_lo = m.sb("m_hi", [P, KT, S], F32R), m.sb("m_lo", [P, KT, S], F32R)
        with Memory(nc, "outsplit") as n:
            raw = n.sb("raw", [P, 2, S])
            loaded = [n.sem(f"loaded{u}") for u in range(2)]
            x_ok, hi_ok, lo_ok = n.sem("x_ok"), n.sem("hi_ok"), n.sem("lo_ok")
            block = n.block()

            @block.sync
            def _(sp):
                def pair(i):
                    for u in range(2):
                        if not first(i):
                            sp.wait_ge(lo_ok, 2 * i - 1 + u)
                        sp.dma_start(raw[:, u], dram["merged"][bass.ds((2 * i + u) * P, P), :]).then_inc(loaded[u], 16)
                over(sp, KT // 2, pair)
                sp.dma_start(x2[:], dram["x"].rearrange("(t p) d -> p t d", p=P)).then_inc(x_ok, 16)
                sp.wait_ge(x_ok, 16)

            @block.scalar
            def _(act):
                def pair(i):
                    for u in range(2):
                        act.wait_ge(loaded[u], 16 * i + 16)
                        nc.scalar.copy(m_hi[:, bass.ds(2 * i + u, 1), :].rearrange("p o s -> p (o s)"),
                                       raw[:, u]).then_inc(hi_ok, 1)
                over(act, KT // 2, pair)

            @block.vector
            def _(dve):
                def pair(i):
                    for u in range(2):
                        dve.wait_ge(hi_ok, 2 * i + u + 1)
                        nc.vector.tensor_tensor(m_lo[:, bass.ds(2 * i + u, 1), :].rearrange("p o s -> p (o s)"), raw[:, u],
                                                m_hi[:, bass.ds(2 * i + u, 1), :].rearrange("p o s -> p (o s)").bitcast(F32),
                                                ALU.subtract).then_inc(lo_ok, 1)
                over(dve, KT // 2, pair)

        def store(eng, b, col, psum):
            dst = x2[:, 2 * b:2 * b + 2, bass.ds(col, 256)]
            return nc.vector.tensor_tensor(dst, psum, dst, ALU.add)

        tokens_out(nc, m, m_hi, m_lo, dram["w_out"], [(D // 512, 0)], store, [])


def route(nc, dram, kept):
    R = GROUPS + EXPERTS
    with Memory(nc, "route") as m:
        x2, ident, logits = kept["x2"], kept["ident"], kept["logits"]
        sq = m.sb("sq", [P, D])
        xn = m.sb("xn", [P, 2, D])
        stat = m.sb("stat", [P, 2, 4])
        whole = m.sb("whole", [P, 2, KT, P])
        w = m.sb("w", [P, KT, R])
        bias = m.sb("bias", [P, R])
        turned = m.ps("turned", [P, 2, KT, P])
        sums = m.ps("sums", [P, 2, HALF])
        consts, rows_out = m.sem("consts"), [m.sem(f"rows_out{u}") for u in range(2)]
        summed, mean, rooted, rstd = m.sem("summed"), m.sem("mean"), m.sem("rooted"), m.sem("rstd")
        scaled, turned_ok, gained = m.sem("scaled"), m.sem("turned_ok"), m.sem("gained")
        routed, logits_ok = m.sem("routed"), m.sem("logits_ok")
        gain = kept["ffn_gain"]
        block = m.block()

        @block.sync
        def _(sp):
            with nc.allow_non_contiguous_dma("router weights have 4 and 32 columns"):
                sp.dma_start(gain[:], dram["ffn_norm"]).then_inc(consts, 16)
                sp.dma_start(w[:, :, 0:GROUPS], dram["w_rg"].rearrange("(k p) c -> p k c", p=P)).then_inc(consts, 16)
                sp.dma_start(w[:, :, GROUPS:R], dram["w_re"].rearrange("(k p) c -> p k c", p=P)).then_inc(consts, 16)
                sp.dma_start(bias[:, 0:GROUPS], dram["b_rg"].to_broadcast([P, GROUPS])).then_inc(consts, 16)
                sp.dma_start(bias[:, GROUPS:R], dram["b_re"].to_broadcast([P, EXPERTS])).then_inc(consts, 16)

            def pair(i):
                for u in range(2):
                    t = 2 * i + u
                    sp.wait_ge(scaled, t + 1)
                    sp.dma_start(dram["rows"][bass.ds(t * P, P), :], xn[:, u, :]).then_inc(rows_out[u], 16)
            over(sp, TT // 2, pair)
            for u in range(2):
                sp.wait_ge(rows_out[u], 16 * TT // 2)

        @block.scalar
        def _(act):
            def pair(i):
                for u in range(2):
                    t = 2 * i + u
                    if not (first(i) and u == 0):
                        act.wait_ge(mean, t)
                    row = x2[:, bass.ds(t, 1), :].rearrange("p o d -> p (o d)")
                    nc.scalar.activation(sq[:], row, ACT.Square, accum_out=stat[:, u, 0:1]).then_inc(summed, 1)
                    act.wait_ge(mean, t + 1)
                    nc.scalar.activation(stat[:, u, 2:3], stat[:, u, 1:2], ACT.Sqrt).then_inc(rooted, 1)
                    act.wait_ge(rstd, t + 1)
                    if not first(i):
                        act.wait_ge(turned_ok, t - 1)
                        act.wait_ge(rows_out[u], 16 * i)
                    nc.scalar.activation(xn[:, u, :], row, ACT.Copy, scale=stat[:, u, 3:4]).then_inc(scaled, 1)
            for i in range(TT // 2):
                pair(i)

        @block.vector
        def _(dve):
            dve.wait_ge(consts, 80)

            def tail(t, u, old):
                dve.wait_ge(turned_ok, t + 1)
                if old:
                    dve.wait_ge(routed, t - 1)
                nc.vector.tensor_tensor(whole[:, u], turned[:, u], bc(gain[:], 2, P), ALU.mult).then_inc(gained, 1)
                dve.wait_ge(routed, t + 1)
                nc.vector.tensor_tensor(logits[:, bass.ds(t, 1), :].rearrange("p o r -> p (o r)"), sums[:, u, 0:R],
                                        bias[:], ALU.add).then_inc(logits_ok, 1)

            def pair(i):
                for u in range(2):
                    t = 2 * i + u
                    dve.wait_ge(summed, t + 1)
                    nc.vector.tensor_scalar(stat[:, u, 1:2], stat[:, u, 0:1], 1.0 / D, EPS,
                                            ALU.mult, ALU.add).then_inc(mean, 1)
                    dve.wait_ge(rooted, t + 1)
                    nc.vector.reciprocal(stat[:, u, 3:4], stat[:, u, 2:3]).then_inc(rstd, 1)
                    tail(t, u, not first(i))
            over(dve, TT // 2, pair)

        @block.tensor
        def _(pe):
            pe.wait_ge(consts, 80)

            def pair(i):
                for u in range(2):
                    t = 2 * i + u
                    pe.wait_ge(scaled, t + 1)
                    if not first(i):
                        pe.wait_ge(gained, t - 1)
                    for k in range(KT):
                        mm = nc.tensor.transpose(turned[:, u, k, :], xn[:, u, k * P:(k + 1) * P], ident[:])
                    mm.then_inc(turned_ok, 1)
                    pe.wait_ge(gained, t + 1)
                    if not first(i):
                        pe.wait_ge(logits_ok, t - 1)
                    for k in range(KT):
                        mm = nc.tensor.matmul(sums[:, u, 0:R], whole[:, u, k, :], w[:, k, :],
                                              start=(k == 0), stop=(k == KT - 1))
                    mm.then_inc(routed, 1)
            over(pe, TT // 2, pair)


def place(nc, dram, kept):
    T, G, E, N = TT, GROUPS, EXPERTS, PER_GROUP
    with Memory(nc, "place") as m:
        L = kept["logits"]
        names = ("gmax", "gsum", "gw", "gbest", "m1", "m2", "best", "p2", "den", "inv")
        small = {n: m.sb(n, [P, T]) for n in names}
        g4, g4b, gone = m.sb("g4", [P, T, G]), m.sb("g4b", [P, T, G]), m.sb("gone", [P, T, G])
        all32 = m.sb("all32", [P, T, G, N])
        e8, e8b, s8 = m.sb("e8", [P, T, N]), m.sb("e8b", [P, T, N]), m.sb("s8", [P, T, N])
        one8 = m.sb("one8", [P, 2, T, N])
        chosen = m.sb("chosen", [P, 2, T, E])
        either = m.sb("either", [P, T, E])
        prod = m.sb("prod", [P, 2, T, E])
        rank, base, ide = m.sb("rank", [P, 2, T]), m.sb("base", [P, 2, T]), m.sb("ide", [P, 2, T])
        rank_i, tile_i, row_i = (m.sb(n, [P, 2, T], I32) for n in ("rank_i", "tile_i", "row_i"))
        tile_f, row_f, is_over, col = (m.sb(n, [P, 2, T]) for n in ("tile_f", "row_f", "is_over", "col"))
        cnt_i, cnt_j, more = m.sb("cnt_i", [P, E], I32), m.sb("cnt_j", [P, E], I32), m.sb("more", [P, E])
        incl, excl = m.sb("incl", [P, E]), m.sb("excl", [P, E])
        below = m.sb("below", [P, OVER, E])
        owner = m.sb("owner", [P, OVER + 1])
        rows1 = m.sb("rows1", [P, 2 * T, P])
        cols1 = m.sb("cols1", [P, 2 * T, COLS])
        colv = m.sb("colv", [P, 2 * T, 2, COLS])
        full = m.sb("full", [P, 2, COLS])
        empty = m.sb("empty", [P, 2, COLS])
        desc, iota = m.sb("desc", [P, N]), m.sb("iota", [P, P])
        earlier, ones = m.sb("earlier", [P, P]), m.sb("ones", [P, P])
        ids = m.sb("ids", [P, 2 * T, 2])
        ps_rank = m.ps("ps_rank", [P, T, E])
        ps_count = m.ps("ps_count", [P, HALF])
        ps_slots = m.ps("ps_slots", [P, HALF])
        consts, v, a, pe_ok = m.sem("consts"), m.sem("dve"), m.sem("act"), m.sem("pe")
        block = m.block()

        @block.sync
        def _(sp):
            for tile, name in ((desc, "desc"), (iota, "iota"), (earlier, "earlier"), (ones, "ones"), (ids, "pair_ids")):
                sp.dma_start(tile[:], dram[name]).then_inc(consts, 16)

        marks = {}

        @block.vector
        def _(dve):
            V = nc.vector
            steps = Steps(dve, v)
            link = steps.link
            dve.wait_ge(consts, 80)
            Lg = L[:, :, 0:G]
            Le = L[:, :, G:G + E].rearrange("p t (g n) -> p t g n", g=G)
            one = [one8[:, k] for k in range(2)]

            def first_best(src, best, n, tmp, out):
                link(V.tensor_tensor(tmp, src, bc(best[:], 2, n), ALU.is_equal))
                link(V.tensor_tensor(tmp, tmp, bc(desc[:, N - n:N], 1, T), ALU.mult))
                link(V.reduce_max(small["best"][:], tmp, AX.X))
                link(V.tensor_tensor(out, tmp, bc(small["best"][:], 2, n), ALU.is_equal))

            link(V.reduce_max(small["gmax"][:], Lg, AX.X))
            link(V.tensor_tensor(g4[:], Lg, bc(small["gmax"][:], 2, G), ALU.subtract))
            marks["group"] = steps.n
            first_best(Lg, small["gmax"], G, g4b[:], gone[:])
            dve.wait_ge(a, 1)
            link(V.reduce_sum(small["gsum"][:], g4[:], AX.X))
            link(V.reciprocal(small["gw"][:], small["gsum"][:]))
            link(V.tensor_tensor(all32[:], Le, bc(gone[:], 3, N), ALU.mult))
            link(V.reduce_sum(e8[:], all32[:].rearrange("p t g n -> p t n g"), AX.X))
            link(V.reduce_max(small["m1"][:], e8[:], AX.X))
            first_best(e8[:], small["m1"], N, s8[:], one[0])
            link(V.scalar_tensor_tensor(out=e8b[:], in0=one[0], scalar=-3.0e38, in1=e8[:],
                                        op0=ALU.mult, op1=ALU.add))
            link(V.reduce_max(small["m2"][:], e8b[:], AX.X))
            first_best(e8b[:], small["m2"], N, s8[:], one[1])
            link(V.tensor_tensor(small["den"][:], small["m2"][:], small["m1"][:], ALU.subtract))
            marks["expert"] = steps.n
            for k in range(2):
                link(V.tensor_tensor(chosen[:, k].rearrange("p t (g n) -> p t g n", g=G),
                                     bc(gone[:], 3, N), bc(one[k], 2, G), ALU.mult))
            link(V.tensor_tensor(either[:], chosen[:, 0], chosen[:, 1], ALU.add))
            marks["either"] = steps.n
            dve.wait_ge(a, 2)
            link(V.tensor_scalar(small["den"][:], small["p2"][:], 1.0, None, ALU.add))
            link(V.reciprocal(small["inv"][:], small["den"][:]))
            link(V.tensor_tensor(kept["weight"][:, 0, :], small["inv"][:], small["gw"][:], ALU.mult))
            link(V.tensor_tensor(kept["weight"][:, 1, :], kept["weight"][:, 0, :], small["p2"][:], ALU.mult))
            dve.wait_ge(pe_ok, 1)
            link(V.tensor_copy(cnt_i[:], ps_count[:, 0:E]))
            link(V.tensor_scalar(cnt_j[:], cnt_i[:], P - 1, None, ALU.add))
            link(V.tensor_scalar(cnt_i[:], cnt_j[:], 7, None, ALU.arith_shift_right))
            link(V.tensor_copy(more[:], cnt_i[:]))
            link(V.tensor_scalar(more[:], more[:], -1.0, 0.0, ALU.add, ALU.max))
            link(V.tensor_tensor_scan(incl[:], ones[:, 0:E], more[:], 0.0, ALU.mult, ALU.add))
            link(V.tensor_tensor(excl[:], incl[:], more[:], ALU.subtract))
            link(V.tensor_tensor(below[:], bc(incl[:], 1, OVER), bc(iota[:, 0:OVER], 2, E), ALU.is_le))
            link(V.reduce_sum(owner[:, 0:OVER], below[:], AX.X))
            link(V.tensor_scalar(owner[:, 0:OVER], owner[:, 0:OVER], float(E - 1), None, ALU.min))
            link(V.tensor_copy(owner[:, OVER:OVER + 1], incl[:, E - 1:E]))
            link(V.tensor_copy(kept["owner"][:], owner[:]))
            dve.wait_ge(pe_ok, 2)
            for out, table in ((rank, ps_rank[:]), (ide, bc(iota[:, 0:E], 1, T)), (base, bc(excl[:], 1, T))):
                for k in range(2):
                    link(V.tensor_tensor(prod[:, k], chosen[:, k], table, ALU.mult))
                link(V.reduce_sum(out[:], prod[:], AX.X))
            link(V.tensor_copy(rank_i[:], rank[:]))
            link(V.tensor_scalar(tile_i[:], rank_i[:], 7, None, ALU.arith_shift_right))
            link(V.tensor_scalar(row_i[:], rank_i[:], P - 1, None, ALU.bitwise_and))
            link(V.tensor_copy(tile_f[:], tile_i[:]))
            link(V.tensor_copy(row_f[:], row_i[:]))
            link(V.tensor_scalar(is_over[:], tile_f[:], 1.0, None, ALU.min))
            link(V.tensor_tensor(col[:], base[:], tile_f[:], ALU.add))
            link(V.scalar_tensor_tensor(out=col[:], in0=col[:], scalar=float(E - 1), in1=ide[:],
                                        op0=ALU.add, op1=ALU.subtract))
            link(V.tensor_tensor(col[:], col[:], is_over[:], ALU.mult))
            link(V.tensor_tensor(col[:], col[:], ide[:], ALU.add))
            flat = lambda x: x[:].rearrange("p k t -> p (k t)")
            link(V.tensor_tensor(rows1[:], bc(flat(row_f), 2, P), bc(iota[:], 1, 2 * T), ALU.is_equal))
            link(V.tensor_tensor(cols1[:], bc(flat(col), 2, COLS), bc(iota[:, 0:COLS], 1, 2 * T), ALU.is_equal))
            for w in range(2):
                link(V.tensor_tensor(colv[:, :, w, :], cols1[:], bc(ids[:, :, w], 2, COLS), ALU.mult))
            marks["slots"] = steps.n
            dve.wait_ge(pe_ok, 3)
            link(V.tensor_copy(full[:], ps_slots[:, 0:2 * COLS].rearrange("p (w c) -> p w c", w=2)))
            link(V.tensor_scalar(empty[:], full[:], 0.0, float(FAR), ALU.is_equal, ALU.mult))
            link(V.scalar_tensor_tensor(out=full[:], in0=full[:], scalar=-1.0, in1=empty[:],
                                        op0=ALU.add, op1=ALU.add))
            link(V.tensor_copy(kept["slots"][:], full[:].rearrange("p w c -> p c w")))

        @block.scalar
        def _(act):
            act.wait_ge(v, marks["group"])
            nc.scalar.activation(g4[:], g4[:], ACT.Exp).then_inc(a, 1)
            act.wait_ge(v, marks["expert"])
            nc.scalar.activation(small["p2"][:], small["den"][:], ACT.Exp).then_inc(a, 1)

        @block.tensor
        def _(pe):
            pe.wait_ge(consts, 80)
            pe.wait_ge(v, marks["either"])
            for t in range(T):
                mm = nc.tensor.matmul(ps_count[:, 0:E], ones[:], either[:, t, :], start=(t == 0), stop=(t == T - 1))
            mm.then_inc(pe_ok, 1)
            for t in range(T):
                for s in range(t):
                    nc.tensor.matmul(ps_rank[:, t, :], ones[:], either[:, s, :], start=(s == 0), stop=False)
                mm = nc.tensor.matmul(ps_rank[:, t, :], earlier[:], either[:, t, :], start=(t == 0), stop=True)
            mm.then_inc(pe_ok, 1)
            pe.wait_ge(v, marks["slots"])
            for j in range(2 * T):
                mm = nc.tensor.matmul(ps_slots[:, 0:2 * COLS], rows1[:, j, :],
                                      colv[:, j].rearrange("p w c -> p (w c)"),
                                      start=(j == 0), stop=(j == 2 * T - 1))
            mm.then_inc(pe_ok, 1)


def expert_weights(dram, e):
    def of(name, k):
        return dram[name].rearrange("(e k p) c -> e p k c", p=P, k=k)[bass.ds(e, 1)].rearrange("o p k c -> p (o k) c")
    return of("w_eg", KT), of("w_eu", KT), of("w_ed", DE // P)


def run_experts(nc, dram, kept):
    KD = DE // P
    with Memory(nc, "moe") as m:
        ident, gain, slots, owner = kept["ident"], kept["ffn_gain"], kept["slots"], kept["owner"]
        w_gu = m.sb("w_gu", [P, 2, KT, 2, DE])
        w_d = m.sb("w_d", [P, 2, KD, D])
        x = m.sb("x", [P, 2, D])
        xT = m.sb("xT", [P, 2, KT, P])
        silu = m.sb("silu", [P, 2, DE])
        h = m.sb("h", [P, 2, DE])
        hT = m.sb("hT", [P, 2, KD, P])
        y = m.sb("y", [P, 2, D])
        idx = m.sb("idx", [P, 2, 2], I32)
        ps_x = m.ps("ps_x", [P, KT, P])
        ps_gu = m.ps("ps_gu", [P, 2, DE])
        ps_h = m.ps("ps_h", [P, 4, P])
        ps_y = m.ps("ps_y", [P, 2, HALF])
        gu_in = [m.sem(f"gu_in{u}") for u in range(2)]
        d_in = [m.sem(f"d_in{u}") for u in range(2)]
        zeroed, idx_ok = m.sem("zeroed"), m.sem("idx_ok")
        gathered = [m.sem(f"gathered{u}") for u in range(2)]
        scattered = [m.sem(f"scattered{u}") for u in range(2)]
        x_turned, xT_ok = m.sem("x_turned"), m.sem("xT_ok")
        gu_ok, silu_ok, h_ok = m.sem("gu_ok"), m.sem("silu_ok"), m.sem("h_ok")
        h_turned, hT_ok = m.sem("h_turned"), m.sem("hT_ok")
        down_ok, y_act, y_dve = m.sem("down_ok"), m.sem("y_act"), m.sem("y_dve")
        o = {n: m.sem("over_" + n) for n in ("w_in", "idx", "gathered", "x_turned", "xT", "gu", "silu", "h",
                                             "h_turned", "hT", "down", "y", "scattered")}
        block = m.block()
        PAIRS_OF_EXPERTS = EXPERTS // 2

        def load(sp, u, e, gu_sem, d_sem):
            g_src, u_src, d_src = expert_weights(dram, e)
            sp.dma_start(w_gu[:, u, :, 0, :], g_src).then_inc(gu_sem, 16)
            sp.dma_start(w_gu[:, u, :, 1, :], u_src).then_inc(gu_sem, 16)
            sp.dma_start(w_d[:, u], d_src).then_inc(d_sem, 16)

        def gather(pool, u, sem):
            pool.indirect_dma_start(x[:, u, :], None, dram["rows"],
                                    bass.IndirectOffsetOnAxis(ap=idx[:, u, 0:1], axis=0),
                                    bounds_check=S - 1, oob_is_err=False).then_inc(sem, 16)

        def scatter(pool, u, sem):
            pool.indirect_dma_start(dram["results"], bass.IndirectOffsetOnAxis(ap=idx[:, u, 1:2], axis=0),
                                    y[:, u, :], None, bounds_check=PAIRS - 1, oob_is_err=False).then_inc(sem, 16)

        def turn_x(u):
            for k in range(KT):
                mm = nc.tensor.transpose(ps_x[:, k, :], x[:, u, k * P:(k + 1) * P], ident[:])
            return mm

        def gate_up(u):
            out = ps_gu[:].rearrange("p a b -> p (a b)")
            for k in range(KT):
                mm = nc.tensor.matmul(out, xT[:, u, k, :], w_gu[:, u, k].rearrange("p a b -> p (a b)"),
                                      start=(k == 0), stop=(k == KT - 1))
            return mm

        def turn_h(u):
            for k in range(KD):
                mm = nc.tensor.transpose(ps_h[:, k, :], h[:, u, k * P:(k + 1) * P], ident[:])
            return mm

        def down(u):
            for half in range(2):
                for k in range(KD):
                    mm = nc.tensor.matmul(ps_y[:, half, :], hT[:, u, k, :],
                                          w_d[:, u, k, half * HALF:(half + 1) * HALF],
                                          start=(k == 0), stop=(k == KD - 1))
            return mm

        def further(eng, body):
            n = eng.value_load(owner[0:1, OVER:OVER + 1], min_val=0, max_val=OVER)
            with eng.Fori(0, OVER) as j:
                with eng.If(n > j):
                    body(j)

        @block.sync
        def _(sp):
            def pair(i):
                for u in range(2):
                    if not first(i):
                        sp.wait_ge(gu_ok, 2 * i - 1 + u)
                        sp.wait_ge(down_ok, 2 * i - 1 + u)
                    load(sp, u, 2 * i + u, gu_in[u], d_in[u])
            over(sp, PAIRS_OF_EXPERTS, pair)

            sp.wait_ge(gu_ok, EXPERTS)
            sp.wait_ge(down_ok, EXPERTS)

            def more(j):
                sp.wait_ge(o["scattered"], 16 * j)
                e = sp.value_load(owner[0:1, bass.ds(j, 1)], min_val=0, max_val=EXPERTS - 1)
                load(sp, 0, e, o["w_in"], o["w_in"])
            further(sp, more)

        @block.gpsimd
        def _(pool):
            for u in range(2):
                nc.gpsimd.memset(x[:, u, :], 0.0).then_inc(zeroed, 1)
            pool.wait_ge(zeroed, 2)

            def fetch(e):
                u = e % 2
                if e >= 2:
                    pool.wait_ge(scattered[u], 16 * (e // 2))
                nc.gpsimd.tensor_copy(idx[:, u, :], slots[:, e, :]).then_inc(idx_ok, 1)
                pool.wait_ge(idx_ok, e + 1)
                if e >= 2:
                    pool.wait_ge(x_turned, e - 1)
                gather(pool, u, gathered[u])

            fetch(0)
            for e in range(EXPERTS):
                if e + 1 < EXPERTS:
                    fetch(e + 1)
                pool.wait_ge(y_act, e + 1)
                pool.wait_ge(y_dve, e + 1)
                scatter(pool, e % 2, scattered[e % 2])
            for u in range(2):
                pool.wait_ge(scattered[u], 16 * PAIRS_OF_EXPERTS)

            n = pool.value_load(owner[0:1, OVER:OVER + 1], min_val=0, max_val=OVER)
            for j in range(OVER):
                with pool.If(n > j):
                    nc.gpsimd.tensor_copy(idx[:, 0, :], slots[:, EXPERTS + j, :]).then_inc(o["idx"], 1)
                    pool.wait_ge(o["idx"], j + 1)
                    gather(pool, 0, o["gathered"])
                    pool.wait_ge(o["y"], 2 * j + 2)
                    scatter(pool, 0, o["scattered"])
                    pool.wait_ge(o["scattered"], 16 * j + 16)

        @block.scalar
        def _(act):
            def store(t, u, old):
                act.wait_ge(down_ok, t + 1)
                if old is not None:
                    act.wait_ge(scattered[u], old)
                nc.scalar.copy(y[:, u, 0:HALF], ps_y[:, 0, :]).then_inc(y_act, 1)

            def pair(i):
                for u in range(2):
                    e = 2 * i + u
                    act.wait_ge(gu_ok, e + 1)
                    if not first(i):
                        act.wait_ge(h_ok, e - 1)
                    nc.scalar.activation(silu[:, u, :], ps_gu[:, 0, :], ACT.Silu).then_inc(silu_ok, 1)
                    if not (first(i) and u == 0):
                        store(e - 1, 1 - u, None if first(i) else (16 * i if u else 16 * i - 16))
                    act.wait_ge(h_turned, e + 1)
                    nc.scalar.copy(hT[:, u], ps_h[:, 0:KD, :]).then_inc(hT_ok, 1)
            over(act, PAIRS_OF_EXPERTS, pair)
            store(EXPERTS - 1, 1, 16 * (PAIRS_OF_EXPERTS - 1))

            def more(j):
                act.wait_ge(o["gu"], j + 1)
                nc.scalar.activation(silu[:, 0, :], ps_gu[:, 0, :], ACT.Silu).then_inc(o["silu"], 1)
                act.wait_ge(o["h_turned"], j + 1)
                nc.scalar.copy(hT[:, 0], ps_h[:, 0:KD, :]).then_inc(o["hT"], 1)
                act.wait_ge(o["down"], j + 1)
                for half in range(2):
                    nc.scalar.copy(y[:, 0, half * HALF:(half + 1) * HALF], ps_y[:, half, :]).then_inc(o["y"], 1)
            further(act, more)

        @block.vector
        def _(dve):
            def gained(e, u, old):
                dve.wait_ge(x_turned, e + 1)
                if old:
                    dve.wait_ge(gu_ok, e - 1)
                nc.vector.tensor_tensor(xT[:, u], ps_x[:], bc(gain[:], 2, P), ALU.mult).then_inc(xT_ok, 1)

            def store(t, u, old):
                dve.wait_ge(down_ok, t + 1)
                if old is not None:
                    dve.wait_ge(scattered[u], old)
                nc.vector.tensor_copy(y[:, u, HALF:D], ps_y[:, 1, :]).then_inc(y_dve, 1)

            gained(0, 0, False)

            def pair(i):
                for u in range(2):
                    e = 2 * i + u
                    dve.wait_ge(silu_ok, e + 1)
                    if not first(i):
                        dve.wait_ge(h_turned, e - 1)
                    nc.vector.tensor_tensor(h[:, u, :], silu[:, u, :], ps_gu[:, 1, :], ALU.mult).then_inc(h_ok, 1)
                    if not (first(i) and u == 0):
                        store(e - 1, 1 - u, None if first(i) else (16 * i if u else 16 * i - 16))
                    if not (at(i, PAIRS_OF_EXPERTS - 1) and u == 1):
                        gained(e + 1, 1 - u, not (first(i) and u == 0))
            over(dve, PAIRS_OF_EXPERTS, pair)
            store(EXPERTS - 1, 1, 16 * (PAIRS_OF_EXPERTS - 1))

            def more(j):
                dve.wait_ge(o["x_turned"], j + 1)
                nc.vector.tensor_tensor(xT[:, 0], ps_x[:], bc(gain[:], 2, P), ALU.mult).then_inc(o["xT"], 1)
                dve.wait_ge(o["silu"], j + 1)
                nc.vector.tensor_tensor(h[:, 0, :], silu[:, 0, :], ps_gu[:, 1, :], ALU.mult).then_inc(o["h"], 1)
            further(dve, more)

        @block.tensor
        def _(pe):
            def turn(i, u, e, old):
                pe.wait_ge(gathered[u], 16 * i + 16)
                if old:
                    pe.wait_ge(xT_ok, e)
                turn_x(u).then_inc(x_turned, 1)

            def last_down(e, u, i, old):
                pe.wait_ge(hT_ok, e + 1)
                pe.wait_ge(d_in[u], 16 * i + 16)
                if old:
                    pe.wait_ge(y_act, e)
                    pe.wait_ge(y_dve, e)
                down(u).then_inc(down_ok, 1)

            turn(0, 0, 0, False)

            def pair(i):
                for u in range(2):
                    e = 2 * i + u
                    pe.wait_ge(xT_ok, e + 1)
                    pe.wait_ge(gu_in[u], 32 * i + 32)
                    gate_up(u).then_inc(gu_ok, 1)
                    if not (first(i) and u == 0):
                        last_down(e - 1, 1 - u, i if u else i - 1, not (first(i) and u == 1))
                    pe.wait_ge(h_ok, e + 1)
                    if not (first(i) and u == 0):
                        pe.wait_ge(hT_ok, e)
                    turn_h(u).then_inc(h_turned, 1)
                    if not (at(i, PAIRS_OF_EXPERTS - 1) and u == 1):
                        turn(i + u, 1 - u, e + 1, True)
            over(pe, PAIRS_OF_EXPERTS, pair)
            last_down(EXPERTS - 1, 1, PAIRS_OF_EXPERTS - 1, True)

            pe.wait_ge(y_act, EXPERTS)
            pe.wait_ge(y_dve, EXPERTS)

            def more(j):
                pe.wait_ge(o["gathered"], 16 * j + 16)
                turn_x(0).then_inc(o["x_turned"], 1)
                pe.wait_ge(o["xT"], j + 1)
                pe.wait_ge(o["w_in"], 48 * j + 48)
                gate_up(0).then_inc(o["gu"], 1)
                pe.wait_ge(o["h"], j + 1)
                turn_h(0).then_inc(o["h_turned"], 1)
                pe.wait_ge(o["hT"], j + 1)
                down(0).then_inc(o["down"], 1)
            further(pe, more)


def finish(nc, dram, kept, out):
    KP = PLE // P
    with Memory(nc, "fin") as m:
        x2, weight, ident = kept["x2"], kept["weight"], kept["ident"]
        g_hi, g_lo = m.sb("g_hi", [P, KT, D], F32R), m.sb("g_lo", [P, KT, D], F32R)
        w_p = m.sb("w_p", [P, KP, D])
        raw = m.sb("raw", [P, 2, D])
        r = m.sb("r", [P, 2, 2, D])
        pt = m.sb("pt", [P, 2, PLE])
        pT = m.sb("pT", [P, KP, P])
        sq = m.sb("sq", [P, D])
        stat = m.sb("stat", [P, 2, 8])
        xn = m.sb("xn", [P, D])
        whole = m.sb("whole", [P, KT, P])
        t_hi, t_lo = m.sb("t_hi", [P, 2, KT, P], F32R), m.sb("t_lo", [P, 2, KT, P], F32R)
        gate = m.sb("gate", [P, D])
        res = m.sb("res", [P, D])
        ple_gain, out_gain = m.sb("ple_gain", [P, KT]), m.sb("out_gain", [P, D])
        turned = m.ps("turned", [P, KT, P])
        p_turned = m.ps("p_turned", [P, 4, P])
        s_gate, s_proj = m.ps("s_gate", [P, 2, HALF]), m.ps("s_proj", [P, 2, HALF])
        consts = m.sem("consts")
        w_loaded = [m.sem(f"w_loaded{u}") for u in range(2)]
        w_hi_ok, w_lo_ok = m.sem("w_hi_ok"), m.sem("w_lo_ok")
        rows_in = [m.sem(f"rows_in{u}") for u in range(2)]
        p_in = [m.sem(f"p_in{u}") for u in range(2)]
        added = m.sem("added")
        summed, mean, rooted, rstd, scaled = (m.sem(n) for n in ("summed", "mean", "rooted", "rstd", "scaled"))
        turned_ok, gained, hi_ok, lo_ok = (m.sem(n) for n in ("turned_ok", "gained", "hi_ok", "lo_ok"))
        p_turned_ok, pT_ok = m.sem("p_turned_ok"), m.sem("pT_ok")
        gate_mm, proj_mm, sig_ok = m.sem("gate_mm"), m.sem("proj_mm"), m.sem("sig_ok")
        mixed = m.sem("mixed")
        summed2, mean2, rooted2, rstd2 = (m.sem(n) for n in ("summed2", "mean2", "rooted2", "rstd2"))
        res_ok, stored = m.sem("res_ok"), m.sem("stored")
        block = m.block()

        @block.sync
        def _(sp):
            sp.dma_start(ple_gain[:], dram["ple_norm"]).then_inc(consts, 16)
            sp.dma_start(out_gain[:], dram["final_norm"].to_broadcast([P, D])).then_inc(consts, 16)
            sp.dma_start(w_p[:], dram["w_pp"].rearrange("(k p) c -> p k c", p=P)).then_inc(consts, 16)
            for t in range(TT + 1):
                if t < TT:
                    u = t % 2
                    if t >= 2:
                        sp.wait_ge(added, 2 * t - 2)
                    for k in range(2):
                        sp.dma_start(r[:, u, k, :], dram["results"][k * S + t * P:k * S + (t + 1) * P, :]).then_inc(rows_in[u], 16)
                    if t >= 2:
                        sp.wait_ge(p_turned_ok, t - 1)
                    sp.dma_start(pt[:, u, :], dram["p"][t * P:(t + 1) * P, :]).then_inc(p_in[u], 16)
                if t == 0:
                    for k in range(KT):
                        if k >= 2:
                            sp.wait_ge(w_lo_ok, k - 1)
                        sp.dma_start(raw[:, k % 2], dram["w_pg"][k * P:(k + 1) * P, :]).then_inc(w_loaded[k % 2], 16)
                if t >= 1:
                    sp.wait_ge(res_ok, t)
                    sp.dma_start(out[(t - 1) * P:t * P, :], res[:]).then_inc(stored, 16)
            sp.wait_ge(stored, 16 * TT)

        @block.scalar
        def _(act):
            A = nc.scalar

            def split(k):
                act.wait_ge(w_loaded[k % 2], 16 * (k // 2) + 16)
                A.copy(g_hi[:, k, :], raw[:, k % 2]).then_inc(w_hi_ok, 1)

            def front(t):
                act.wait_ge(added, 2 * t + 2)
                if t >= 1:
                    act.wait_ge(summed, t)
                    act.wait_ge(summed2, t - 1)
                    act.wait_ge(mean2, t - 1)
                u = t % 2
                A.activation(sq[:], x2[:, t, :], ACT.Square, accum_out=stat[:, u, 0:1]).then_inc(summed, 1)
                act.wait_ge(mean, t + 1)
                A.activation(stat[:, u, 2:3], stat[:, u, 1:2], ACT.Sqrt).then_inc(rooted, 1)
                act.wait_ge(rstd, t + 1)
                if t >= 1:
                    act.wait_ge(turned_ok, t)
                A.activation(xn[:], x2[:, t, :], ACT.Copy, scale=stat[:, u, 3:4]).then_inc(scaled, 1)
                act.wait_ge(gained, t + 1)
                if t >= 2:
                    act.wait_ge(gate_mm, t - 1)
                A.copy(t_hi[:, u], whole[:]).then_inc(hi_ok, 1)
                act.wait_ge(p_turned_ok, t + 1)
                if t >= 1:
                    act.wait_ge(proj_mm, t)
                A.copy(pT[:], p_turned[:, 0:KP, :]).then_inc(pT_ok, 1)

            def back(t):
                u = t % 2
                act.wait_ge(gate_mm, t + 1)
                if t >= 1:
                    act.wait_ge(mixed, 2 * t)
                A.activation(gate[:], s_gate[:].rearrange("p a b -> p (a b)"), ACT.Sigmoid).then_inc(sig_ok, 1)
                act.wait_ge(mixed, 2 * t + 2)
                act.wait_ge(summed, min(t + 2, TT))
                A.activation(sq[:], x2[:, t, :], ACT.Square, accum_out=stat[:, u, 4:5]).then_inc(summed2, 1)
                act.wait_ge(mean2, t + 1)
                A.activation(stat[:, u, 6:7], stat[:, u, 5:6], ACT.Sqrt).then_inc(rooted2, 1)

            for k in range(2):
                split(k)
            front(0)
            for k in range(2, KT):
                split(k)
            for t in range(TT):
                if t + 1 < TT:
                    front(t + 1)
                back(t)

        @block.vector
        def _(dve):
            V = nc.vector
            dve.wait_ge(consts, 48)

            def split(k):
                dve.wait_ge(w_hi_ok, k + 1)
                V.tensor_tensor(g_lo[:, k, :], raw[:, k % 2], g_hi[:, k, :].bitcast(F32), ALU.subtract).then_inc(w_lo_ok, 1)

            def front(t):
                u = t % 2
                dve.wait_ge(rows_in[u], 32 * (t // 2) + 32)
                for k in range(2):
                    if k:
                        dve.wait_ge(added, 2 * t + 1)
                    V.scalar_tensor_tensor(out=x2[:, t, :], in0=r[:, u, k, :], scalar=weight[:, k, t:t + 1],
                                           in1=x2[:, t, :], op0=ALU.mult, op1=ALU.add).then_inc(added, 1)
                dve.wait_ge(summed, t + 1)
                V.tensor_scalar(stat[:, u, 1:2], stat[:, u, 0:1], 1.0 / D, EPS, ALU.mult, ALU.add).then_inc(mean, 1)
                dve.wait_ge(rooted, t + 1)
                V.reciprocal(stat[:, u, 3:4], stat[:, u, 2:3]).then_inc(rstd, 1)
                dve.wait_ge(turned_ok, t + 1)
                if t >= 1:
                    dve.wait_ge(lo_ok, t)
                V.tensor_tensor(whole[:], turned[:], bc(ple_gain[:], 2, P), ALU.mult).then_inc(gained, 1)
                dve.wait_ge(hi_ok, t + 1)
                V.tensor_tensor(t_lo[:, u], whole[:], t_hi[:, u].bitcast(F32), ALU.subtract).then_inc(lo_ok, 1)

            def back(t):
                u = t % 2
                dve.wait_ge(sig_ok, t + 1)
                dve.wait_ge(proj_mm, t + 1)
                V.tensor_tensor(gate[:], s_proj[:].rearrange("p a b -> p (a b)"), gate[:], ALU.mult).then_inc(mixed, 1)
                dve.wait_ge(mixed, 2 * t + 1)
                V.tensor_tensor(x2[:, t, :], x2[:, t, :], gate[:], ALU.add).then_inc(mixed, 1)
                dve.wait_ge(summed2, t + 1)
                V.tensor_scalar(stat[:, u, 5:6], stat[:, u, 4:5], 1.0 / D, EPS, ALU.mult, ALU.add).then_inc(mean2, 1)
                dve.wait_ge(rooted2, t + 1)
                V.reciprocal(stat[:, u, 7:8], stat[:, u, 6:7]).then_inc(rstd2, 1)
                dve.wait_ge(rstd2, t + 1)
                if t >= 1:
                    dve.wait_ge(stored, 16 * t)
                V.scalar_tensor_tensor(out=res[:], in0=x2[:, t, :], scalar=stat[:, u, 7:8], in1=out_gain[:],
                                       op0=ALU.mult, op1=ALU.mult).then_inc(res_ok, 1)

            for k in range(2):
                split(k)
            front(0)
            for k in range(2, KT):
                split(k)
            for t in range(TT):
                if t + 1 < TT:
                    front(t + 1)
                back(t)

        @block.tensor
        def _(pe):
            pe.wait_ge(consts, 48)

            def front(t):
                pe.wait_ge(scaled, t + 1)
                if t >= 1:
                    pe.wait_ge(gained, t)
                for k in range(KT):
                    mm = nc.tensor.transpose(turned[:, k, :], xn[:, k * P:(k + 1) * P], ident[:])
                mm.then_inc(turned_ok, 1)
                pe.wait_ge(p_in[t % 2], 16 * (t // 2) + 16)
                if t >= 1:
                    pe.wait_ge(pT_ok, t)
                for k in range(KP):
                    mm = nc.tensor.transpose(p_turned[:, k, :], pt[:, t % 2, k * P:(k + 1) * P], ident[:])
                mm.then_inc(p_turned_ok, 1)

            front(0)
            pe.wait_ge(w_lo_ok, KT)
            for t in range(TT):
                u = t % 2
                pe.wait_ge(lo_ok, t + 1)
                if t >= 1:
                    pe.wait_ge(sig_ok, t)
                for half in range(2):
                    cols = slice(half * HALF, (half + 1) * HALF)
                    mm = three_passes(nc, s_gate[:, half, :], [(t_hi[:, u, k, :], t_lo[:, u, k, :], g_hi[:, k, cols],
                                                                g_lo[:, k, cols]) for k in range(KT)])
                mm.then_inc(gate_mm, 1)
                pe.wait_ge(pT_ok, t + 1)
                if t >= 1:
                    pe.wait_ge(mixed, 2 * t)
                for half in range(2):
                    for k in range(KP):
                        mm = nc.tensor.matmul(s_proj[:, half, :], pT[:, k, :], w_p[:, k, half * HALF:(half + 1) * HALF],
                                              start=(k == 0), stop=(k == KP - 1))
                mm.then_inc(proj_mm, 1)
                if t + 1 < TT:
                    front(t + 1)


def shape_constants():
    f32 = np.float32
    c = {"ident": np.eye(P, dtype=f32)}
    s, t = np.meshgrid(np.arange(HG_CHUNK), np.arange(HG_CHUNK), indexing="ij")
    masks = [(s // (2 * h) == t // (2 * h)) & (s // h % 2 == 0) & (t // h % 2 == 1) for h in LEVELS] + [s == t]
    masks = np.stack(masks, axis=1).astype(np.int32)
    c["hg_masks"] = np.concatenate([masks, masks], axis=0)
    c["hg_reset"] = np.tile((np.arange(S) % HG_CHUNK != 0).astype(f32), (P, 1))
    inv = f32(10000.0) ** (-np.arange(0, RET_DK, 2, dtype=f32) / f32(RET_DK))
    angle = np.arange(S, dtype=f32)[None, :] * inv[:, None]
    c["cos"] = np.tile(np.cos(angle), (2, 1)).astype(f32)
    c["sin"] = np.concatenate([-np.sin(angle), np.sin(angle)], axis=0).astype(f32)
    lg = np.log1p(-np.exp2(-5.0 - np.arange(RET_HEADS)))
    idx = np.arange(P)
    rel = idx[None, :] - idx[:, None]
    scale = RET_DK ** -0.5
    intra = np.where(rel[:, None, :] >= 0, np.exp(np.maximum(rel, 0)[:, None, :] * lg[None, :, None]), 0.0) * scale
    c["ret_intra"] = intra.astype(f32)
    inter = np.exp((idx[None, :] + 1.0) * lg[:, None]) * scale
    c["ret_inter"] = np.tile(inter[None], (P, 1, 1)).astype(f32)
    c["ret_to_state"] = np.exp((P - 1.0 - idx[:, None]) * lg[None, :]).astype(f32)
    c["desc"] = np.tile(np.arange(PER_GROUP, 0, -1, dtype=f32), (P, 1))
    c["iota"] = np.tile(np.arange(P, dtype=f32), (P, 1))
    c["earlier"] = np.triu(np.ones((P, P), f32), 1)
    c["ones"] = np.ones((P, P), f32)
    tok = np.arange(P)[:, None, None] + P * np.arange(TT)[None, None, :] + np.zeros((1, 2, 1))
    dst = tok + S * np.arange(2)[None, :, None]
    c["pair_ids"] = (np.stack([tok, dst], axis=-1) + 1).reshape(P, 2 * TT, 2).astype(f32)
    c["ret_decay"] = np.tile(np.exp(P * lg)[None, :], (P, 1)).astype(f32)
    return c


def build(nc, dram, out):
    dram = dict(dram)
    Memory.sems.clear()
    dram["rows"] = nc.dram_tensor("rows", [S, D], F32, kind="Internal").ap()
    dram["results"] = nc.dram_tensor("results", [PAIRS, D], F32, kind="Internal").ap()
    dram["merged"] = nc.dram_tensor("merged", [D, S], F32, kind="Internal").ap()
    with Memory(nc, "kept") as top:
        kept = {"ident": top.sb("ident", [P, P])}
        with Memory(nc, "mix") as mix:
            kept["hT_hi"] = mix.sb("hT_hi", [P, KT, S], F32R)
            kept["hT_lo"] = mix.sb("hT_lo", [P, KT, S], F32R)
            with Memory(nc, "heads") as heads:
                kept["values"] = heads.sb("values", [P, TT, VW])
                normalise_input(nc, dram, kept)
                project_values(nc, dram, kept)
                hgrn_heads(nc, dram, kept)
                retention_heads(nc, dram, kept)
            kept["y_hi"] = mix.sb("y_hi", [P, TT, VW], F32R)
            kept["y_lo"] = mix.sb("y_lo", [P, VW // P, S], F32R)
            gate_heads(nc, dram, kept)
            merge_branches(nc, dram, kept)
        Memory.recycle(nc)
        kept["x2"] = top.sb("x2", [P, TT, D])
        project_out(nc, dram, kept)
        kept["logits"] = top.sb("logits", [P, TT, GROUPS + EXPERTS])
        kept["ffn_gain"] = top.sb("ffn_gain", [P, KT])
        kept["weight"] = top.sb("weight", [P, 2, TT])
        kept["slots"] = top.sb("slots", [P, COLS, 2], I32)
        kept["owner"] = top.sb("owner", [P, OVER + 1], I32)
        route(nc, dram, kept)
        place(nc, dram, kept)
        run_experts(nc, dram, kept)
        finish(nc, dram, kept, out)


def layout(x, p, mix_norm, w_in, hg_lb_logits, hg_norm, ret_norm, w_branch_a, w_branch_b, w_out,
           ffn_norm, w_router_group, b_router_group, w_router_expert, b_router_expert,
           w_expert_gate, w_expert_up, w_expert_down, ple_norm, w_ple_gate, w_ple_proj, final_norm):
    def turned(v):
        return np.ascontiguousarray(np.asarray(v).reshape(-1, P).T)

    a = {
        "x": x.reshape(S, D), "p": p.reshape(S, PLE), "w_in": w_in[0],
        "w_a": w_branch_a[0], "w_b": w_branch_b[0], "w_out": w_out[0],
        "w_rg": w_router_group[0], "w_re": w_router_expert[0], "b_rg": b_router_group, "b_re": b_router_expert,
        "w_eg": w_expert_gate.reshape(EXPERTS * D, DE), "w_eu": w_expert_up.reshape(EXPERTS * D, DE),
        "w_ed": w_expert_down.reshape(EXPERTS * DE, D),
        "w_pg": w_ple_gate[0], "w_pp": w_ple_proj[0], "final_norm": final_norm.reshape(1, D),
        "mix_norm": turned(mix_norm), "ffn_norm": turned(ffn_norm), "ple_norm": turned(ple_norm),
        "hg_norm": turned(hg_norm), "ret_norm": turned(ret_norm),
        "hg_lb_logits": hg_lb_logits.reshape(2, HG_HEADS, P).transpose(2, 0, 1),
    }
    a.update(shape_constants())
    return {n: np.ascontiguousarray(v) for n, v in a.items()}


def kernel(**inputs):
    from concourse import bacc
    from concourse.bass_utils import run_bass_kernel_spmd

    arrays = layout(**{n: np.asarray(v) for n, v in inputs.items()})
    nc = bacc.Bacc("TRN2", target_bir_lowering=False, num_devices=1)
    dram = {n: nc.dram_tensor(n, a.shape, mybir.dt.from_np(a.dtype), kind="ExternalInput").ap()
            for n, a in arrays.items()}
    out = nc.dram_tensor("out", (S, D), F32, kind="ExternalOutput").ap()
    build(nc, dram, out)
    result = run_bass_kernel_spmd(nc, [arrays], core_ids=[0])
    return result.results[0]["out"].reshape(1, S, D)
```

```python
from contextlib import ExitStack

import numpy as np

import concourse.bass as bass
import concourse.mybir as mybir

F32 = mybir.dt.float32
F32R = mybir.dt.float32r
I32 = mybir.dt.int32
ALU = mybir.AluOpType
ACT = mybir.ActivationFunctionType
AX = mybir.AxisListType

P = 128
S = 1024
D = 1024
KT = D // P
TT = S // P
HALF = 512
EPS = 1e-6

HG_HEADS, HG_DK, HG_DV = 4, 128, 128
HG_CHUNK = 64
HG_NC = S // HG_CHUNK
RET_HEADS, RET_DK, RET_DV = 4, 128, 256
HG_W = HG_HEADS * HG_DV
RET_QK = RET_HEADS * RET_DK
RET_V = RET_HEADS * RET_DV
VW = HG_W + RET_V
HQ, HF, HI, HGATE = 0, HG_W, 2 * HG_W, 3 * HG_W
RQ = 4 * HG_W
RK = RQ + RET_QK
RV = RK + RET_QK
RGATE = RV + RET_V
GA = RGATE + RET_V
GB = GA + D
IN_TOTAL = GB + D
PLE = 256

GROUPS, PER_GROUP = 4, 8
EXPERTS = GROUPS * PER_GROUP
DE = 256
PAIRS = 2 * S
OVER = (PAIRS - 1) // P
COLS = EXPERTS + OVER
LEVELS = [32, 16, 8, 4, 2, 1]
AHEAD = 4
FAR = 1 << 20
TABLES = ("desc", "iota", "earlier", "ones", "pair_ids")


class Steps:

    def __init__(self, eng, sem, base=0):
        self.eng, self.sem, self.base, self.n = eng, sem, base, 0

    def add(self, ins):
        ins.then_inc(self.sem, 1)
        self.n += 1
        return self.n

    def wait(self, n=None):
        self.eng.wait_ge(self.sem, self.base + (self.n if n is None else n))

    def link(self, ins):
        self.add(ins)
        self.wait()


def over(eng, n, body):
    body(0)
    if n > 2:
        with eng.Fori(1, n - 1) as i:
            body(i)
    if n > 1:
        body(n - 1)


def at(i, n):
    return isinstance(i, int) and i == n


def first(i):
    return at(i, 0)


def bc(ap, dim, n):
    a = ap.unsqueeze(dim)
    shape = list(a.shape)
    shape[dim] = n
    return a.to_broadcast(shape)


class Memory:

    sems = []

    @classmethod
    def recycle(cls, nc):
        nc.clear_and_free_semaphores(cls.sems)
        nc.all_engine_barrier()
        cls.sems.clear()

    def __init__(self, nc, stage):
        self.nc, self.stage, self.ctx = nc, stage, ExitStack()

    def __enter__(self):
        return self

    def __exit__(self, *a):
        return self.ctx.__exit__(*a)

    def sb(self, name, shape, dt=F32):
        return self.ctx.enter_context(self.nc.sbuf_tensor(f"{self.stage}_{name}", shape, dt))

    def ps(self, name, shape):
        return self.ctx.enter_context(self.nc.psum_tensor(f"{self.stage}_{name}", shape, F32))

    def sem(self, name):
        self.sems.append(self.nc.alloc_semaphore(f"{self.stage}_{name}"))
        return self.sems[-1]

    def block(self):
        return self.ctx.enter_context(self.nc.Block())


def normalise_input(nc, dram, kept):
    with Memory(nc, "norm") as m:
        xt = m.sb("xt", [P, TT, D])
        sq = m.sb("sq", [P, D])
        stat = m.sb("stat", [P, 4, TT])
        gain = m.sb("gain", [P, KT])
        whole = m.sb("whole", [P, 2, KT, P])
        turned = m.ps("turned", [P, 2, KT, P])
        loaded = [m.sem(f"loaded{t}") for t in range(TT)]
        consts = m.sem("consts")
        summed, mean, rooted, rstd = m.sem("summed"), m.sem("mean"), m.sem("rooted"), m.sem("rstd")
        scaled, turned_ok, gained = m.sem("scaled"), m.sem("turned_ok"), m.sem("gained")
        hi_ok, lo_ok = m.sem("hi_ok"), m.sem("lo_ok")
        block = m.block()

        @block.sync
        def _(sp):
            for t in range(TT):
                sp.dma_start(xt[:, t, :], dram["x"][t * P:(t + 1) * P, :]).then_inc(loaded[t], 16)
            sp.dma_start(gain[:], dram["mix_norm"]).then_inc(consts, 16)
            sp.dma_start(kept["ident"][:], dram["ident"]).then_inc(consts, 16)
            for u in range(2):
                src = dram["w_in"].rearrange("(k p) c -> p k c", p=P)[:, :, HI + u * 256:HI + (u + 1) * 256]
                sp.dma_start(kept["value_raw"][:, u], src).then_inc(kept["value_asked"][u], 16)

        @block.scalar
        def _(act):
            def statistics(part):
                tiles = range(part * TT // 2, (part + 1) * TT // 2)
                for t in tiles:
                    act.wait_ge(loaded[t], 16)
                    if t:
                        act.wait_ge(summed, t)
                    nc.scalar.activation(sq[:], xt[:, t, :], ACT.Square,
                                         accum_out=stat[:, 0, t:t + 1]).then_inc(summed, 1)
                act.wait_ge(mean, part + 1)
                nc.scalar.activation(stat[:, 2, tiles[0]:tiles[-1] + 1], stat[:, 1, tiles[0]:tiles[-1] + 1],
                                     ACT.Sqrt).then_inc(rooted, 1)
                act.wait_ge(rstd, part + 1)

            def hi(t, u):
                act.wait_ge(gained, t + 1)
                nc.scalar.copy(kept["hT_hi"][:, :, bass.ds(t * P, P)], whole[:, u, :, :]).then_inc(hi_ok, 1)

            for t in range(TT):
                if t % (TT // 2) == 0:
                    statistics(t // (TT // 2))
                nc.scalar.activation(xt[:, t, :], xt[:, t, :], ACT.Copy, scale=stat[:, 3, t:t + 1]).then_inc(scaled, 1)
                if t >= 1:
                    hi(t - 1, (t - 1) % 2)
            hi(TT - 1, (TT - 1) % 2)

        @block.tensor
        def _(pe):
            pe.wait_ge(consts, 32)

            def pair(i):
                for u in range(2):
                    t = 2 * i + u
                    pe.wait_ge(scaled, t + 1)
                    if not first(i):
                        pe.wait_ge(gained, t - 1)
                    for k in range(KT):
                        mm = nc.tensor.transpose(turned[:, u, k, :], xt[:, t, k * P:(k + 1) * P], kept["ident"][:])
                    mm.then_inc(turned_ok, 1)
            for i in range(TT // 2):
                pair(i)

        @block.vector
        def _(dve):
            def statistics(part):
                tiles = slice(part * TT // 2, (part + 1) * TT // 2)
                dve.wait_ge(summed, (part + 1) * TT // 2)
                nc.vector.tensor_scalar(stat[:, 1, tiles], stat[:, 0, tiles], 1.0 / D, EPS,
                                        ALU.mult, ALU.add).then_inc(mean, 1)
                dve.wait_ge(rooted, part + 1)
                nc.vector.reciprocal(stat[:, 3, tiles], stat[:, 2, tiles]).then_inc(rstd, 1)

            statistics(0)
            dve.wait_ge(consts, 32)

            def scale(t, u):
                dve.wait_ge(turned_ok, t + 1)
                if t >= 2:
                    dve.wait_ge(lo_ok, t - 1)
                nc.vector.tensor_tensor(whole[:, u, :, :], turned[:, u, :, :], bc(gain[:], 2, P),
                                        ALU.mult).then_inc(gained, 1)

            def lo(t, u):
                dve.wait_ge(hi_ok, t + 1)
                nc.vector.tensor_tensor(kept["hT_lo"][:, :, t * P:(t + 1) * P], whole[:, u, :, :],
                                        kept["hT_hi"][:, :, t * P:(t + 1) * P].bitcast(F32),
                                        ALU.subtract).then_inc(lo_ok, 1)

            scale(0, 0)
            for t in range(TT):
                if t == 2:
                    statistics(1)
                if t + 1 < TT:
                    scale(t + 1, (t + 1) % 2)
                lo(t, t % 2)


def three_passes(nc, out, parts):
    n = len(parts)
    for k, (sh, sl, mh, ml) in enumerate(parts):
        nc.tensor.matmul(out, sh, mh, start=(k == 0), stop=False)
        nc.tensor.matmul(out, sh, ml, start=False, stop=False)
        mm = nc.tensor.matmul(out, sl, mh, start=False, stop=(k == n - 1))
    return mm


class Ring:

    def __init__(self, nc, m, kt, w, used, per=1, name="w", slots=None, asked=None):
        self.nc = nc
        self.raw, self.hi, self.lo = slots or Ring.slots(m, kt, w, name)
        self.asked = asked is not None
        self.loaded = asked or [m.sem(f"{name}_loaded{u}") for u in range(2)]
        self.hi_ok, self.lo_ok = m.sem(name + "_hi_ok"), m.sem(name + "_lo_ok")
        self.used, self.per = used, per

    @staticmethod
    def slots(m, kt, w, name, raw=None):
        return (raw or m.sb(name + "_raw", [P, 2, kt, w]), m.sb(name + "_hi", [P, 2, kt, w], F32R),
                m.sb(name + "_lo", [P, 2, kt, w], F32R))

    def ask(self, sp, blocks, sources, loaded):
        sp.wait_ge(self.lo_ok, blocks)
        for u in range(2):
            sp.dma_start(self.raw[:, u], sources[u]).then_inc(loaded[u], 16)

    def load(self, sp, i, u, src, kt=KT):
        if first(i) and self.asked:
            return
        if not first(i):
            sp.wait_ge(self.lo_ok, 2 * i - 1 + u)
        sp.dma_start(self.raw[:, u, 0:kt], src).then_inc(self.loaded[u], 16)

    def split_hi(self, act, i, u, kt=KT):
        act.wait_ge(self.loaded[u], 16 * i + 16)
        if not first(i):
            act.wait_ge(self.used, self.per * (2 * i - 1 + u))
        self.nc.scalar.copy(self.hi[:, u, 0:kt], self.raw[:, u, 0:kt]).then_inc(self.hi_ok, 1)

    def split_lo(self, dve, i, u, kt=KT):
        dve.wait_ge(self.hi_ok, 2 * i + u + 1)
        self.nc.vector.tensor_tensor(self.lo[:, u, 0:kt], self.raw[:, u, 0:kt],
                                     self.hi[:, u, 0:kt].bitcast(F32), ALU.subtract).then_inc(self.lo_ok, 1)


def tokens_out(nc, m, src_hi, src_lo, w_dram, runs, store, act_banks, also=None, slots=None, asked=None):
    W = 256
    BANKS = TT // 2
    sums = m.ps("sums", [P, 2, BANKS, 2, W])
    full = m.sem("full")
    stored = {True: m.sem("stored_act"), False: m.sem("stored_dve")}
    dve_banks = [b for b in range(BANKS) if b not in act_banks]
    ring = Ring(nc, m, KT, W, full, BANKS, slots=slots, asked=asked)
    pairs = sum(n for n, _ in runs)
    w_dram = w_dram.rearrange("(k p) c -> p k c", p=P)
    block = m.block()

    @block.sync
    def _(sp):
        done = 0
        for n, col in runs:
            if done == 0:
                def pair(i, col=col):
                    for u in range(2):
                        ring.load(sp, i, u, w_dram[:, :, bass.ds(col + (2 * i + u) * W, W)])
                    if also is not None and first(i):
                        also[0](sp)
                over(sp, n, pair)
            else:
                with sp.Fori(done, done + n) as i:
                    for u in range(2):
                        ring.load(sp, i, u, w_dram[:, :, bass.ds(col + (2 * (i - done) + u) * W, W)])
            done += n

    def drain(eng, i, u, banks, mine):
        for b in banks:
            eng.wait_ge(full, (2 * i + u) * BANKS + b + 1)
            store(eng, b, (2 * i + u) * W, sums[:, u, b]).then_inc(stored[mine], 1)

    @block.scalar
    def _(act):
        ring.split_hi(act, 0, 0)

        def pair(i):
            ring.split_hi(act, i, 1)
            drain(act, i, 0, act_banks, True)
            if not at(i, pairs - 1):
                ring.split_hi(act, i + 1, 0)
            drain(act, i, 1, act_banks, True)
        over(act, pairs, pair)

    @block.vector
    def _(dve):
        ring.split_lo(dve, 0, 0)

        def pair(i):
            ring.split_lo(dve, i, 1)
            if also is not None and also[2] and first(i):
                dve.wait_ge(also[1], also[2])
            drain(dve, i, 0, dve_banks, False)
            if not at(i, pairs - 1):
                ring.split_lo(dve, i + 1, 0)
            drain(dve, i, 1, dve_banks, False)
        over(dve, pairs, pair)

    @block.tensor
    def _(pe):
        def pair(i):
            for u in range(2):
                pe.wait_ge(ring.lo_ok, 2 * i + u + 1)
                for tt in range(TT):
                    b = tt // 2
                    if not first(i) and tt % 2 == 0:
                        mine = b in act_banks
                        banks = act_banks if mine else dve_banks
                        pe.wait_ge(stored[mine], (2 * i - 2 + u) * len(banks) + banks.index(b) + 1)
                    mm = three_passes(nc, sums[:, u, b, tt % 2, :],
                                      [(src_hi[:, k, tt * P:(tt + 1) * P], src_lo[:, k, tt * P:(tt + 1) * P],
                                        ring.hi[:, u, k, :], ring.lo[:, u, k, :]) for k in range(KT)])
                    if tt % 2 == 1:
                        mm.then_inc(full, 1)
        over(pe, pairs, pair)


def project_values(nc, dram, kept):
    with Memory(nc, "vals") as m:
        values = kept["values"]

        def store(eng, b, col, psum):
            dst = values[:, 2 * b:2 * b + 2, bass.ds(col, 256)]
            if eng.engine == nc.scalar.engine:
                return nc.scalar.copy(dst, psum)
            return nc.vector.tensor_copy(dst, psum)

        def ask(sp):
            for u, src in enumerate(first_weights(dram, "hgrn")):
                sp.dma_start(kept["weight_slots"][0][:, u], src).then_inc(kept["asked"]["hgrn"][u], 16)

        tokens_out(nc, m, kept["hT_hi"], kept["hT_lo"], dram["w_in"], [(1, HI), (2, RV)], store, [0, 2], (ask, None, 0),
                   Ring.slots(m, KT, 256, "w", kept["value_raw"]), kept["value_asked"])


def first_weights(dram, stage):
    w_in = dram["w_in"].rearrange("(k p) c -> p k c", p=P)
    cols = {"hgrn": (HF, HQ), "reten": (RQ, RK), "gate": (HGATE, HGATE + P), "merge": (GA, GB)}[stage]
    return [w_in[:, :, c:c + P] for c in cols]


def project_block(nc, pe, ring, kept, i, u, sums, per_done, then=None):
    pe.wait_ge(ring.lo_ok, 2 * i + u + 1)
    for half in range(2):
        cols = slice(half * HALF, (half + 1) * HALF)
        mm = three_passes(nc, sums[:, half, :],
                          [(ring.hi[:, u, k, :], ring.lo[:, u, k, :], kept["hT_hi"][:, k, cols],
                            kept["hT_lo"][:, k, cols]) for k in range(KT)])
    mm.then_inc(per_done, 1)


def hgrn_heads(nc, dram, kept):
    NL = len(LEVELS)
    with Memory(nc, "hgrn") as m:
        ga, gb_, gc = m.sb("sig_z", [P, S]), m.sb("sig_minus_z", [P, S]), m.sb("sig_q", [P, S])
        q, k, b = m.sb("q", [P, S]), m.sb("k", [P, S]), m.sb("b", [P, S])
        X = m.sb("scaled", [P, 3, S])
        q_in, k_out = m.sb("q_in", [P, S]), m.sb("k_out", [P, S])
        k_tok = m.sb("k_tok", [P, TT, P])
        v = m.sb("v", [P, TT, HG_DV])
        scores = m.sb("scores", [P, TT, HG_CHUNK])
        state = m.sb("state", [P, HG_NC, HG_DV])
        masks = m.sb("masks", [P, NL + 1, HG_CHUNK], I32)
        reset = m.sb("reset", [P, S])
        ends = m.sb("ends", [P, HG_NC])
        logits = m.sb("logits", [P, 2, HG_HEADS])
        lb = m.sb("lb", [P, 4, HG_HEADS])
        tick = m.sb("tick", [P, NL + 1])
        ticked = m.sem("ticked")
        sums = m.ps("sums", [P, 2, 2, HALF])
        pairs = m.ps("pairs", [P, 2, TT, HG_CHUNK])
        kv = m.ps("kv", [P, 4, P])
        outs = m.ps("outs", [P, 4, HG_DV])
        consts, bound_d, bound, zeroed = m.sem("consts"), m.sem("bound_d"), m.sem("bound"), m.sem("zeroed")
        projected = m.sem("projected")
        sig = m.sem("sig")
        qk = m.sem("qk")
        sub, expd, mul = m.sem("sub"), m.sem("expd"), m.sem("mul")
        paired, masked = m.sem("paired"), m.sem("masked")
        since, tail_sub, tail = m.sem("since"), m.sem("tail_sub"), m.sem("tail")
        q_in_ok, k_out_ok = m.sem("q_in_ok"), m.sem("k_out_ok")
        k_turned, k_tok_ok = m.sem("k_turned"), m.sem("k_tok_ok")
        kv_ok, state_ok = m.sem("kv_ok"), m.sem("state_ok")
        out_ok, out_stored = m.sem("out_ok"), m.sem("out_stored")
        v_ok, ends_ok = m.sem("v_ok"), m.sem("ends_ok")
        ring = Ring(nc, m, KT, P, projected, slots=kept["weight_slots"], asked=kept["asked"]["hgrn"])
        values, ident = kept["values"], kept["ident"]
        w_in = dram["w_in"].rearrange("(k p) c -> p k c", p=P)
        SU = 15
        block = m.block()

        @block.sync
        def _(sp):
            sp.dma_start(masks[:], dram["hg_masks"]).then_inc(consts, 16)
            sp.dma_start(reset[:], dram["hg_reset"]).then_inc(consts, 16)
            sp.dma_start(logits[:], dram["hg_lb_logits"]).then_inc(consts, 16)

            for i in range(HG_HEADS):
                ring.load(sp, i, 0, w_in[:, :, HF + i * HG_DK:HF + (i + 1) * HG_DK])
                ring.load(sp, i, 1, w_in[:, :, HQ + i * HG_DK:HQ + (i + 1) * HG_DK])
            ring.ask(sp, 2 * HG_HEADS, first_weights(dram, "reten"), kept["asked"]["reten"])

        @block.gpsimd
        def _(pool):
            def head(i):
                if not first(i):
                    pool.wait_ge(out_ok, 2 * i)
                nc.gpsimd.tensor_copy(v[:], values[:, :, bass.ds(i * HG_DV, HG_DV)]).then_inc(v_ok, 1)
            over(pool, HG_HEADS, head)

        @block.scalar
        def _(act):
            ring.split_hi(act, 0, 0)
            ring.split_hi(act, 0, 1)
            act.wait_ge(bound_d, 1)
            nc.scalar.activation(lb[:, 1, :], lb[:, 0, :], ACT.Sigmoid).then_inc(bound, 1)
            nc.scalar.activation(lb[:, 2, :], lb[:, 0, :], ACT.Sigmoid, scale=-1.0).then_inc(bound, 1)
            act.wait_ge(bound, 2)

            def level(i, l):
                act.wait_ge(sub, 2 * NL * i + 2 * l + 2)
                nc.scalar.activation(X[:, l % 3, :], X[:, l % 3, :], ACT.Exp).then_inc(expd, 1)

            def gates(i):
                if not first(i):
                    act.wait_ge(k_out_ok, i)
                    act.wait_ge(q_in_ok, i)
                    act.wait_ge(ends_ok, i)
                act.wait_ge(projected, 2 * i + 1)
                nc.scalar.activation(ga[:], sums[:, 1].rearrange("p a b -> p (a b)"), ACT.Sigmoid).then_inc(sig, 1)
                nc.scalar.activation(gb_[:], sums[:, 1].rearrange("p a b -> p (a b)"), ACT.Sigmoid,
                                     scale=-1.0).then_inc(sig, 1)
                act.wait_ge(sig, 4 * i + 1)
                nc.scalar.activation(ga[:], ga[:], ACT.Ln, bias=lb[:, 1, bass.ds(i, 1)],
                                     scale=lb[:, 2, bass.ds(i, 1)]).then_inc(sig, 1)
                act.wait_ge(qk, 3 * i + 2)
                nc.scalar.activation(gb_[:], b[:], ACT.Exp).then_inc(since, 1)
                level(i, 0)
                level(i, 1)
                act.wait_ge(tail_sub, i + 1)
                nc.scalar.activation(ga[:], ga[:], ACT.Exp).then_inc(tail, 1)
                act.wait_ge(projected, 2 * i + 2)
                nc.scalar.activation(gc[:], sums[:, 0].rearrange("p a b -> p (a b)"), ACT.Sigmoid).then_inc(sig, 1)

            gates(0)

            def head(i):
                def keys(half):
                    act.wait_ge(k_turned, 2 * i + half + 1)
                    nc.scalar.copy(k_tok[:, 4 * half:4 * half + 4, :], kv[:]).then_inc(k_tok_ok, 1)

                if not at(i, HG_HEADS - 1):
                    ring.split_hi(act, i + 1, 0)
                level(i, 2)
                if not at(i, HG_HEADS - 1):
                    ring.split_hi(act, i + 1, 1)
                level(i, 3)
                level(i, 4)
                keys(0)
                level(i, 5)
                keys(1)
                if not at(i, HG_HEADS - 1):
                    gates(i + 1)
                for half in range(2):
                    act.wait_ge(out_ok, 2 * i + half + 1)
                    nc.scalar.copy(values[:, 4 * half:4 * half + 4, bass.ds(i * HG_DV, HG_DV)],
                                   outs[:]).then_inc(out_stored, 1)
            over(act, HG_HEADS, head)

        @block.vector
        def _(dve):
            nc.vector.memset(scores[:], 0.0).then_inc(zeroed, 1)
            nc.vector.memset(state[:, 0, :], 0.0).then_inc(zeroed, 1)
            nc.vector.memset(lb[:, 3, :], 0.0).then_inc(zeroed, 1)
            ring.split_lo(dve, 0, 0)
            ring.split_lo(dve, 0, 1)
            dve.wait_ge(consts, 48)
            nc.vector.tensor_tensor(lb[:, 0, :], logits[:, 0, :], logits[:, 1, :], ALU.subtract).then_inc(bound_d, 1)
            dve.wait_ge(zeroed, 3)
            dve.wait_ge(bound, 2)

            def halves(t, h):
                v = t.rearrange("p (n two h) -> p n two h", two=2, h=h)
                return v[:, :, 0, :], v[:, :, 1, :]

            def exponents(l):
                h = LEVELS[l]
                lower, upper = halves(b[:], h)
                x_lower, x_upper = halves(X[:, l % 3, :], h)
                ref = lower[:, :, h - 1:h].to_broadcast([P, S // (2 * h), h])
                nc.vector.tensor_tensor(x_upper, upper, ref, ALU.subtract).then_inc(sub, 1)
                nc.vector.tensor_tensor(x_lower, ref, lower, ALU.subtract).then_inc(sub, 1)

            def gated(i):
                dve.wait_ge(sig, 4 * i + 2)
                nc.vector.tensor_scalar(k[:], gb_[:], lb[:, 2, bass.ds(i, 1)], None, ALU.mult).then_inc(qk, 1)
                dve.wait_ge(sig, 4 * i + 3)
                nc.vector.tensor_tensor_scan(b[:], reset[:], ga[:], 0.0, ALU.mult, ALU.add).then_inc(qk, 1)
                dve.wait_ge(qk, 3 * i + 2)
                exponents(0)
                exponents(1)
                bv = b[:].rearrange("p (n c) -> p n c", c=HG_CHUNK)
                nc.vector.tensor_tensor(ga[:].rearrange("p (n c) -> p n c", c=HG_CHUNK),
                                        bv[:, :, HG_CHUNK - 1:HG_CHUNK].to_broadcast([P, HG_NC, HG_CHUNK]), bv,
                                        ALU.subtract).then_inc(tail_sub, 1)
                dve.wait_ge(sig, 4 * i + 4)
                nc.vector.tensor_tensor(q[:], sums[:, 0].rearrange("p a b -> p (a b)"), gc[:], ALU.mult).then_inc(qk, 1)

            gated(0)

            def head(i):
                dve.wait_ge(qk, 3 * i + 3)

                def products(l):
                    h = LEVELS[l]
                    x_lower, x_upper = halves(X[:, l % 3, :], h)
                    dve.wait_ge(expd, NL * i + l + 1)
                    nc.vector.tensor_tensor(x_upper, x_upper, halves(q[:], h)[1], ALU.mult).then_inc(mul, 1)
                    nc.vector.tensor_tensor(x_lower, x_lower, halves(k[:], h)[0], ALU.mult).then_inc(mul, 1)

                def mask(n):
                    l = (n - 1) % (NL + 1)
                    dve.wait_ge(paired, (NL + 1) * i + n + 1)
                    if not (first(i) and n == 0):
                        dve.wait_ge(masked, (NL + 1) * i + n)
                    nc.vector.tensor_copy(tick[:, l:l + 1], lb[:, 3, 0:1]).then_inc(ticked, 1)
                    nc.vector.copy_predicated(scores[:], bc(masks[:, l, :], 1, TT), pairs[:, n % 2]).then_inc(masked, 1)

                def states(g):
                    dve.wait_ge(kv_ok, 2 * i + g + 1)
                    for c in range(8 * g, min(8 * g + 8, SU)):
                        if c:
                            dve.wait_ge(state_ok, SU * i + c)
                        nc.vector.scalar_tensor_tensor(
                            out=state[:, c + 1, :], in0=state[:, c, :],
                            scalar=ends[:, c:c + 1],
                            in1=(kv, outs)[c % 2][:, (c // 2) % 4, :], op0=ALU.mult, op1=ALU.add).then_inc(state_ok, 1)

                products(0)
                exponents(2)
                products(1)
                if not at(i, HG_HEADS - 1):
                    ring.split_lo(dve, i + 1, 0)
                dve.wait_ge(tail, i + 1)
                nc.vector.tensor_tensor(k_out[:], k[:], ga[:], ALU.mult).then_inc(k_out_ok, 1)
                mask(0)
                mask(1)
                exponents(3)
                products(2)
                if not first(i):
                    dve.wait_ge(out_ok, 2 * i)
                    dve.wait_ge(state_ok, SU * i)
                dve.wait_ge(since, i + 1)
                nc.vector.tensor_copy(ends[:], gb_[:].rearrange("p (n c) -> p n c", c=HG_CHUNK)[:, :, HG_CHUNK - 1]
                                      ).then_inc(ends_ok, 1)
                nc.vector.tensor_tensor(q_in[:], q[:], gb_[:], ALU.mult).then_inc(q_in_ok, 1)
                mask(2)
                if not at(i, HG_HEADS - 1):
                    ring.split_lo(dve, i + 1, 1)
                exponents(4)
                products(3)
                mask(3)
                exponents(5)
                products(4)
                mask(4)
                products(5)
                mask(5)
                dve.wait_ge(ends_ok, i + 1)
                states(0)
                mask(6)
                states(1)
                if not at(i, HG_HEADS - 1):
                    gated(i + 1)
            over(dve, HG_HEADS, head)

        @block.tensor
        def _(pe):
            def project_z(i):
                if not first(i):
                    pe.wait_ge(sig, 4 * i - 2)
                project_block(nc, pe, ring, kept, i, 0, sums[:, 1], projected)

            def project_q(i):
                if not first(i):
                    pe.wait_ge(qk, 3 * i)
                project_block(nc, pe, ring, kept, i, 1, sums[:, 0], projected)

            def chunk(t, c):
                return t[:, c * HG_CHUNK:(c + 1) * HG_CHUNK]

            def head(i):
                def pair(n):
                    l = (n - 1) % (NL + 1)
                    if l < NL:
                        pe.wait_ge(mul, 2 * NL * i + 2 * l + 2)
                    else:
                        pe.wait_ge(qk, 3 * i + 3)
                    if n >= 2:
                        pe.wait_ge(masked, (NL + 1) * i + n - 1)
                    elif not first(i):
                        pe.wait_ge(masked, (NL + 1) * i)
                    for c in range(HG_NC):
                        lhs, rhs = (X[:, l % 3, :], X[:, l % 3, :]) if l < NL else (k[:], q[:])
                        r = HG_CHUNK * (c % 2)
                        mm = nc.tensor.matmul(pairs[r:r + HG_CHUNK, n % 2, c // 2, :], chunk(lhs, c), chunk(rhs, c),
                                              start=True, stop=True)
                    mm.then_inc(paired, 1)

                def keys(half):
                    pe.wait_ge(k_out_ok, i + 1)
                    if half:
                        pe.wait_ge(k_tok_ok, 2 * i + 1)
                    elif not first(i):
                        pe.wait_ge(state_ok, SU * i)
                    for j in range(4):
                        t = 4 * half + j
                        mm = nc.tensor.transpose(kv[:, j, :], k_out[:, t * P:(t + 1) * P], ident[:])
                    mm.then_inc(k_turned, 1)

                def updates(g):
                    if g:
                        pe.wait_ge(state_ok, SU * i + 8)
                    else:
                        pe.wait_ge(k_tok_ok, 2 * i + 2)
                        pe.wait_ge(v_ok, i + 1)
                        if not first(i):
                            pe.wait_ge(out_stored, 2 * i)
                    for c in range(8 * g, min(8 * g + 8, SU)):
                        r = HG_CHUNK * (c % 2)
                        mm = nc.tensor.matmul((kv, outs)[c % 2][:, (c // 2) % 4, :], k_tok[r:r + HG_CHUNK, c // 2, :],
                                              v[r:r + HG_CHUNK, c // 2, :], start=True, stop=True)
                    mm.then_inc(kv_ok, 1)

                def output(half):
                    if half:
                        pe.wait_ge(out_stored, 2 * i + 1)
                    else:
                        pe.wait_ge(masked, (NL + 1) * i + NL + 1)
                        pe.wait_ge(q_in_ok, i + 1)
                        pe.wait_ge(state_ok, SU * i + SU)
                    for c in range(8 * half, 8 * half + 8):
                        r = HG_CHUNK * (c % 2)
                        out = outs[r:r + HG_CHUNK, (c // 2) % 4, :]
                        nc.tensor.matmul(out, chunk(q_in[:], c), state[:, c, :], start=True, stop=False)
                        mm = nc.tensor.matmul(out, scores[r:r + HG_CHUNK, c // 2, :],
                                              v[r:r + HG_CHUNK, c // 2, :], start=False, stop=True)
                    mm.then_inc(out_ok, 1)

                pair(0)
                pair(1)
                pair(2)
                pair(3)
                keys(0)
                if not at(i, HG_HEADS - 1):
                    project_z(i + 1)
                pair(4)
                keys(1)
                pair(5)
                updates(0)
                pair(6)
                updates(1)
                if not at(i, HG_HEADS - 1):
                    project_q(i + 1)
                output(0)
                output(1)

            project_z(0)
            project_q(0)
            pe.wait_ge(zeroed, 3)
            over(pe, HG_HEADS, head)


def retention_heads(nc, dram, kept):
    NC = TT
    with Memory(nc, "reten") as m:
        raw = m.sb("raw", [P, 2, S])
        swapped = m.sb("swapped", [P, 2, S])
        rot = m.sb("rot", [P, 2, S])
        q_in = m.sb("q_in", [P, S])
        k_tok = m.sb("k_tok", [P, NC, P])
        scores = m.sb("scores", [P, NC, P])
        v = m.sb("v", [P, NC, RET_DV])
        state = m.sb("state", [P, NC, RET_DV])
        cos, sin = m.sb("cos", [P, S]), m.sb("sin", [P, S])
        intra = m.sb("intra", [P, RET_HEADS, P])
        inter = m.sb("inter", [P, RET_HEADS, P])
        to_state = m.sb("to_state", [P, RET_HEADS])
        decay = m.sb("decay", [P, RET_HEADS])
        sums = m.ps("sums", [P, 2, 2, HALF])
        keys_ps = m.ps("keys", [P, 4, P])
        pairs = m.ps("pairs", [P, 4, P])
        kv = m.ps("kv", [P, 2, RET_DV])
        outs = m.ps("outs", [P, 2, RET_DV])
        consts, zeroed = m.sem("consts"), m.sem("zeroed")
        projected, copied, swap_ok = m.sem("projected"), m.sem("copied"), m.sem("swap_ok")
        parts, rot_ok, q_in_ok = m.sem("parts"), m.sem("rot_ok"), m.sem("q_in_ok")
        k_turned, k_tok_ok = m.sem("k_turned"), m.sem("k_tok_ok")
        paired, scored = m.sem("paired"), m.sem("scored")
        kv_ok, state_ok = m.sem("kv_ok"), m.sem("state_ok")
        out_ok, out_stored, v_ok = m.sem("out_ok"), m.sem("out_stored"), m.sem("v_ok")
        ring = Ring(nc, m, KT, P, projected, slots=kept["weight_slots"], asked=kept["asked"]["reten"])
        values, ident = kept["values"], kept["ident"]
        w_in = dram["w_in"].rearrange("(k p) c -> p k c", p=P)
        SU = NC - 1
        H = P // 2
        block = m.block()

        @block.sync
        def _(sp):
            for tile, name in ((cos, "cos"), (sin, "sin"), (intra, "ret_intra"), (inter, "ret_inter"),
                               (to_state, "ret_to_state"), (decay, "ret_decay")):
                sp.dma_start(tile[:], dram[name]).then_inc(consts, 16)

            def head(i):
                if not at(i, RET_HEADS - 1):
                    ring.load(sp, i + 1, 0, w_in[:, :, bass.ds(RQ + P + i * RET_DK, P)])
                    ring.load(sp, i + 1, 1, w_in[:, :, bass.ds(RK + P + i * RET_DK, P)])
                sp.wait_ge(copied, 2 * i + 2)
                if not first(i):
                    sp.wait_ge(rot_ok, 2 * i)
                sp.dma_start(swapped[0:H], raw[H:P]).then_inc(swap_ok, 16)
                sp.dma_start(swapped[H:P], raw[0:H]).then_inc(swap_ok, 16)
            over(sp, RET_HEADS, head)
            ring.ask(sp, 2 * RET_HEADS, first_weights(dram, "gate"), kept["asked"]["gate"])

        @block.gpsimd
        def _(pool):
            def head(i):
                if not first(i):
                    pool.wait_ge(out_ok, 4 * i)
                nc.gpsimd.tensor_copy(v[:], values[:, :, bass.ds(HG_W + i * RET_DV, RET_DV)]).then_inc(v_ok, 1)
            over(pool, RET_HEADS, head)

        @block.scalar
        def _(act):
            ring.split_hi(act, 0, 0)
            ring.split_hi(act, 0, 1)
            act.wait_ge(consts, 16 * 6)

            def head(i):
                if not at(i, RET_HEADS - 1):
                    ring.split_hi(act, i + 1, 0)
                if not first(i):
                    act.wait_ge(rot_ok, 2 * i)
                    act.wait_ge(swap_ok, 32 * i)
                for u in range(2):
                    act.wait_ge(projected, 2 * i + u + 1)
                    nc.scalar.copy(raw[:, u, :], sums[:, u].rearrange("p a b -> p (a b)")).then_inc(copied, 1)
                if not at(i, RET_HEADS - 1):
                    ring.split_hi(act, i + 1, 1)

                def keys(half):
                    act.wait_ge(consts, 16 * 6)
                    act.wait_ge(k_turned, 2 * i + half + 1)
                    nc.scalar.activation(k_tok[:, 4 * half:4 * half + 4, :], keys_ps[:], ACT.Copy,
                                         scale=to_state[:, bass.ds(i, 1)]).then_inc(k_tok_ok, 1)

                keys(0)
                keys(1)
                for g in range(4):
                    act.wait_ge(out_ok, 4 * i + g + 1)
                    nc.scalar.copy(values[:, 2 * g:2 * g + 2, bass.ds(HG_W + i * RET_DV, RET_DV)],
                                   outs[:]).then_inc(out_stored, 1)
            over(act, RET_HEADS, head)

        @block.vector
        def _(dve):
            nc.vector.memset(state[:, 0, :], 0.0).then_inc(zeroed, 1)
            ring.split_lo(dve, 0, 0)
            ring.split_lo(dve, 0, 1)
            dve.wait_ge(consts, 16 * 6)
            dve.wait_ge(zeroed, 1)

            def head(i):
                if not at(i, RET_HEADS - 1):
                    ring.split_lo(dve, i + 1, 0)
                    ring.split_lo(dve, i + 1, 1)
                dve.wait_ge(copied, 2 * i + 2)
                if not first(i):
                    dve.wait_ge(out_ok, 4 * i)
                nc.vector.tensor_tensor(rot[:], raw[:], bc(cos[:], 1, 2), ALU.mult).then_inc(parts, 1)
                dve.wait_ge(swap_ok, 32 * i + 32)
                nc.vector.tensor_tensor(swapped[:], swapped[:], bc(sin[:], 1, 2), ALU.mult).then_inc(parts, 1)
                dve.wait_ge(parts, 2 * i + 2)
                for u in range(2):
                    nc.vector.tensor_tensor(rot[:, u, :], rot[:, u, :], swapped[:, u, :], ALU.add).then_inc(rot_ok, 1)
                dve.wait_ge(rot_ok, 2 * i + 1)
                nc.vector.tensor_tensor(q_in[:].rearrange("p (n c) -> p n c", c=P),
                                        rot[:, 0, :].rearrange("p (n c) -> p n c", c=P),
                                        inter[:, bass.ds(i, 1), :].to_broadcast([P, NC, P]),
                                        ALU.mult).then_inc(q_in_ok, 1)
                def score(half):
                    dve.wait_ge(paired, 2 * i + half + 1)
                    nc.vector.tensor_tensor(scores[:, 4 * half:4 * half + 4, :], pairs[:],
                                            intra[:, bass.ds(i, 1), :].to_broadcast([P, 4, P]),
                                            ALU.mult).then_inc(scored, 1)

                def states(g):
                    dve.wait_ge(kv_ok, 4 * i + g + 1)
                    for c in range(2 * g, min(2 * g + 2, SU)):
                        if c:
                            dve.wait_ge(state_ok, SU * i + c)
                        nc.vector.scalar_tensor_tensor(out=state[:, c + 1, :], in0=state[:, c, :],
                                                       scalar=decay[:, bass.ds(i, 1)], in1=kv[:, c % 2, :],
                                                       op0=ALU.mult, op1=ALU.add).then_inc(state_ok, 1)

                score(0)
                score(1)
                for g in range(4):
                    states(g)
            over(dve, RET_HEADS, head)

        @block.tensor
        def _(pe):
            def project(i):
                for u in range(2):
                    if not first(i):
                        pe.wait_ge(copied, 2 * i - 1 + u)
                    project_block(nc, pe, ring, kept, i, u, sums[:, u], projected)

            def chunk(t, c):
                return t[:, c * P:(c + 1) * P]

            def head(i):
                if not at(i, RET_HEADS - 1):
                    project(i + 1)

                def keys(half):
                    pe.wait_ge(rot_ok, 2 * i + 2)
                    if half or not first(i):
                        pe.wait_ge(k_tok_ok, 2 * i + half)
                    for j in range(4):
                        mm = nc.tensor.transpose(keys_ps[:, j, :], chunk(rot[:, 1, :], 4 * half + j), ident[:])
                    mm.then_inc(k_turned, 1)

                def pair(half):
                    if half or not first(i):
                        pe.wait_ge(scored, 2 * i + half)
                    for j in range(4):
                        c = 4 * half + j
                        mm = nc.tensor.matmul(pairs[:, j, :], chunk(rot[:, 1, :], c), chunk(rot[:, 0, :], c),
                                              start=True, stop=True)
                    mm.then_inc(paired, 1)

                def updates(g):
                    if g:
                        pe.wait_ge(state_ok, SU * i + 2 * g)
                    else:
                        pe.wait_ge(k_tok_ok, 2 * i + 2)
                        pe.wait_ge(v_ok, i + 1)
                        if not first(i):
                            pe.wait_ge(state_ok, SU * i)
                    for c in range(2 * g, min(2 * g + 2, SU)):
                        mm = nc.tensor.matmul(kv[:, c % 2, :], k_tok[:, c, :], v[:, c, :], start=True, stop=True)
                    mm.then_inc(kv_ok, 1)

                def output(g):
                    if g or not first(i):
                        pe.wait_ge(out_stored, 4 * i + g)
                    pe.wait_ge(scored, 2 * i + g // 2 + 1)
                    pe.wait_ge(q_in_ok, i + 1)
                    pe.wait_ge(state_ok, SU * i + 2 * g + 1)
                    for c in range(2 * g, 2 * g + 2):
                        nc.tensor.matmul(outs[:, c % 2, :], scores[:, c, :], v[:, c, :], start=True, stop=False)
                        mm = nc.tensor.matmul(outs[:, c % 2, :], chunk(q_in[:], c), state[:, c, :],
                                              start=False, stop=True)
                    mm.then_inc(out_ok, 1)

                keys(0)
                pair(0)
                keys(1)
                pair(1)
                updates(0)
                updates(1)
                output(0)
                updates(2)
                output(1)
                updates(3)
                output(2)
                output(3)

            project(0)
            pe.wait_ge(zeroed, 1)
            over(pe, RET_HEADS, head)


def gate_heads(nc, dram, kept):
    NJ = VW // P
    HG_PAIRS = HG_W // (2 * P)
    HEADS = HG_HEADS + RET_HEADS
    with Memory(nc, "gate") as m:
        values, y_hi, y_lo, ident = kept["values"], kept["y_hi"], kept["y_lo"], kept["ident"]
        sq = m.sb("sq", [P, VW])
        mean, root, rstd = (m.sb(n, [P, TT, HEADS]) for n in ("mean", "root", "rstd"))
        hg_gain, ret_gain = m.sb("hg_gain", [P, 1]), m.sb("ret_gain", [P, 2])
        scaled = m.sb("scaled", [P, TT, P])
        silu = m.sb("silu", [P, S])
        y = m.sb("y", [P, S])
        gates = m.ps("gates", [P, 2, 2, HALF])
        turned = m.ps("turned", [P, 2, TT, P])
        consts = m.sem("consts")
        squared, reduced = m.sem("squared"), m.sem("reduced")
        means, rooted, rstd_ok = m.sem("means"), m.sem("rooted"), m.sem("rstd_ok")
        projected, scaled_ok, turned_ok = m.sem("projected"), m.sem("scaled_ok"), m.sem("turned_ok")
        silu_ok, y_ok, hi_ok, lo_ok = m.sem("silu_ok"), m.sem("y_ok"), m.sem("hi_ok"), m.sem("lo_ok")
        ring = Ring(nc, m, KT, P, projected, slots=kept["weight_slots"], asked=kept["asked"]["gate"])
        w_in = dram["w_in"].rearrange("(k p) c -> p k c", p=P)
        block = m.block()

        def is_hg(i):
            return isinstance(i, int) and i < HG_PAIRS

        def over_pairs(eng, body):
            for i in range(HG_PAIRS):
                body(i)
            with eng.Fori(HG_PAIRS, NJ // 2 - 1) as i:
                body(i)
            body(NJ // 2 - 1)

        def is_last(i, u):
            return at(i, NJ // 2 - 1) and u == 1

        @block.sync
        def _(sp):
            sp.dma_start(hg_gain[:], dram["hg_norm"]).then_inc(consts, 16)
            sp.dma_start(ret_gain[:], dram["ret_norm"]).then_inc(consts, 16)

            def pair(i):
                for u in range(2):
                    col = HGATE + (2 * i + u) * P if is_hg(i) else RGATE + (2 * i + u - HG_W // P) * P
                    ring.load(sp, i, u, w_in[:, :, bass.ds(col, P)])
            over_pairs(sp, pair)
            ring.ask(sp, NJ, first_weights(dram, "merge"), kept["asked"]["merge"])

        @block.scalar
        def _(act):
            ring.split_hi(act, 0, 0)
            ring.split_hi(act, 0, 1)

            def squares(t):
                for n, (a, b) in enumerate(((0, HG_W), (HG_W, VW))):
                    if not first(t):
                        act.wait_ge(reduced, 2 * t - 1 + n)
                    nc.scalar.activation(sq[:, a:b], values[:, bass.ds(t, 1), a:b].rearrange("p o c -> p (o c)"),
                                         ACT.Square).then_inc(squared, 1)
            over(act, TT, squares)
            act.wait_ge(means, 2)
            nc.scalar.activation(root[:], mean[:], ACT.Sqrt).then_inc(rooted, 1)

            def pair(i):
                for u in range(2):
                    t = 2 * i + u
                    act.wait_ge(projected, t + 1)
                    if not (first(i) and u == 0):
                        act.wait_ge(y_ok, t)
                    nc.scalar.activation(silu[:], gates[:, u].rearrange("p a b -> p (a b)"),
                                         ACT.Silu).then_inc(silu_ok, 1)
                    if not at(i, NJ // 2 - 1):
                        ring.split_hi(act, i + 1, u)
                    act.wait_ge(y_ok, t + 1)
                    nc.scalar.copy(y_hi[:, :, bass.ds(t * P, P)],
                                   y[:].rearrange("p (a b) -> p a b", b=P)).then_inc(hi_ok, 1)
            over_pairs(act, pair)

        @block.vector
        def _(dve):
            ring.split_lo(dve, 0, 0)
            ring.split_lo(dve, 0, 1)

            def sums(t):
                dve.wait_ge(squared, 2 * t + 1)
                nc.vector.reduce_sum(mean[:, bass.ds(t, 1), 0:HG_HEADS].rearrange("p o h -> p (o h)"),
                                     sq[:, 0:HG_W].rearrange("p (h c) -> p h c", c=HG_DV), AX.X).then_inc(reduced, 1)
                dve.wait_ge(squared, 2 * t + 2)
                nc.vector.reduce_sum(mean[:, bass.ds(t, 1), HG_HEADS:HEADS].rearrange("p o h -> p (o h)"),
                                     sq[:, HG_W:VW].rearrange("p (h c) -> p h c", c=RET_DV), AX.X).then_inc(reduced, 1)
            over(dve, TT, sums)
            dve.wait_ge(reduced, 2 * TT)
            nc.vector.tensor_scalar(mean[:, :, 0:HG_HEADS], mean[:, :, 0:HG_HEADS], 1.0 / HG_DV, EPS,
                                    ALU.mult, ALU.add).then_inc(means, 1)
            nc.vector.tensor_scalar(mean[:, :, HG_HEADS:HEADS], mean[:, :, HG_HEADS:HEADS], 1.0 / RET_DV, EPS,
                                    ALU.mult, ALU.add).then_inc(means, 1)
            dve.wait_ge(rooted, 1)
            nc.vector.reciprocal(rstd[:], root[:]).then_inc(rstd_ok, 1)
            dve.wait_ge(rstd_ok, 1)
            dve.wait_ge(consts, 32)

            def scale(i, u):
                t = 2 * i + u
                if not (first(i) and u == 0):
                    dve.wait_ge(turned_ok, t)
                head = bass.ds(t, 1) if is_hg(i) else bass.ds(i - HG_PAIRS + HG_HEADS, 1)
                nc.vector.tensor_tensor(scaled[:], values[:, :, bass.ds(t * P, P)],
                                        rstd[:, :, head].to_broadcast([P, TT, P]), ALU.mult).then_inc(scaled_ok, 1)

            scale(0, 0)

            def pair(i):
                for u in range(2):
                    t = 2 * i + u
                    if not at(i, NJ // 2 - 1):
                        ring.split_lo(dve, i + 1, u)
                    if not is_last(i, u):
                        scale(i + u, 1 - u)
                    dve.wait_ge(silu_ok, t + 1)
                    dve.wait_ge(turned_ok, t + 1)
                    if not (first(i) and u == 0):
                        dve.wait_ge(lo_ok, t)
                        dve.wait_ge(hi_ok, t)
                    nc.vector.scalar_tensor_tensor(
                        out=y[:], in0=turned[:, u].rearrange("p a b -> p (a b)"),
                        scalar=hg_gain[:, 0:1] if is_hg(i) else ret_gain[:, u:u + 1],
                        in1=silu[:], op0=ALU.mult, op1=ALU.mult).then_inc(y_ok, 1)
                    dve.wait_ge(hi_ok, t + 1)
                    nc.vector.tensor_tensor(y_lo[:, bass.ds(t, 1), :].rearrange("p o (a b) -> p (o a) b", b=P),
                                            y[:].rearrange("p (a b) -> p a b", b=P),
                                            y_hi[:, :, bass.ds(t * P, P)].bitcast(F32), ALU.subtract).then_inc(lo_ok, 1)
            over_pairs(dve, pair)

        @block.tensor
        def _(pe):
            project_block(nc, pe, ring, kept, 0, 0, gates[:, 0], projected)

            def pair(i):
                for u in range(2):
                    t = 2 * i + u
                    if not is_last(i, u):
                        if not (first(i) and u == 0):
                            pe.wait_ge(silu_ok, t)
                        project_block(nc, pe, ring, kept, i + u, 1 - u, gates[:, 1 - u], projected)
                    if not first(i):
                        pe.wait_ge(y_ok, t - 1)
                    pe.wait_ge(scaled_ok, t + 1)
                    for j in range(TT):
                        mm = nc.tensor.transpose(turned[:, u, j, :], scaled[:, j, :], ident[:])
                    mm.then_inc(turned_ok, 1)
            over_pairs(pe, pair)


def merge_branches(nc, dram, kept):
    KA, KB = HG_W // P, RET_V // P
    with Memory(nc, "merge") as m:
        y_hi, y_lo = kept["y_hi"], kept["y_lo"]
        sig = m.sb("sig", [P, 2, S])
        merged = m.sb("merged", [P, S])
        sums = [m.ps(n, [P, 2, HALF]) for n in ("ga", "gb", "a", "b")]
        multiplied = m.sem("multiplied")
        sig_ok, gated, merged_ok, stored = m.sem("sig_ok"), m.sem("gated"), m.sem("merged_ok"), m.sem("stored")
        ring = Ring(nc, m, KT, P, multiplied, slots=kept["weight_slots"], asked=kept["asked"]["merge"])
        w_in = dram["w_in"].rearrange("(k p) c -> p k c", p=P)
        w_a = dram["w_a"].rearrange("(k p) c -> p k c", p=P)
        w_b = dram["w_b"].rearrange("(k p) c -> p k c", p=P)
        kts = [KT, KT, KA, KB]
        block = m.block()

        def slot(c, n):
            return 2 * c + n // 2, n % 2

        @block.sync
        def _(sp):
            def load(c, n):
                i, u = slot(c, n)
                src = [w_in[:, :, bass.ds(GA + c * P, P)], w_in[:, :, bass.ds(GB + c * P, P)],
                       w_a[:, :, bass.ds(c * P, P)], w_b[:, :, bass.ds(c * P, P)]][n]
                ring.load(sp, i, u, src, kts[n])

            load(0, 0)
            load(0, 1)

            def tile(c):
                load(c, 2)
                load(c, 3)
                if not at(c, KT - 1):
                    load(c + 1, 0)
                    load(c + 1, 1)
                sp.wait_ge(merged_ok, c + 1)
                sp.dma_start(dram["merged"][bass.ds(c * P, P), :], merged[:]).then_inc(stored, 16)
            over(sp, KT, tile)
            sp.wait_ge(stored, 16 * KT)

        @block.scalar
        def _(act):
            ring.split_hi(act, 0, 0)

            def tile(c):
                ring.split_hi(act, *slot(c, 1))
                for n in range(2):
                    act.wait_ge(multiplied, 4 * c + n + 1)
                    if not first(c):
                        act.wait_ge(merged_ok, c)
                    nc.scalar.activation(sig[:, n], sums[n][:].rearrange("p a b -> p (a b)"),
                                         ACT.Sigmoid).then_inc(sig_ok, 1)
                    ring.split_hi(act, *slot(c, 2 + n), kt=kts[2 + n])
                if not at(c, KT - 1):
                    ring.split_hi(act, *slot(c + 1, 0))
            over(act, KT, tile)

        @block.vector
        def _(dve):
            ring.split_lo(dve, 0, 0)

            def tile(c):
                for n in range(1, 4):
                    ring.split_lo(dve, *slot(c, n), kt=kts[n])
                for n in range(2):
                    dve.wait_ge(multiplied, 4 * c + 3 + n)
                    dve.wait_ge(sig_ok, 2 * c + n + 1)
                    nc.vector.tensor_tensor(sig[:, n], sums[2 + n][:].rearrange("p a b -> p (a b)"), sig[:, n],
                                            ALU.mult).then_inc(gated, 1)
                    if n == 0 and not at(c, KT - 1):
                        ring.split_lo(dve, *slot(c + 1, 0))
                dve.wait_ge(gated, 2 * c + 2)
                if not first(c):
                    dve.wait_ge(stored, 16 * c)
                nc.vector.tensor_tensor(merged[:], sig[:, 0], sig[:, 1], ALU.add).then_inc(merged_ok, 1)
            over(dve, KT, tile)

        @block.tensor
        def _(pe):
            def tile(c):
                for n in range(2):
                    i, u = slot(c, n)
                    if not first(c):
                        pe.wait_ge(sig_ok, 2 * c - 1 + n)
                    project_block(nc, pe, ring, kept, i, u, sums[n], multiplied)
                for n, (j0, kt) in enumerate(((0, KA), (KA, KB))):
                    i, u = slot(c, 2 + n)
                    if not first(c):
                        pe.wait_ge(gated, 2 * c - 1 + n)
                    pe.wait_ge(ring.lo_ok, 2 * i + u + 1)
                    for half in range(2):
                        out = sums[2 + n][:, half, :].rearrange("p (a b) -> p a b", b=P)
                        mm = three_passes(nc, out, [
                            (ring.hi[:, u, k, :], ring.lo[:, u, k, :],
                             y_hi[:, 4 * half:4 * half + 4, (j0 + k) * P:(j0 + k + 1) * P],
                             y_lo[:, j0 + k, half * HALF:(half + 1) * HALF].rearrange("p (a b) -> p a b", b=P))
                            for k in range(kt)])
                    mm.then_inc(multiplied, 1)
            over(pe, KT, tile)


def project_out(nc, dram, kept):
    with Memory(nc, "out") as m:
        x2 = kept["x2"]
        m_hi, m_lo = m.sb("m_hi", [P, KT, S], F32R), m.sb("m_lo", [P, KT, S], F32R)
        x_ok = m.sem("x_ok")
        slots = Ring.slots(m, KT, 256, "w")
        asked = [m.sem(f"asked{u}") for u in range(2)]
        with Memory(nc, "outsplit") as n:
            raw = n.sb("raw", [P, KT, S])
            loaded = [n.sem(f"loaded{k}") for k in range(KT)]
            hi_ok, lo_ok = n.sem("hi_ok"), n.sem("lo_ok")
            block = n.block()

            @block.sync
            def _(sp):
                for k in range(KT):
                    sp.dma_start(raw[:, k], dram["merged"][k * P:(k + 1) * P, :]).then_inc(loaded[k], 16)
                for u in range(2):
                    src = dram["w_out"].rearrange("(k p) c -> p k c", p=P)[:, :, u * 256:(u + 1) * 256]
                    sp.dma_start(slots[0][:, u], src).then_inc(asked[u], 16)

            @block.scalar
            def _(act):
                for k in range(KT):
                    act.wait_ge(loaded[k], 16)
                    nc.scalar.copy(m_hi[:, k], raw[:, k]).then_inc(hi_ok, 1)

            @block.vector
            def _(dve):
                for k in range(KT):
                    dve.wait_ge(hi_ok, k + 1)
                    nc.vector.tensor_tensor(m_lo[:, k], raw[:, k], m_hi[:, k].bitcast(F32),
                                            ALU.subtract).then_inc(lo_ok, 1)
                dve.wait_ge(lo_ok, KT)

        def load_x(sp):
            sp.dma_start(x2[:], dram["x"].rearrange("(t p) d -> p t d", p=P)).then_inc(x_ok, 16)

        def store(eng, b, col, psum):
            dst = x2[:, 2 * b:2 * b + 2, bass.ds(col, 256)]
            return nc.vector.tensor_tensor(dst, psum, dst, ALU.add)

        tokens_out(nc, m, m_hi, m_lo, dram["w_out"], [(D // 512, 0)], store, [], (load_x, x_ok, 16), slots, asked)


def route(nc, dram, kept):
    R = GROUPS + EXPERTS
    with Memory(nc, "route") as m:
        x2, ident, logits = kept["x2"], kept["ident"], kept["logits"]
        sq = m.sb("sq", [P, D])
        xn = m.sb("xn", [P, 2, D])
        stat = m.sb("stat", [P, 4, TT])
        whole = m.sb("whole", [P, 2, KT, P])
        w = m.sb("w", [P, KT, R])
        bias = m.sb("bias", [P, R])
        turned = m.ps("turned", [P, 2, KT, P])
        sums = m.ps("sums", [P, 2, HALF])
        consts, rows_out = m.sem("consts"), [m.sem(f"rows_out{u}") for u in range(2)]
        summed, mean, rooted, rstd = m.sem("summed"), m.sem("mean"), m.sem("rooted"), m.sem("rstd")
        scaled, turned_ok, gained = m.sem("scaled"), m.sem("turned_ok"), m.sem("gained")
        routed, logits_ok = m.sem("routed"), m.sem("logits_ok")
        gain = kept["ffn_gain"]
        block = m.block()

        @block.sync
        def _(sp):
            with nc.allow_non_contiguous_dma("router weights have 4 and 32 columns"):
                sp.dma_start(gain[:], dram["ffn_norm"]).then_inc(consts, 16)
                sp.dma_start(w[:, :, 0:GROUPS], dram["w_rg"].rearrange("(k p) c -> p k c", p=P)).then_inc(consts, 16)
                sp.dma_start(w[:, :, GROUPS:R], dram["w_re"].rearrange("(k p) c -> p k c", p=P)).then_inc(consts, 16)
                sp.dma_start(bias[:, 0:GROUPS], dram["b_rg"].to_broadcast([P, GROUPS])).then_inc(consts, 16)
                sp.dma_start(bias[:, GROUPS:R], dram["b_re"].to_broadcast([P, EXPERTS])).then_inc(consts, 16)

            def pair(i):
                for u in range(2):
                    t = 2 * i + u
                    sp.wait_ge(scaled, t + 1)
                    sp.dma_start(dram["rows"][bass.ds(t * P, P), :], xn[:, u, :]).then_inc(rows_out[u], 16)
            over(sp, TT // 2, pair)
            for name in TABLES:
                sp.dma_start(kept[name][:], dram[name]).then_inc(kept["tables_in"], 16)
            for u in range(2):
                sp.wait_ge(rows_out[u], 16 * TT // 2)

        @block.scalar
        def _(act):
            for t in range(TT):
                if t:
                    act.wait_ge(summed, t)
                nc.scalar.activation(sq[:], x2[:, t, :], ACT.Square, accum_out=stat[:, 0, t:t + 1]).then_inc(summed, 1)
            act.wait_ge(mean, 1)
            nc.scalar.activation(stat[:, 2, :], stat[:, 1, :], ACT.Sqrt).then_inc(rooted, 1)
            act.wait_ge(rstd, 1)
            for t in range(TT):
                u = t % 2
                if t >= 2:
                    act.wait_ge(turned_ok, t - 1)
                    act.wait_ge(rows_out[u], 16 * (t // 2))
                nc.scalar.activation(xn[:, u, :], x2[:, t, :], ACT.Copy, scale=stat[:, 3, t:t + 1]).then_inc(scaled, 1)

        @block.vector
        def _(dve):
            dve.wait_ge(summed, TT)
            nc.vector.tensor_scalar(stat[:, 1, :], stat[:, 0, :], 1.0 / D, EPS, ALU.mult, ALU.add).then_inc(mean, 1)
            dve.wait_ge(rooted, 1)
            nc.vector.reciprocal(stat[:, 3, :], stat[:, 2, :]).then_inc(rstd, 1)
            dve.wait_ge(consts, 80)

            def scale(t, u, old):
                dve.wait_ge(turned_ok, t + 1)
                if old:
                    dve.wait_ge(routed, t - 1)
                nc.vector.tensor_tensor(whole[:, u], turned[:, u], bc(gain[:], 2, P), ALU.mult).then_inc(gained, 1)

            def pair(i):
                for u in range(2):
                    t = 2 * i + u
                    if not (at(i, TT // 2 - 1) and u == 1):
                        scale(t + 1, 1 - u, not (first(i) and u == 0))
                    dve.wait_ge(routed, t + 1)
                    nc.vector.tensor_tensor(logits[:, bass.ds(t, 1), :].rearrange("p o r -> p (o r)"), sums[:, u, 0:R],
                                            bias[:], ALU.add).then_inc(logits_ok, 1)
            scale(0, 0, False)
            over(dve, TT // 2, pair)

        @block.tensor
        def _(pe):
            pe.wait_ge(consts, 80)

            def turn(t, u, old):
                pe.wait_ge(scaled, t + 1)
                if old:
                    pe.wait_ge(gained, t - 1)
                for k in range(KT):
                    mm = nc.tensor.transpose(turned[:, u, k, :], xn[:, u, k * P:(k + 1) * P], ident[:])
                mm.then_inc(turned_ok, 1)

            def pair(i):
                for u in range(2):
                    t = 2 * i + u
                    if not (at(i, TT // 2 - 1) and u == 1):
                        turn(t + 1, 1 - u, not (first(i) and u == 0))
                    pe.wait_ge(gained, t + 1)
                    if not first(i):
                        pe.wait_ge(logits_ok, t - 1)
                    for k in range(KT):
                        mm = nc.tensor.matmul(sums[:, u, 0:R], whole[:, u, k, :], w[:, k, :],
                                              start=(k == 0), stop=(k == KT - 1))
                    mm.then_inc(routed, 1)
            turn(0, 0, False)
            over(pe, TT // 2, pair)


def place(nc, dram, kept):
    T, G, E, N = TT, GROUPS, EXPERTS, PER_GROUP
    with Memory(nc, "place") as m:
        L = kept["logits"]
        names = ("gmax", "gsum", "gw", "gbest", "m1", "m2", "best", "p2", "den", "inv")
        small = {n: m.sb(n, [P, T]) for n in names}
        g4, g4b, gone = m.sb("g4", [P, T, G]), m.sb("g4b", [P, T, G]), m.sb("gone", [P, T, G])
        all32 = m.sb("all32", [P, T, G, N])
        e8, e8b, s8 = m.sb("e8", [P, T, N]), m.sb("e8b", [P, T, N]), m.sb("s8", [P, T, N])
        one8 = m.sb("one8", [P, 2, T, N])
        chosen = m.sb("chosen", [P, 2, T, E])
        either = m.sb("either", [P, T, E])
        prod = m.sb("prod", [P, 2, T, E])
        rank, base, ide = m.sb("rank", [P, 2, T]), m.sb("base", [P, 2, T]), m.sb("ide", [P, 2, T])
        rank_i, tile_i, row_i = (m.sb(n, [P, 2, T], I32) for n in ("rank_i", "tile_i", "row_i"))
        tile_f, row_f, is_over, col = (m.sb(n, [P, 2, T]) for n in ("tile_f", "row_f", "is_over", "col"))
        cnt_i, cnt_j, more = m.sb("cnt_i", [P, E], I32), m.sb("cnt_j", [P, E], I32), m.sb("more", [P, E])
        incl, excl = m.sb("incl", [P, E]), m.sb("excl", [P, E])
        below = m.sb("below", [P, OVER, E])
        owner = m.sb("owner", [P, OVER + 1])
        rows1 = m.sb("rows1", [P, 2 * T, P])
        cols1 = m.sb("cols1", [P, 2 * T, COLS])
        colv = m.sb("colv", [P, 2 * T, 2, COLS])
        full = m.sb("full", [P, 2, COLS])
        empty = m.sb("empty", [P, 2, COLS])
        desc, iota, earlier, ones, ids = (kept[n] for n in ("desc", "iota", "earlier", "ones", "pair_ids"))
        before = m.sb("before", [P, T + 1, E])
        ranks = m.sb("ranks", [P, T, E])
        ps_rank = m.ps("ps_rank", [P, T, E])
        ps_count = m.ps("ps_count", [P, HALF])
        ps_slots = m.ps("ps_slots", [P, HALF])
        consts, v, a, pe_ok = kept["tables_in"], m.sem("dve"), m.sem("act"), m.sem("pe")
        block = m.block()

        @block.sync
        def _(sp):
            for b in range(AHEAD):
                load_gate_up(sp, dram, kept["w_gu"], b, b, kept["gu_in"][b])
                load_down(sp, dram, kept["w_d"], b, b, kept["d_in"][b])

        marks = {}

        @block.vector
        def _(dve):
            V = nc.vector
            steps = Steps(dve, v)
            link = steps.link
            dve.wait_ge(consts, 80)
            Lg = L[:, :, 0:G]
            Le = L[:, :, G:G + E].rearrange("p t (g n) -> p t g n", g=G)
            one = [one8[:, k] for k in range(2)]

            def first_best(src, best, n, tmp, out):
                link(V.tensor_tensor(tmp, src, bc(best[:], 2, n), ALU.is_equal))
                link(V.tensor_tensor(tmp, tmp, bc(desc[:, N - n:N], 1, T), ALU.mult))
                link(V.reduce_max(small["best"][:], tmp, AX.X))
                link(V.tensor_tensor(out, tmp, bc(small["best"][:], 2, n), ALU.is_equal))

            link(V.reduce_max(small["gmax"][:], Lg, AX.X))
            link(V.tensor_tensor(g4[:], Lg, bc(small["gmax"][:], 2, G), ALU.subtract))
            marks["group"] = steps.n
            first_best(Lg, small["gmax"], G, g4b[:], gone[:])
            dve.wait_ge(a, 1)
            link(V.reduce_sum(small["gsum"][:], g4[:], AX.X))
            link(V.reciprocal(small["gw"][:], small["gsum"][:]))
            link(V.tensor_tensor(all32[:], Le, bc(gone[:], 3, N), ALU.mult))
            link(V.reduce_sum(e8[:], all32[:].rearrange("p t g n -> p t n g"), AX.X))
            link(V.reduce_max(small["m1"][:], e8[:], AX.X))
            first_best(e8[:], small["m1"], N, s8[:], one[0])
            link(V.scalar_tensor_tensor(out=e8b[:], in0=one[0], scalar=-3.0e38, in1=e8[:],
                                        op0=ALU.mult, op1=ALU.add))
            link(V.reduce_max(small["m2"][:], e8b[:], AX.X))
            first_best(e8b[:], small["m2"], N, s8[:], one[1])
            link(V.tensor_tensor(small["den"][:], small["m2"][:], small["m1"][:], ALU.subtract))
            marks["expert"] = steps.n
            for k in range(2):
                link(V.tensor_tensor(chosen[:, k].rearrange("p t (g n) -> p t g n", g=G),
                                     bc(gone[:], 3, N), bc(one[k], 2, G), ALU.mult))
            link(V.tensor_tensor(either[:], chosen[:, 0], chosen[:, 1], ALU.add))
            marks["either"] = steps.n
            dve.wait_ge(a, 2)
            link(V.tensor_scalar(small["den"][:], small["p2"][:], 1.0, None, ALU.add))
            link(V.reciprocal(small["inv"][:], small["den"][:]))
            link(V.tensor_tensor(kept["weight"][:, 0, :], small["inv"][:], small["gw"][:], ALU.mult))
            link(V.tensor_tensor(kept["weight"][:, 1, :], kept["weight"][:, 0, :], small["p2"][:], ALU.mult))
            link(V.memset(before[:, 0, :], 0.0))
            dve.wait_ge(pe_ok, 1)
            for t in range(T):
                link(V.tensor_tensor(before[:, t + 1, :], before[:, t, :], ps_count[:, t * E:(t + 1) * E], ALU.add))
            link(V.tensor_copy(cnt_i[:], before[:, T, :]))
            link(V.tensor_scalar(cnt_j[:], cnt_i[:], P - 1, None, ALU.add))
            link(V.tensor_scalar(cnt_i[:], cnt_j[:], 7, None, ALU.arith_shift_right))
            link(V.tensor_copy(more[:], cnt_i[:]))
            link(V.tensor_scalar(more[:], more[:], -1.0, 0.0, ALU.add, ALU.max))
            link(V.tensor_tensor_scan(incl[:], ones[:, 0:E], more[:], 0.0, ALU.mult, ALU.add))
            link(V.tensor_tensor(excl[:], incl[:], more[:], ALU.subtract))
            link(V.tensor_tensor(below[:], bc(incl[:], 1, OVER), bc(iota[:, 0:OVER], 2, E), ALU.is_le))
            link(V.reduce_sum(owner[:, 0:OVER], below[:], AX.X))
            link(V.tensor_scalar(owner[:, 0:OVER], owner[:, 0:OVER], float(E - 1), None, ALU.min))
            link(V.tensor_copy(owner[:, OVER:OVER + 1], incl[:, E - 1:E]))
            link(V.tensor_copy(kept["owner"][:], owner[:]))
            dve.wait_ge(pe_ok, 2)
            link(V.tensor_tensor(ranks[:], ps_rank[:], before[:, 0:T, :], ALU.add))
            for out, table in ((rank, ranks[:]), (ide, bc(iota[:, 0:E], 1, T)), (base, bc(excl[:], 1, T))):
                for k in range(2):
                    link(V.tensor_tensor(prod[:, k], chosen[:, k], table, ALU.mult))
                link(V.reduce_sum(out[:], prod[:], AX.X))
            link(V.tensor_copy(rank_i[:], rank[:]))
            link(V.tensor_scalar(tile_i[:], rank_i[:], 7, None, ALU.arith_shift_right))
            link(V.tensor_scalar(row_i[:], rank_i[:], P - 1, None, ALU.bitwise_and))
            link(V.tensor_copy(tile_f[:], tile_i[:]))
            link(V.tensor_copy(row_f[:], row_i[:]))
            link(V.tensor_scalar(is_over[:], tile_f[:], 1.0, None, ALU.min))
            link(V.tensor_tensor(col[:], base[:], tile_f[:], ALU.add))
            link(V.scalar_tensor_tensor(out=col[:], in0=col[:], scalar=float(E - 1), in1=ide[:],
                                        op0=ALU.add, op1=ALU.subtract))
            link(V.tensor_tensor(col[:], col[:], is_over[:], ALU.mult))
            link(V.tensor_tensor(col[:], col[:], ide[:], ALU.add))
            flat = lambda x: x[:].rearrange("p k t -> p (k t)")
            link(V.tensor_tensor(rows1[:], bc(flat(row_f), 2, P), bc(iota[:], 1, 2 * T), ALU.is_equal))
            link(V.tensor_tensor(cols1[:], bc(flat(col), 2, COLS), bc(iota[:, 0:COLS], 1, 2 * T), ALU.is_equal))
            for w in range(2):
                link(V.tensor_tensor(colv[:, :, w, :], cols1[:], bc(ids[:, :, w], 2, COLS), ALU.mult))
            marks["slots"] = steps.n
            dve.wait_ge(pe_ok, 3)
            link(V.tensor_copy(full[:], ps_slots[:, 0:2 * COLS].rearrange("p (w c) -> p w c", w=2)))
            link(V.tensor_scalar(empty[:], full[:], 0.0, float(FAR), ALU.is_equal, ALU.mult))
            link(V.scalar_tensor_tensor(out=full[:], in0=full[:], scalar=-1.0, in1=empty[:],
                                        op0=ALU.add, op1=ALU.add))
            link(V.tensor_copy(kept["slots"][:], full[:].rearrange("p w c -> p c w")))

        @block.scalar
        def _(act):
            act.wait_ge(v, marks["group"])
            nc.scalar.activation(g4[:], g4[:], ACT.Exp).then_inc(a, 1)
            act.wait_ge(v, marks["expert"])
            nc.scalar.activation(small["p2"][:], small["den"][:], ACT.Exp).then_inc(a, 1)

        @block.tensor
        def _(pe):
            pe.wait_ge(consts, 80)
            pe.wait_ge(v, marks["either"])
            every = either[:].rearrange("p t e -> p (t e)")
            nc.tensor.matmul(ps_count[:, 0:T * E], ones[:], every, start=True, stop=True).then_inc(pe_ok, 1)
            nc.tensor.matmul(ps_rank[:].rearrange("p t e -> p (t e)"), earlier[:], every,
                             start=True, stop=True).then_inc(pe_ok, 1)
            pe.wait_ge(v, marks["slots"])
            for j in range(2 * T):
                mm = nc.tensor.matmul(ps_slots[:, 0:2 * COLS], rows1[:, j, :],
                                      colv[:, j].rearrange("p w c -> p (w c)"),
                                      start=(j == 0), stop=(j == 2 * T - 1))
            mm.then_inc(pe_ok, 1)


def expert_weights(dram, e):
    def of(name, k):
        return dram[name].rearrange("(e k p) c -> e p k c", p=P, k=k)[bass.ds(e, 1)].rearrange("o p k c -> p (o k) c")
    return of("w_eg", KT), of("w_eu", KT), of("w_ed", DE // P)


def load_gate_up(eng, dram, w_gu, b, e, sem):
    g_src, u_src, _ = expert_weights(dram, e)
    eng.dma_start(w_gu[:, b, :, 0, :], g_src).then_inc(sem, 16)
    eng.dma_start(w_gu[:, b, :, 1, :], u_src).then_inc(sem, 16)


def load_down(eng, dram, w_d, b, e, sem):
    eng.dma_start(w_d[:, b], expert_weights(dram, e)[2]).then_inc(sem, 16)


def run_experts(nc, dram, kept):
    KD = DE // P
    with Memory(nc, "moe") as m:
        ident, gain, slots, owner = kept["ident"], kept["ffn_gain"], kept["slots"], kept["owner"]
        w_gu, w_d, gu_in, d_in = (kept[n] for n in ("w_gu", "w_d", "gu_in", "d_in"))
        x = m.sb("x", [P, AHEAD, D])
        xT = m.sb("xT", [P, 2, KT, P])
        silu = m.sb("silu", [P, 2, DE])
        hT = m.sb("hT", [P, 2, KD, P])
        y = m.sb("y", [P, AHEAD, D])
        ps_x = m.ps("ps_x", [P, KT, P])
        ps_gu = m.ps("ps_gu", [P, 2, DE])
        ps_h = m.ps("ps_h", [P, 4, P])
        ps_y = m.ps("ps_y", [P, 2, HALF])
        zeroed = m.sem("zeroed")
        gathered = [m.sem(f"gathered{b}") for b in range(AHEAD)]
        scattered = [m.sem(f"scattered{b}") for b in range(AHEAD)]
        x_turned, xT_ok = m.sem("x_turned"), m.sem("xT_ok")
        gu_ok, silu_ok, h_ok = m.sem("gu_ok"), m.sem("silu_ok"), m.sem("h_ok")
        h_turned, hT_ok = m.sem("h_turned"), m.sem("hT_ok")
        down_ok, y_act, y_dve = m.sem("down_ok"), m.sem("y_act"), m.sem("y_dve")
        o = {n: m.sem("over_" + n) for n in ("w_in", "gathered", "x_turned", "xT", "gu", "silu", "h",
                                             "h_turned", "hT", "y", "scattered")}
        block = m.block()
        ROUNDS = EXPERTS // AHEAD

        def gather(pool, b, column, sem):
            pool.indirect_dma_start(x[:, b, :], None, dram["rows"],
                                    bass.IndirectOffsetOnAxis(ap=slots[:, column, 0:1], axis=0),
                                    bounds_check=S - 1, oob_is_err=False).then_inc(sem, 16)

        def scatter(pool, b, column, sem):
            pool.indirect_dma_start(dram["results"], bass.IndirectOffsetOnAxis(ap=slots[:, column, 1:2], axis=0),
                                    y[:, b, :], None, bounds_check=PAIRS - 1, oob_is_err=False).then_inc(sem, 16)

        def turn_x(b):
            for k in range(KT):
                mm = nc.tensor.transpose(ps_x[:, k, :], x[:, b, k * P:(k + 1) * P], ident[:])
            return mm

        def gate_up(b):
            u = b % 2
            out = ps_gu[:].rearrange("p a b -> p (a b)")
            for k in range(KT):
                mm = nc.tensor.matmul(out, xT[:, u, k, :], w_gu[:, b, k].rearrange("p a b -> p (a b)"),
                                      start=(k == 0), stop=(k == KT - 1))
            return mm

        def turn_h(u):
            for k in range(KD):
                mm = nc.tensor.transpose(ps_h[:, k, :], silu[:, u, k * P:(k + 1) * P], ident[:])
            return mm

        def down(b):
            u = b % 2
            for half in range(2):
                for k in range(KD):
                    mm = nc.tensor.matmul(ps_y[:, half, :], hT[:, u, k, :],
                                          w_d[:, b, k, half * HALF:(half + 1) * HALF],
                                          start=(k == 0), stop=(k == KD - 1))
            return mm

        def further(eng, body):
            n = eng.value_load(owner[0:1, OVER:OVER + 1], min_val=0, max_val=OVER)
            with eng.If(n > 0):
                with eng.Fori(0, OVER) as j:
                    with eng.If(n > j):
                        body(j)

        def scatters_before(i, b):
            if first(i) or (at(i, 1) and b == 0):
                return None
            return 16 * i if b else 16 * i - 16

        @block.sync
        def _(sp):
            with sp.Fori(1, ROUNDS) as i:
                for b in range(AHEAD):
                    sp.wait_ge(gu_ok, AHEAD * i + (b + 1 - AHEAD))
                    load_gate_up(sp, dram, w_gu, b, AHEAD * i + b, gu_in[b])
                    sp.wait_ge(down_ok, AHEAD * i + (b + 1 - AHEAD))
                    load_down(sp, dram, w_d, b, AHEAD * i + b, d_in[b])

            for k in range(KT):
                sp.dma_start(kept["ple_raw"][:, k], dram["w_pg"][k * P:(k + 1) * P, :]).then_inc(kept["ple_in"][k], 16)
            sp.wait_ge(gu_ok, EXPERTS)
            sp.wait_ge(down_ok, EXPERTS)

            def more(j):
                sp.wait_ge(down_ok, EXPERTS + j)
                e = sp.value_load(owner[0:1, bass.ds(j, 1)], min_val=0, max_val=EXPERTS - 1)
                load_gate_up(sp, dram, w_gu, 0, e, o["w_in"])
                load_down(sp, dram, w_d, 0, e, o["w_in"])
            further(sp, more)

        @block.gpsimd
        def _(pool):
            def zero(b):
                nc.gpsimd.memset(x[:, b, :], 0.0).then_inc(zeroed, 1)
                pool.wait_ge(zeroed, b + 1)

            for e in range(AHEAD - 1):
                zero(e)
                gather(pool, e, e, gathered[e])
            zero(AHEAD - 1)
            for e in range(EXPERTS):
                nxt = e + AHEAD - 1
                if nxt < EXPERTS:
                    if e > 0:
                        pool.wait_ge(x_turned, e)
                    gather(pool, nxt % AHEAD, nxt, gathered[nxt % AHEAD])
                pool.wait_ge(y_act, e + 1)
                pool.wait_ge(y_dve, e + 1)
                scatter(pool, e % AHEAD, e, scattered[e % AHEAD])
            for b in range(AHEAD):
                pool.wait_ge(scattered[b], 16 * ROUNDS)

            n = pool.value_load(owner[0:1, OVER:OVER + 1], min_val=0, max_val=OVER)
            with pool.If(n > 0):
                for j in range(OVER):
                    with pool.If(n > j):
                        gather(pool, 0, EXPERTS + j, o["gathered"])
                        pool.wait_ge(o["y"], 2 * j + 2)
                        scatter(pool, 0, EXPERTS + j, o["scattered"])
                        pool.wait_ge(o["scattered"], 16 * j + 16)

        @block.scalar
        def _(act):
            def store(t, b, old):
                act.wait_ge(down_ok, t + 1)
                if old is not None:
                    act.wait_ge(scattered[b], old)
                nc.scalar.copy(y[:, b, 0:HALF], ps_y[:, 0, :]).then_inc(y_act, 1)

            def step(i):
                for b in range(AHEAD):
                    e, u = AHEAD * i + b, b % 2
                    act.wait_ge(gu_ok, e + 1)
                    if not (first(i) and b < 2):
                        act.wait_ge(h_turned, e - 1)
                    nc.scalar.activation(silu[:, u, :], ps_gu[:, 0, :], ACT.Silu).then_inc(silu_ok, 1)
                    if not (first(i) and b == 0):
                        store(e - 1, (b - 1) % AHEAD, scatters_before(i, b))
                    act.wait_ge(h_turned, e + 1)
                    nc.scalar.copy(hT[:, u], ps_h[:, 0:KD, :]).then_inc(hT_ok, 1)
            over(act, ROUNDS, step)
            store(EXPERTS - 1, AHEAD - 1, 16 * (ROUNDS - 1))

            def more(j):
                act.wait_ge(o["gu"], j + 1)
                nc.scalar.activation(silu[:, 0, :], ps_gu[:, 0, :], ACT.Silu).then_inc(o["silu"], 1)
                act.wait_ge(o["h_turned"], j + 1)
                nc.scalar.copy(hT[:, 0], ps_h[:, 0:KD, :]).then_inc(o["hT"], 1)
                act.wait_ge(down_ok, EXPERTS + j + 1)
                for half in range(2):
                    nc.scalar.copy(y[:, 0, half * HALF:(half + 1) * HALF], ps_y[:, half, :]).then_inc(o["y"], 1)
            further(act, more)

        @block.vector
        def _(dve):
            def gained(e, u, old):
                dve.wait_ge(x_turned, e + 1)
                if old:
                    dve.wait_ge(gu_ok, e - 1)
                nc.vector.tensor_tensor(xT[:, u], ps_x[:], bc(gain[:], 2, P), ALU.mult).then_inc(xT_ok, 1)

            def store(t, b, old):
                dve.wait_ge(down_ok, t + 1)
                if old is not None:
                    dve.wait_ge(scattered[b], old)
                nc.vector.tensor_copy(y[:, b, HALF:D], ps_y[:, 1, :]).then_inc(y_dve, 1)

            gained(0, 0, False)

            def step(i):
                for b in range(AHEAD):
                    e, u = AHEAD * i + b, b % 2
                    dve.wait_ge(silu_ok, e + 1)
                    nc.vector.tensor_tensor(silu[:, u, :], silu[:, u, :], ps_gu[:, 1, :], ALU.mult).then_inc(h_ok, 1)
                    if not (at(i, ROUNDS - 1) and b == AHEAD - 1):
                        gained(e + 1, 1 - u, not (first(i) and b == 0))
                    if not (first(i) and b == 0):
                        store(e - 1, (b - 1) % AHEAD, scatters_before(i, b))
            over(dve, ROUNDS, step)
            store(EXPERTS - 1, AHEAD - 1, 16 * (ROUNDS - 1))

            def more(j):
                dve.wait_ge(o["x_turned"], j + 1)
                nc.vector.tensor_tensor(xT[:, 0], ps_x[:], bc(gain[:], 2, P), ALU.mult).then_inc(o["xT"], 1)
                dve.wait_ge(o["silu"], j + 1)
                nc.vector.tensor_tensor(silu[:, 0, :], silu[:, 0, :], ps_gu[:, 1, :], ALU.mult).then_inc(o["h"], 1)
            further(dve, more)

        @block.tensor
        def _(pe):
            def turn(i, b, e, old):
                pe.wait_ge(gathered[b], 16 * i + 16)
                if old:
                    pe.wait_ge(xT_ok, e)
                turn_x(b).then_inc(x_turned, 1)

            def last_down(e, b, i, old):
                pe.wait_ge(hT_ok, e + 1)
                pe.wait_ge(d_in[b], 16 * i + 16)
                if old:
                    pe.wait_ge(y_act, e)
                    pe.wait_ge(y_dve, e)
                down(b).then_inc(down_ok, 1)

            turn(0, 0, 0, False)

            def step(i):
                for b in range(AHEAD):
                    e = AHEAD * i + b
                    pe.wait_ge(xT_ok, e + 1)
                    pe.wait_ge(gu_in[b], 32 * i + 32)
                    gate_up(b).then_inc(gu_ok, 1)
                    if not (at(i, ROUNDS - 1) and b == AHEAD - 1):
                        turn(i + (b + 1) // AHEAD, (b + 1) % AHEAD, e + 1, True)
                    if not (first(i) and b == 0):
                        last_down(e - 1, (b - 1) % AHEAD, i if b else i - 1, not (first(i) and b == 1))
                    pe.wait_ge(h_ok, e + 1)
                    if not (first(i) and b == 0):
                        pe.wait_ge(hT_ok, e)
                    turn_h(b % 2).then_inc(h_turned, 1)
            over(pe, ROUNDS, step)
            last_down(EXPERTS - 1, AHEAD - 1, ROUNDS - 1, True)

            pe.wait_ge(y_act, EXPERTS)
            pe.wait_ge(y_dve, EXPERTS)

            def more(j):
                pe.wait_ge(o["gathered"], 16 * j + 16)
                turn_x(0).then_inc(o["x_turned"], 1)
                pe.wait_ge(o["xT"], j + 1)
                pe.wait_ge(o["w_in"], 48 * j + 48)
                gate_up(0).then_inc(o["gu"], 1)
                pe.wait_ge(o["h"], j + 1)
                turn_h(0).then_inc(o["h_turned"], 1)
                pe.wait_ge(o["hT"], j + 1)
                down(0).then_inc(down_ok, 1)
            further(pe, more)


def finish(nc, dram, kept, out):
    KP = PLE // P
    with Memory(nc, "fin") as m:
        x2, weight, ident = kept["x2"], kept["weight"], kept["ident"]
        g_hi, g_lo = m.sb("g_hi", [P, KT, D], F32R), m.sb("g_lo", [P, KT, D], F32R)
        w_p = m.sb("w_p", [P, KP, D])
        raw, w_loaded = kept["ple_raw"], kept["ple_in"]
        r = m.sb("r", [P, 2, 2, D])
        pt = m.sb("pt", [P, 2, PLE])
        pT = m.sb("pT", [P, 2, KP, P])
        sq = m.sb("sq", [P, D])
        stat = m.sb("stat", [P, 2, 8])
        xn = m.sb("xn", [P, D])
        whole = m.sb("whole", [P, KT, P])
        t_hi, t_lo = m.sb("t_hi", [P, 2, KT, P], F32R), m.sb("t_lo", [P, 2, KT, P], F32R)
        gate = m.sb("gate", [P, D])
        res = m.sb("res", [P, D])
        ple_gain, out_gain = m.sb("ple_gain", [P, KT]), m.sb("out_gain", [P, D])
        turned = m.ps("turned", [P, KT, P])
        p_turned = m.ps("p_turned", [P, 4, P])
        s_gate, s_proj = m.ps("s_gate", [P, 2, HALF]), m.ps("s_proj", [P, 2, HALF])
        consts, w_p_in, out_gain_in = m.sem("consts"), m.sem("w_p_in"), m.sem("out_gain_in")
        w_hi_ok, w_lo_ok = m.sem("w_hi_ok"), m.sem("w_lo_ok")
        rows_in = [m.sem(f"rows_in{u}") for u in range(2)]
        p_in = [m.sem(f"p_in{u}") for u in range(2)]
        added = m.sem("added")
        summed, mean, rooted, rstd, scaled = (m.sem(n) for n in ("summed", "mean", "rooted", "rstd", "scaled"))
        turned_ok, gained, hi_ok, lo_ok = (m.sem(n) for n in ("turned_ok", "gained", "hi_ok", "lo_ok"))
        p_turned_ok, pT_ok = m.sem("p_turned_ok"), m.sem("pT_ok")
        gate_mm, proj_mm, sig_ok = m.sem("gate_mm"), m.sem("proj_mm"), m.sem("sig_ok")
        mixed = m.sem("mixed")
        summed2, mean2, rooted2, rstd2 = (m.sem(n) for n in ("summed2", "mean2", "rooted2", "rstd2"))
        res_ok, stored = m.sem("res_ok"), m.sem("stored")
        block = m.block()

        @block.sync
        def _(sp):
            sp.dma_start(ple_gain[:], dram["ple_norm"]).then_inc(consts, 16)
            for t in range(TT + 2):
                if t < TT:
                    u = t % 2
                    if t >= 2:
                        sp.wait_ge(added, 2 * t - 2)
                    for k in range(2):
                        sp.dma_start(r[:, u, k, :], dram["results"][k * S + t * P:k * S + (t + 1) * P, :]).then_inc(rows_in[u], 16)
                    if t >= 2:
                        sp.wait_ge(p_turned_ok, t - 1)
                    sp.dma_start(pt[:, u, :], dram["p"][t * P:(t + 1) * P, :]).then_inc(p_in[u], 16)
                if t == 0:
                    sp.dma_start(w_p[:], dram["w_pp"].rearrange("(k p) c -> p k c", p=P)).then_inc(w_p_in, 16)
                    sp.dma_start(out_gain[:], dram["final_norm"].to_broadcast([P, D])).then_inc(out_gain_in, 16)
                if t >= 2:
                    sp.wait_ge(res_ok, t - 1)
                    sp.dma_start(out[(t - 2) * P:(t - 1) * P, :], res[:]).then_inc(stored, 16)
            sp.wait_ge(stored, 16 * TT)

        @block.scalar
        def _(act):
            A = nc.scalar

            def split(k):
                act.wait_ge(w_loaded[k], 16)
                A.copy(g_hi[:, k, :], raw[:, k]).then_inc(w_hi_ok, 1)

            def front(t):
                act.wait_ge(added, 2 * t + 2)
                if t >= 1:
                    act.wait_ge(summed, t)
                    act.wait_ge(summed2, t - 1)
                    act.wait_ge(mean2, t - 1)
                u = t % 2
                A.activation(sq[:], x2[:, t, :], ACT.Square, accum_out=stat[:, u, 0:1]).then_inc(summed, 1)
                act.wait_ge(mean, t + 1)
                A.activation(stat[:, u, 2:3], stat[:, u, 1:2], ACT.Sqrt).then_inc(rooted, 1)
                act.wait_ge(rstd, t + 1)
                if t >= 1:
                    act.wait_ge(turned_ok, t)
                A.activation(xn[:], x2[:, t, :], ACT.Copy, scale=stat[:, u, 3:4]).then_inc(scaled, 1)

            def operands(t):
                u = t % 2
                act.wait_ge(gained, t + 1)
                if t >= 2:
                    act.wait_ge(gate_mm, t - 1)
                A.copy(t_hi[:, u], whole[:]).then_inc(hi_ok, 1)
                act.wait_ge(p_turned_ok, t + 1)
                if t >= 2:
                    act.wait_ge(proj_mm, t - 1)
                A.copy(pT[:, u], p_turned[:, 0:KP, :]).then_inc(pT_ok, 1)

            def gates(t):
                act.wait_ge(gate_mm, t + 1)
                if t >= 1:
                    act.wait_ge(mixed, 2 * t)
                A.activation(gate[:], s_gate[:].rearrange("p a b -> p (a b)"), ACT.Sigmoid).then_inc(sig_ok, 1)

            def back(t):
                u = t % 2
                act.wait_ge(mixed, 2 * t + 2)
                act.wait_ge(summed, min(t + 2, TT))
                A.activation(sq[:], x2[:, t, :], ACT.Square, accum_out=stat[:, u, 4:5]).then_inc(summed2, 1)
                act.wait_ge(mean2, t + 1)
                A.activation(stat[:, u, 6:7], stat[:, u, 5:6], ACT.Sqrt).then_inc(rooted2, 1)

            for k in range(KT // 2):
                split(k)
            front(0)
            operands(0)
            for k in range(KT // 2, KT):
                split(k)
            for t in range(TT):
                if t + 1 < TT:
                    front(t + 1)
                gates(t)
                if t + 1 < TT:
                    operands(t + 1)
                back(t)

        @block.vector
        def _(dve):
            V = nc.vector
            dve.wait_ge(consts, 16)

            def split(k):
                dve.wait_ge(w_hi_ok, k + 1)
                V.tensor_tensor(g_lo[:, k, :], raw[:, k], g_hi[:, k, :].bitcast(F32), ALU.subtract).then_inc(w_lo_ok, 1)

            def add_experts(t):
                u = t % 2
                dve.wait_ge(rows_in[u], 32 * (t // 2) + 32)
                for k in range(2):
                    if k:
                        dve.wait_ge(added, 2 * t + 1)
                    V.scalar_tensor_tensor(out=x2[:, t, :], in0=r[:, u, k, :], scalar=weight[:, k, t:t + 1],
                                           in1=x2[:, t, :], op0=ALU.mult, op1=ALU.add).then_inc(added, 1)

            def front(t):
                u = t % 2
                dve.wait_ge(summed, t + 1)
                V.tensor_scalar(stat[:, u, 1:2], stat[:, u, 0:1], 1.0 / D, EPS, ALU.mult, ALU.add).then_inc(mean, 1)
                dve.wait_ge(rooted, t + 1)
                V.reciprocal(stat[:, u, 3:4], stat[:, u, 2:3]).then_inc(rstd, 1)
                dve.wait_ge(turned_ok, t + 1)
                if t >= 1:
                    dve.wait_ge(lo_ok, t)
                V.tensor_tensor(whole[:], turned[:], bc(ple_gain[:], 2, P), ALU.mult).then_inc(gained, 1)
                dve.wait_ge(hi_ok, t + 1)
                V.tensor_tensor(t_lo[:, u], whole[:], t_hi[:, u].bitcast(F32), ALU.subtract).then_inc(lo_ok, 1)

            def back(t):
                u = t % 2
                dve.wait_ge(sig_ok, t + 1)
                dve.wait_ge(proj_mm, t + 1)
                V.tensor_tensor(gate[:], s_proj[:].rearrange("p a b -> p (a b)"), gate[:], ALU.mult).then_inc(mixed, 1)
                dve.wait_ge(mixed, 2 * t + 1)
                V.tensor_tensor(x2[:, t, :], x2[:, t, :], gate[:], ALU.add).then_inc(mixed, 1)
                if t + 2 < TT:
                    add_experts(t + 2)
                dve.wait_ge(summed2, t + 1)
                V.tensor_scalar(stat[:, u, 5:6], stat[:, u, 4:5], 1.0 / D, EPS, ALU.mult, ALU.add).then_inc(mean2, 1)
                dve.wait_ge(rooted2, t + 1)
                V.reciprocal(stat[:, u, 7:8], stat[:, u, 6:7]).then_inc(rstd2, 1)
                dve.wait_ge(rstd2, t + 1)
                if t >= 1:
                    dve.wait_ge(stored, 16 * t)
                V.scalar_tensor_tensor(out=res[:], in0=x2[:, t, :], scalar=stat[:, u, 7:8], in1=out_gain[:],
                                       op0=ALU.mult, op1=ALU.mult).then_inc(res_ok, 1)

            for k in range(KT // 2):
                split(k)
            add_experts(0)
            front(0)
            for k in range(KT // 2, KT):
                split(k)
            add_experts(1)
            dve.wait_ge(out_gain_in, 16)
            for t in range(TT):
                if t + 1 < TT:
                    front(t + 1)
                back(t)

        @block.tensor
        def _(pe):

            def front(t):
                pe.wait_ge(scaled, t + 1)
                if t >= 1:
                    pe.wait_ge(gained, t)
                for k in range(KT):
                    mm = nc.tensor.transpose(turned[:, k, :], xn[:, k * P:(k + 1) * P], ident[:])
                mm.then_inc(turned_ok, 1)
                pe.wait_ge(p_in[t % 2], 16 * (t // 2) + 16)
                if t >= 1:
                    pe.wait_ge(pT_ok, t)
                for k in range(KP):
                    mm = nc.tensor.transpose(p_turned[:, k, :], pt[:, t % 2, k * P:(k + 1) * P], ident[:])
                mm.then_inc(p_turned_ok, 1)

            front(0)
            pe.wait_ge(w_lo_ok, KT)
            pe.wait_ge(w_p_in, 16)
            for t in range(TT):
                u = t % 2
                pe.wait_ge(lo_ok, t + 1)
                if t >= 1:
                    pe.wait_ge(sig_ok, t)
                for half in range(2):
                    cols = slice(half * HALF, (half + 1) * HALF)
                    mm = three_passes(nc, s_gate[:, half, :], [(t_hi[:, u, k, :], t_lo[:, u, k, :], g_hi[:, k, cols],
                                                                g_lo[:, k, cols]) for k in range(KT)])
                mm.then_inc(gate_mm, 1)
                if t + 1 < TT:
                    front(t + 1)
                pe.wait_ge(pT_ok, t + 1)
                if t >= 1:
                    pe.wait_ge(mixed, 2 * t)
                for half in range(2):
                    for k in range(KP):
                        mm = nc.tensor.matmul(s_proj[:, half, :], pT[:, u, k, :], w_p[:, k, half * HALF:(half + 1) * HALF],
                                              start=(k == 0), stop=(k == KP - 1))
                mm.then_inc(proj_mm, 1)


def shape_constants():
    f32 = np.float32
    c = {"ident": np.eye(P, dtype=f32)}
    s, t = np.meshgrid(np.arange(HG_CHUNK), np.arange(HG_CHUNK), indexing="ij")
    masks = [(s // (2 * h) == t // (2 * h)) & (s // h % 2 == 0) & (t // h % 2 == 1) for h in LEVELS] + [s == t]
    masks = np.stack(masks, axis=1).astype(np.int32)
    c["hg_masks"] = np.concatenate([masks, masks], axis=0)
    c["hg_reset"] = np.tile((np.arange(S) % HG_CHUNK != 0).astype(f32), (P, 1))
    inv = f32(10000.0) ** (-np.arange(0, RET_DK, 2, dtype=f32) / f32(RET_DK))
    angle = np.arange(S, dtype=f32)[None, :] * inv[:, None]
    c["cos"] = np.tile(np.cos(angle), (2, 1)).astype(f32)
    c["sin"] = np.concatenate([-np.sin(angle), np.sin(angle)], axis=0).astype(f32)
    lg = np.log1p(-np.exp2(-5.0 - np.arange(RET_HEADS)))
    idx = np.arange(P)
    rel = idx[None, :] - idx[:, None]
    scale = RET_DK ** -0.5
    intra = np.where(rel[:, None, :] >= 0, np.exp(np.maximum(rel, 0)[:, None, :] * lg[None, :, None]), 0.0) * scale
    c["ret_intra"] = intra.astype(f32)
    inter = np.exp((idx[None, :] + 1.0) * lg[:, None]) * scale
    c["ret_inter"] = np.tile(inter[None], (P, 1, 1)).astype(f32)
    c["ret_to_state"] = np.exp((P - 1.0 - idx[:, None]) * lg[None, :]).astype(f32)
    c["desc"] = np.tile(np.arange(PER_GROUP, 0, -1, dtype=f32), (P, 1))
    c["iota"] = np.tile(np.arange(P, dtype=f32), (P, 1))
    c["earlier"] = np.triu(np.ones((P, P), f32), 1)
    c["ones"] = np.ones((P, P), f32)
    tok = np.arange(P)[:, None, None] + P * np.arange(TT)[None, None, :] + np.zeros((1, 2, 1))
    dst = tok + S * np.arange(2)[None, :, None]
    c["pair_ids"] = (np.stack([tok, dst], axis=-1) + 1).reshape(P, 2 * TT, 2).astype(f32)
    c["ret_decay"] = np.tile(np.exp(P * lg)[None, :], (P, 1)).astype(f32)
    return c


def build(nc, dram, out):
    dram = dict(dram)
    Memory.sems.clear()
    dram["rows"] = nc.dram_tensor("rows", [S, D], F32, kind="Internal").ap()
    dram["results"] = nc.dram_tensor("results", [PAIRS, D], F32, kind="Internal").ap()
    dram["merged"] = nc.dram_tensor("merged", [D, S], F32, kind="Internal").ap()
    with Memory(nc, "kept") as top:
        kept = {"ident": top.sb("ident", [P, P])}
        with Memory(nc, "mix") as mix:
            kept["hT_hi"] = mix.sb("hT_hi", [P, KT, S], F32R)
            kept["hT_lo"] = mix.sb("hT_lo", [P, KT, S], F32R)
            kept["weight_slots"] = Ring.slots(mix, KT, P, "w")
            kept["asked"] = {stage: [mix.sem(f"{stage}_asked{u}") for u in range(2)]
                             for stage in ("hgrn", "reten", "gate", "merge")}
            with Memory(nc, "heads") as heads:
                kept["values"] = heads.sb("values", [P, TT, VW])
                with Memory(nc, "first") as early:
                    kept["value_raw"] = early.sb("raw", [P, 2, KT, 256])
                    kept["value_asked"] = [early.sem(f"asked{u}") for u in range(2)]
                    normalise_input(nc, dram, kept)
                    project_values(nc, dram, kept)
                hgrn_heads(nc, dram, kept)
                retention_heads(nc, dram, kept)
            kept["y_hi"] = mix.sb("y_hi", [P, TT, VW], F32R)
            kept["y_lo"] = mix.sb("y_lo", [P, VW // P, S], F32R)
            gate_heads(nc, dram, kept)
            merge_branches(nc, dram, kept)
        Memory.recycle(nc)
        kept["x2"] = top.sb("x2", [P, TT, D])
        project_out(nc, dram, kept)
        kept["logits"] = top.sb("logits", [P, TT, GROUPS + EXPERTS])
        kept["ffn_gain"] = top.sb("ffn_gain", [P, KT])
        kept["weight"] = top.sb("weight", [P, 2, TT])
        kept["slots"] = top.sb("slots", [P, COLS, 2], I32)
        kept["owner"] = top.sb("owner", [P, OVER + 1], I32)
        kept["ple_raw"] = top.sb("ple_raw", [P, KT, D])
        kept["ple_in"] = [top.sem(f"ple_in{k}") for k in range(KT)]
        with Memory(nc, "weights") as weights:
            kept["w_gu"] = weights.sb("w_gu", [P, AHEAD, KT, 2, DE])
            kept["w_d"] = weights.sb("w_d", [P, AHEAD, DE // P, D])
            kept["gu_in"] = [weights.sem(f"gu_in{b}") for b in range(AHEAD)]
            kept["d_in"] = [weights.sem(f"d_in{b}") for b in range(AHEAD)]
            with Memory(nc, "tables") as tables:
                for name in TABLES:
                    kept[name] = tables.sb(name, list(dram[name].shape))
                kept["tables_in"] = tables.sem("in")
                route(nc, dram, kept)
                place(nc, dram, kept)
            run_experts(nc, dram, kept)
        finish(nc, dram, kept, out)


def layout(x, p, mix_norm, w_in, hg_lb_logits, hg_norm, ret_norm, w_branch_a, w_branch_b, w_out,
           ffn_norm, w_router_group, b_router_group, w_router_expert, b_router_expert,
           w_expert_gate, w_expert_up, w_expert_down, ple_norm, w_ple_gate, w_ple_proj, final_norm):
    def turned(v):
        return np.ascontiguousarray(np.asarray(v).reshape(-1, P).T)

    a = {
        "x": x.reshape(S, D), "p": p.reshape(S, PLE), "w_in": w_in[0],
        "w_a": w_branch_a[0], "w_b": w_branch_b[0], "w_out": w_out[0],
        "w_rg": w_router_group[0], "w_re": w_router_expert[0], "b_rg": b_router_group, "b_re": b_router_expert,
        "w_eg": w_expert_gate.reshape(EXPERTS * D, DE), "w_eu": w_expert_up.reshape(EXPERTS * D, DE),
        "w_ed": w_expert_down.reshape(EXPERTS * DE, D),
        "w_pg": w_ple_gate[0], "w_pp": w_ple_proj[0], "final_norm": final_norm.reshape(1, D),
        "mix_norm": turned(mix_norm), "ffn_norm": turned(ffn_norm), "ple_norm": turned(ple_norm),
        "hg_norm": turned(hg_norm), "ret_norm": turned(ret_norm),
        "hg_lb_logits": hg_lb_logits.reshape(2, HG_HEADS, P).transpose(2, 0, 1),
    }
    a.update(shape_constants())
    return {n: np.ascontiguousarray(v) for n, v in a.items()}


def kernel(**inputs):
    from concourse import bacc
    from concourse.bass_utils import run_bass_kernel_spmd

    arrays = layout(**{n: np.asarray(v) for n, v in inputs.items()})
    nc = bacc.Bacc("TRN2", target_bir_lowering=False, num_devices=1)
    dram = {n: nc.dram_tensor(n, a.shape, mybir.dt.from_np(a.dtype), kind="ExternalInput").ap()
            for n, a in arrays.items()}
    out = nc.dram_tensor("out", (S, D), F32, kind="ExternalOutput").ap()
    build(nc, dram, out)
    result = run_bass_kernel_spmd(nc, [arrays], core_ids=[0])
    return result.results[0]["out"].reshape(1, S, D)
```
